# Optimizing a Trainium2 kernel written in Bass

```python
import jax, jax.numpy as jnp
from jax import lax
import numpy as np

D_MODEL = 1024
BATCH = 1
SEQ = 512
DEPTH = 1

GRID_W = 64
CTX_LEN = 256
N_MIXERS = 4
MIX_WIDTH = D_MODEL
GROUP_WIDTH = MIX_WIDTH // N_MIXERS
HEAD_DIM = 64
NA_HEADS = GROUP_WIDTH // HEAD_DIM
FOURIER_HEADS = GROUP_WIDTH // HEAD_DIM
CONV_K = 3
POOL_WINDOWS = (2, 4, 8, 16)
POOL_GROUPS = len(POOL_WINDOWS)
POOL_GROUP = GROUP_WIDTH // POOL_GROUPS
WIN_ROWS = 8
WIN_COLS = 16
N_PROJ_CHUNKS = 8
IN_COLS = N_PROJ_CHUNKS * GROUP_WIDTH
N_EXPERTS = 16
N_EXPERT_GROUPS = 4
EXPERTS_PER_GROUP = N_EXPERTS // N_EXPERT_GROUPS
TOP_K = 2
MOE_HIDDEN = D_MODEL // 2
EPS = 1e-6

kernel_name = "hybrid_parallel_mixer_dit_block"

F32 = jnp.float32

def rms_norm(x, g):
    xf = x.astype(F32)
    y = xf * lax.rsqrt(jnp.mean(jnp.square(xf), axis=-1, keepdims=True) + EPS)
    return (y * g.astype(F32)).astype(x.dtype)

def gated_short_conv(val, gate_b, gate_c, w):
    n = val.shape[1]
    pad = CONV_K // 2
    z = jnp.pad(gate_c * val, ((0, 0), (pad, CONV_K - 1 - pad), (0, 0)))
    conv = sum(z[:, j:j + n] * w[j] for j in range(CONV_K))
    return gate_b * conv

def multiscale_pool(u, pool_w, pool_scale):
    b, n, _ = u.shape
    uf = u.astype(F32)
    csum = jnp.concatenate([jnp.zeros((b, 1, GROUP_WIDTH), F32), jnp.cumsum(uf, axis=1)], axis=1)
    t = jnp.arange(n)
    outs = []
    for gi, w in enumerate(POOL_WINDOWS):
        lo = jnp.maximum(t - w // 2, 0)
        hi = jnp.minimum(t + w // 2, n)
        sl = slice(gi * POOL_GROUP, (gi + 1) * POOL_GROUP)
        win_sum = csum[:, hi, sl] - csum[:, lo, sl]
        cnt = (hi - lo).astype(F32)[None, :, None]
        outs.append(win_sum / cnt - uf[:, :, sl])
    d = jnp.stack(outs, axis=2)
    y = jnp.einsum('bngc,gcd->bngd', d, pool_w.astype(F32))
    return (y.reshape(b, n, GROUP_WIDTH) * pool_scale.astype(F32)).astype(u.dtype)

def fourier_mix(u):
    b, n, _ = u.shape
    uh = u.astype(F32).reshape(b, n, FOURIER_HEADS, HEAD_DIM)
    y = jnp.fft.fft2(uh, axes=(1, 3), norm='ortho').real
    return y.reshape(b, n, GROUP_WIDTH).astype(u.dtype)

def neighborhood_attention(q, k, v, kc, vc, rpb):
    b, n, _ = q.shape
    rows = n // GRID_W
    kr = min(WIN_ROWS, rows)
    scale = HEAD_DIM ** -0.5

    def to_grid(a):
        return a.reshape(b, rows, GRID_W, NA_HEADS, HEAD_DIM).transpose(0, 3, 1, 2, 4)

    qg, kg, vg = to_grid(q), to_grid(k), to_grid(v)
    kch = kc.reshape(b, -1, NA_HEADS, HEAD_DIM).transpose(0, 2, 1, 3)
    vch = vc.reshape(b, -1, NA_HEADS, HEAD_DIM).transpose(0, 2, 1, 3)
    r = jnp.arange(rows)
    col = jnp.arange(GRID_W)
    row_idx = jnp.clip(r - kr // 2, 0, rows - kr)[:, None] + jnp.arange(kr)[None, :]
    col_idx = jnp.clip(col - WIN_COLS // 2, 0, GRID_W - WIN_COLS)[:, None] + jnp.arange(WIN_COLS)[None, :]
    k_band = kg[:, :, row_idx]
    v_band = vg[:, :, row_idx]
    s_band = jnp.einsum('bhrqd,bhrkwd->bhrqkw', qg, k_band, preferred_element_type=F32) * scale
    sel = jax.nn.one_hot(col_idx, GRID_W, dtype=F32)
    s_win = jnp.einsum('bhrqkw,qjw->bhrqkj', s_band, sel)
    rel_r = row_idx - r[:, None] + (WIN_ROWS - 1)
    rel_c = col_idx - col[:, None] + (WIN_COLS - 1)
    bias = rpb[:, rel_r[:, None, :, None], rel_c[None, :, None, :]]
    n_win = kr * WIN_COLS
    s_win = (s_win + bias[None].astype(F32)).reshape(b, NA_HEADS, rows, GRID_W, n_win)
    s_ctx = jnp.einsum('bhrqd,bhld->bhrql', qg, kch, preferred_element_type=F32) * scale
    p = jax.nn.softmax(jnp.concatenate([s_win, s_ctx], axis=-1), axis=-1)
    p_win = p[..., :n_win].reshape(b, NA_HEADS, rows, GRID_W, kr, WIN_COLS)
    p_ctx = p[..., n_win:]
    p_band = jnp.einsum('bhrqkj,qjw->bhrqkw', p_win, sel)
    o = (jnp.einsum('bhrqkw,bhrkwd->bhrqd', p_band.astype(v.dtype), v_band)
         + jnp.einsum('bhrql,bhld->bhrqd', p_ctx.astype(v.dtype), vch))
    return o.transpose(0, 2, 3, 1, 4).reshape(b, n, GROUP_WIDTH)

def context_attention(qc, kc, vc):
    b, l, _ = qc.shape
    sp = lambda a: a.reshape(b, l, NA_HEADS, HEAD_DIM)
    s = jnp.einsum('blhd,bmhd->bhlm', sp(qc), sp(kc), preferred_element_type=F32) * (HEAD_DIM ** -0.5)
    p = jax.nn.softmax(s, axis=-1)
    o = jnp.einsum('bhlm,bmhd->blhd', p.astype(vc.dtype), sp(vc))
    return o.reshape(b, l, GROUP_WIDTH)

def moe_ffn(h, router_w, router_b, w1, w3, w2):
    scores = jax.nn.sigmoid(jnp.dot(h.astype(F32), router_w.astype(F32)))
    biased = scores + router_b.astype(F32)
    grp = biased.reshape(h.shape[0], N_EXPERT_GROUPS, EXPERTS_PER_GROUP)
    grp_score = jnp.sum(lax.top_k(grp, TOP_K)[0], axis=-1)
    best = jnp.argmax(grp_score, axis=-1)
    expert_group = jnp.arange(N_EXPERTS) // EXPERTS_PER_GROUP
    masked = jnp.where(expert_group[None, :] == best[:, None], biased, -jnp.inf)
    _, idx = lax.top_k(masked, TOP_K)
    wsel = jnp.take_along_axis(scores, idx, axis=-1)
    wsel = wsel / jnp.sum(wsel, axis=-1, keepdims=True)
    gates = jnp.sum(jax.nn.one_hot(idx, N_EXPERTS, dtype=F32) * wsel[..., None], axis=1)
    y = jnp.zeros(h.shape, F32)
    for e in range(N_EXPERTS):
        he = jax.nn.silu(h @ w1[e]) * (h @ w3[e])
        y = y + gates[:, e:e + 1] * (he @ w2[e]).astype(F32)
    return y.astype(h.dtype)

def setup_inputs(seed: int = 0) -> dict:
    key = jax.random.key(seed)
    ks = jax.random.split(key, 22)
    nrm = lambda k, shape, s: jax.random.normal(k, shape, F32) * s
    return {
        "x": nrm(ks[0], (BATCH, SEQ, D_MODEL), 1.0),
        "c": nrm(ks[1], (BATCH, D_MODEL), 1.0),
        "ctx": nrm(ks[2], (BATCH, CTX_LEN, D_MODEL), 1.0),
        "c_ctx": nrm(ks[3], (D_MODEL,), 1.0),
        "ada_w": nrm(ks[4], (DEPTH, D_MODEL, 6 * D_MODEL), 0.5 * D_MODEL ** -0.5),
        "ada_b": nrm(ks[5], (DEPTH, 6 * D_MODEL), 0.02),
        "norm1_g": 1.0 + nrm(ks[6], (DEPTH, D_MODEL), 0.02),
        "norm2_g": 1.0 + nrm(ks[7], (DEPTH, D_MODEL), 0.02),
        "w_in": nrm(ks[8], (DEPTH, D_MODEL, IN_COLS), D_MODEL ** -0.5),
        "conv_w": nrm(ks[9], (DEPTH, CONV_K, GROUP_WIDTH), CONV_K ** -0.5),
        "pool_w": nrm(ks[10], (DEPTH, POOL_GROUPS, POOL_GROUP, POOL_GROUP), POOL_GROUP ** -0.5),
        "pool_scale": 1.0 + nrm(ks[11], (DEPTH, GROUP_WIDTH), 0.1),
        "na_rpb": nrm(ks[12], (DEPTH, NA_HEADS, 2 * WIN_ROWS - 1, 2 * WIN_COLS - 1), 0.1),
        "w_out": nrm(ks[13], (DEPTH, MIX_WIDTH, D_MODEL), MIX_WIDTH ** -0.5),
        "router_w": nrm(ks[14], (D_MODEL, N_EXPERTS), D_MODEL ** -0.5),
        "router_b": nrm(ks[15], (N_EXPERTS,), 0.01),
        "moe_w1": nrm(ks[16], (DEPTH, N_EXPERTS, D_MODEL, MOE_HIDDEN), D_MODEL ** -0.5),
        "moe_w3": nrm(ks[17], (DEPTH, N_EXPERTS, D_MODEL, MOE_HIDDEN), D_MODEL ** -0.5),
        "moe_w2": nrm(ks[18], (DEPTH, N_EXPERTS, MOE_HIDDEN, D_MODEL), MOE_HIDDEN ** -0.5),
        "final_g": 1.0 + nrm(ks[19], (D_MODEL,), 0.02),
    }

def reference(x, c, ctx, c_ctx, ada_w, ada_b, norm1_g, norm2_g, w_in, conv_w, pool_w, pool_scale,
              na_rpb, w_out, router_w, router_b, moe_w1, moe_w3, moe_w2, final_g):
    b, n, d = x.shape
    l = ctx.shape[1]
    xc = ctx
    c_act = jax.nn.silu(c)
    cc_act = jax.nn.silu(c_ctx)
    for layer in range(DEPTH):
        last = layer == DEPTH - 1
        mod = c_act @ ada_w[layer] + ada_b[layer]
        mod_c = cc_act @ ada_w[layer] + ada_b[layer]
        sh1, sc1, g1, sh2, sc2, g2 = jnp.split(mod[:, None, :], 6, axis=-1)
        csh1, csc1, cg1, csh2, csc2, cg2 = jnp.split(mod_c, 6, axis=-1)

        h = rms_norm(x, norm1_g[layer]) * (1 + sc1) + sh1
        hc = rms_norm(xc, norm1_g[layer]) * (1 + csc1) + csh1
        u = h @ w_in[layer]
        a_v, a_b, a_c, p_in, q, k, v, f_in = jnp.split(u, N_PROJ_CHUNKS, axis=-1)
        if last:
            kc, vc = jnp.split(hc @ w_in[layer][:, 5 * GROUP_WIDTH:7 * GROUP_WIDTH], 2, axis=-1)
        else:
            uc = hc @ w_in[layer]
            ca_v, ca_b, ca_c, cp_in, cq, kc, vc, cf_in = jnp.split(uc, N_PROJ_CHUNKS, axis=-1)

        y = jnp.concatenate([
            gated_short_conv(a_v, a_b, a_c, conv_w[layer]),
            multiscale_pool(p_in, pool_w[layer], pool_scale[layer]),
            neighborhood_attention(q, k, v, kc, vc, na_rpb[layer]),
            fourier_mix(f_in),
        ], axis=-1)
        x = x + g1 * (y @ w_out[layer])
        if not last:
            yc = jnp.concatenate([
                gated_short_conv(ca_v, ca_b, ca_c, conv_w[layer]),
                multiscale_pool(cp_in, pool_w[layer], pool_scale[layer]),
                context_attention(cq, kc, vc),
                fourier_mix(cf_in),
            ], axis=-1)
            xc = xc + cg1 * (yc @ w_out[layer])

        h2 = rms_norm(x, norm2_g[layer]) * (1 + sc2) + sh2
        tokens = h2.reshape(b * n, d)
        if not last:
            h2c = rms_norm(xc, norm2_g[layer]) * (1 + csc2) + csh2
            tokens = jnp.concatenate([tokens, h2c.reshape(b * l, d)], axis=0)
        f = moe_ffn(tokens, router_w, router_b, moe_w1[layer], moe_w3[layer], moe_w2[layer])
        x = x + g2 * f[:b * n].reshape(b, n, d)
        if not last:
            xc = xc + cg2 * f[b * n:].reshape(b, l, d)
    return rms_norm(x, final_g)


_drawn_inputs = setup_inputs


def setup_inputs(seed=0):
    import zlib

    import numpy as np

    out = dict(_drawn_inputs(seed))
    spreads = {}
    factors = {'norm1_g': 3.277,
     'pool_scale': 2.789,
     'na_rpb': 47.022,
     'final_g': 8.111,
     'norm2_g': 8.0,
     'router_b': 8.0}
    for name, (base, spread) in spreads.items():
        noise = np.random.default_rng([zlib.crc32(name.encode()), seed]).standard_normal(out[name].shape)
        drawn = base * np.exp(spread * noise) if base else spread * noise
        out[name] = __import__('jax').numpy.asarray(drawn.astype(out[name].dtype))
    for name, factor in factors.items():
        out[name] = (out[name] * factor).astype(out[name].dtype)
    return out
```

```python
from contextlib import ExitStack

import numpy as np

import concourse.bass as bass
from concourse import mybir

F32 = mybir.dt.float32
I32 = mybir.dt.int32
ALU = mybir.AluOpType
ACT = mybir.ActivationFunctionType
AX = mybir.AxisListType.X

P = 128
D = 1024
N = 512
L = 256
KD = D // P
NT = N // P
LT = L // P
GW = 256
HD = 64
HEADS = GW // HD
ROWS, COLS = 8, 64
WIN_COLS = 16
RPB_R, RPB_C = 15, 31
NE = 16
GROUPS = 4
FF = 512
KF = FF // P
EPS = 1e-6
SCALE = HD ** -0.5
BIG = 1e30
OVER = 8
NB = NE + OVER
EMPTY = 4096
PAD_C = 16
TAB = 960
RUN = 48 * RPB_R
NSEG = 7
KEYS = [(0, 2, 3), (0, 3, 0), (1, 4, 0), (2, 4, 5)]
K1 = 1024


def build(nc, x, c, ctx, c_ctx, ada_w, ada_b, norm1_g, norm2_g, w_in, conv_w, pool_w, pool_scale,
          rpb_t, w_out, router_w, router_b, moe_w1, moe_w3, moe_w2, final_g,
          dft_cos, dft_sin, dft_head, pool_inv, out):
    h2_dram = nc.dram_tensor("h2_rows", (N, D), F32, kind="Internal").ap()
    y_dram = nc.dram_tensor("expert_rows", (NB * P, D), F32, kind="Internal").ap()
    tab_dram = nc.dram_tensor("bias_table", (HEADS, TAB), F32, kind="Internal").ap()

    base = (nc.sbuf_base + 31) // 32 * 32
    stack = ExitStack()
    with stack:
        def at(name, offset, shape, dt=F32):
            return nc.alloc_sbuf_tensor_at(name, shape, dt, offset=base + int(offset))

        def sem(name):
            return stack.enter_context(nc.semaphore(name))

        w1_sb = [at(f"w1_{b}", 48 * K1 * b, [P, KD, FF]) for b in range(2)]
        w3_sb = [at(f"w3_{b}", 48 * K1 * b + 16 * K1, [P, KD, FF]) for b in range(2)]
        w2_sb = [at(f"w2_{b}", 48 * K1 * b + 32 * K1, [P, KF, D]) for b in range(2)]
        ada = [at(f"ada_{i}", 16 * K1 * i, [P, KD, 512]) for i in range(4)]
        yT = at("yT", 0, [P, 8, N])
        av = at("av", 16 * K1, [P, 2, N])
        z = at("z", 20 * K1, [P, 2, N + 2])
        cv = at("cv", 25 * K1, [P, 2, N])
        s8 = at("s8", 29 * K1, [P, N + 16])
        up = at("up", 32 * K1, [P, 2, N + 16])
        s2 = at("s2", 36.5 * K1, [P, 2, N + 16])
        s4 = at("s4", 41 * K1, [P, 2, N + 16])
        zero = at("zero", 46 * K1, [P, 256])
        cos_sb = at("cos_sb", 48 * K1, [P, NT, N])
        sin_sb = at("sin_sb", 56 * K1, [P, NT, N])
        bias = at("bias", 64 * K1, [P, HEADS, NSEG * 16, ROWS])
        raw = at("raw", 78 * K1, [P, HEADS, 48, RPB_R])
        sw = at("sw", 78 * K1, [P, 2, 384])
        pr = at("pr", 81 * K1, [P, 2, 640])
        pT = at("pT", 86 * K1, [P, 2, 640])
        tabpad = at("tabpad", 91 * K1, [HEADS, TAB])
        dpool = at("dpool", 91 * K1, [P, 2, N])
        win = [at(f"win_{i}", (96 + 8 * i) * K1, [P, KD, GW]) for i in range(4)]
        ctx_sb = at("ctx_sb", 120 * K1, [P, LT, D])
        wout = at("wout", 96 * K1, [P, KD, D])
        ygat = at("ygat", 96 * K1, [P, NT, 2, D])
        x1 = at("x1", 128 * K1, [P, NT, D])
        rows = at("rows", 144 * K1, [P, 4, D])
        G1, SH2, SC2, G2 = range(4)
        hT = at("hT", 160 * K1, [P, KD, N])
        hcT = at("hcT", 176 * K1, [P, KD, L])
        fcs = at("fcs", 160 * K1, [P, NT, 2, 2 * P])
        n2g = at("n2g", 168 * K1, [P, D])
        h2T = at("h2T", 160 * K1, [P, KD, N])
        h2 = at("h2", 176 * K1, [P, 2, D])
        fT = at("fT", 176 * K1, [P, 2, N])
        inv = at("inv", 180 * K1, [P, 2, N])
        hot_slot = at("hot_slot", 172 * K1, [P, NT * 2, P])
        xg = [at(f"xg_{b}", (160 + 4 * b) * K1, [P, D]) for b in range(2)]
        xgT = [at(f"xgT_{b}", (168 + 4 * b) * K1, [P, KD, P]) for b in range(2)]
        ysb = [at(f"ysb_{b}", (176 + 4 * b) * K1, [P, D]) for b in range(2)]
        xn = at("xn", 184 * K1, [P, NT, D])
        qT = at("qT", 184 * K1, [P, 2, N])
        kT = at("kT", 188 * K1, [P, 2, N])
        kcT = at("kcT", 192 * K1, [P, 2, L])
        v_sb = at("v_sb", 194 * K1, [P, NT, GW])
        vc_sb = at("vc_sb", 198 * K1, [P, LT, GW])
        rtmp = at("rtmp", 184 * K1, [P, 2, 512])
        sg = at("sg", 184 * K1, [P, FF])
        he = at("he", 186 * K1, [P, FF])
        heT = at("heT", 188 * K1, [P, KF, P])
        fing = at("fing", 190 * K1, [P, D])
        cursor = [194 * K1, 200 * K1]

        def small(name, shape, dt=F32, pool=1):
            n = int(np.prod(shape[1:])) * 4
            n = (n + 31) // 32 * 32
            t = at(name, cursor[pool], shape, dt)
            cursor[pool] += n
            return t

        ident = small("ident", [P, P])
        ones = small("ones", [P, P])
        tri = small("tri", [P, P])
        vec = small("vec", [48, P])
        cols = small("cols", [P, 48])
        cc = small("cc", [P, KD, 2])
        modc = small("modc", [P, 16, 2])
        a1 = small("a1", [P, KD, 2])
        pw = small("pw", [P, 2, P])
        head_dft = small("head_dft", [P, 2 * P])
        rw = small("rw", [P, KD, NE])
        rb = small("rb", [P, NT, NE])
        stat = small("stat", [P, 6, 4])
        st2 = small("st2", [P, NT, 6])
        soft = small("soft", [P, 2, 8])
        slot_idx = small("slot_idx", [P, NT, 2], I32)
        gate = small("gate", [P, NT, 2])
        idx = small("idx", [P, NB], I32)
        idx1 = [small(f"idx1_{b}", [P, 8], I32) for b in range(2)]
        ints = small("ints", [1, 16], I32)
        assert base + cursor[1] <= nc.sbuf_usable_end

        def rt(name, shape, dt=F32):
            return small(name, shape, dt, 0)
        prob = rt("prob", [P, NT, NE])
        biased = rt("biased", [P, NT, NE])
        ra = rt("ra", [P, NT, NE])
        rbuf = rt("rbuf", [P, NT, NE])
        pairs = rt("pairs", [P, NT * GROUPS, 6])
        gs = rt("gs", [P, NT, GROUPS])
        geq = rt("geq", [P, NT, GROUPS])
        pen = rt("pen", [P, NT, GROUPS])
        r1 = rt("r1", [P, NT, 1])
        r2 = rt("r2", [P, NT, 1])
        oh = rt("oh", [P, NT, 2, NE])
        rc = rt("rc", [P, NT, 2, NE])
        sel = rt("sel", [P, NT, NE])
        rank = rt("rank", [P, NT, NE])
        over = rt("over", [P, NT, NE])
        cnt = rt("cnt", [P, NE])
        ext = rt("ext", [P, NE])
        cs = rt("cs", [P, 2, 8 + NE])
        slot = rt("slot", [P, NT, 2])
        rmod = rt("rmod", [P, NT, 2])
        blk_no = rt("blk_no", [P, NT, 2])
        wsel = rt("wsel", [P, NT, 2])
        den = rt("den", [P, NT, 1])
        hot_blk = rt("hot_blk", [P, NT * 2, NB])
        ov = rt("ov", [1, 8, NE])
        ovf = rt("ovf", [1, 16])
        pri4 = rt("pri4", [P, NT, GROUPS])
        pri16 = rt("pri16", [P, NT, NE])
        eno = rt("eno", [P, NE])
        iota_slot = small("iota_slot", [P, P])
        iota_blk = rt("iota_blk", [P, NB])
        iota8 = rt("iota8", [1, 8])
        tok = rt("tok", [P, NT])
        assert cursor[0] <= 200 * K1, cursor[0]

        psum = stack.enter_context(nc.psum_tensor("psum", [P, 8, 512], F32))
        bank = [psum[:, i, :] for i in range(8)]

        vec_in = sem("vec_in")
        ctx_in = sem("ctx_in")
        x_in = [sem(f"x_in{i}") for i in range(2)]
        ada_in = [sem(f"ada_in{i}") for i in range(4)]
        win_in = [sem(f"win_in{i}") for i in range(4)]
        adab_in = sem("adab_in")
        tabpad_in = sem("tabpad_in")
        tab_out = sem("tab_out")
        raw_in = sem("raw_in")
        consts_in = sem("consts_in")
        poolw_in = sem("poolw_in")
        inv_in = sem("inv_in")
        n2g_in = sem("n2g_in")
        fing_in = sem("fing_in")
        dft_in = sem("dft_in")
        wout_in = [sem(f"wout_in{i}") for i in range(4)]
        w1_in = [sem(f"w1_in{b}") for b in range(2)]
        w3_in = [sem(f"w3_in{b}") for b in range(2)]
        w2_in = [sem(f"w2_in{b}") for b in range(2)]
        gp_step = sem("gp_step")
        ident_ok = sem("ident_ok")
        ones_ok = sem("ones_ok")
        rows_zero = sem("rows_zero")
        tab_zero = sem("tab_zero")
        pw_zero = sem("pw_zero")
        pads_ok = sem("pads_ok")
        zero_ok = sem("zero_ok")
        zero_stored = sem("zero_stored")
        bias_ok = sem("bias_ok")
        iota_ok = sem("iota_ok")
        vecT_ok = sem("vecT_ok")
        cols_ok = sem("cols_ok")
        cc_ok = sem("cc_ok")
        ss_ok = sem("ss_ok")
        ms_ok = sem("ms_ok")
        root_ok = sem("root_ok")
        xn_ok = sem("xn_ok")
        tr_ok = sem("tr_ok")
        tr_free = sem("tr_free")
        ab_ok = sem("ab_ok")
        hc_ok = sem("hc_ok")
        h_ok = sem("h_ok")
        ada_pe = sem("ada_pe")
        ada_dve = sem("ada_dve")
        rowsum_ok = sem("rowsum_ok")
        rows_act = sem("rows_act")
        kv_ok = sem("kv_ok")
        kv_free = sem("kv_free")
        pj_ok = sem("pj_ok")
        pj_act = sem("pj_act")
        pj_dve = sem("pj_dve")
        s_ok = sem("s_ok")
        sb_ok = sem("sb_ok")
        nm_ok = sem("nm_ok")
        ex_ok = sem("ex_ok")
        pn_ok = sem("pn_ok")
        pt_ok = sem("pt_ok")
        pt_copied = sem("pt_copied")
        o_ok = sem("o_ok")
        o_copied = sem("o_copied")
        d_ok = sem("d_ok")
        pool_ps = sem("pool_ps")
        pool_ok = sem("pool_ok")
        fd_ok = sem("fd_ok")
        fd_copied = sem("fd_copied")
        fn_ok = sem("fn_ok")
        fn_copied = sem("fn_copied")
        wo_ok = sem("wo_ok")
        x1_ok = sem("x1_ok")
        ss2_ok = sem("ss2_ok")
        ms2_ok = sem("ms2_ok")
        root2_ok = sem("root2_ok")
        h2_ok = sem("h2_ok")
        h2_stored = sem("h2_stored")
        h2tr_ok = sem("h2tr_ok")
        h2T_ok = sem("h2T_ok")
        logit_ok = sem("logit_ok")
        prob_ok = sem("prob_ok")
        sel_ok = sem("sel_ok")
        rank_ok = sem("rank_ok")
        hot_ok = sem("hot_ok")
        idxps_ok = sem("idxps_ok")
        route_ok = sem("route_ok")
        idx1_ok = sem("idx1_ok")
        gather_go = sem("gather_go")
        xg_in = [sem(f"xg_in{b}") for b in range(2)]
        xt_ok = sem("xt_ok")
        xt_copied = sem("xt_copied")
        h1_ok = sem("h1_ok")
        h3_ok = sem("h3_ok")
        sg_ok = sem("sg_ok")
        he_ok = sem("he_ok")
        het_ok = sem("het_ok")
        het_copied = sem("het_copied")
        y0_ok = sem("y0_ok")
        y1_ok = sem("y1_ok")
        y0_copied = sem("y0_copied")
        y1_copied = sem("y1_copied")
        ysb_free = [sem(f"ysb_free{b}") for b in range(2)]
        gat_in = [sem(f"gat_in{i}") for i in range(NT)]
        part_ok = sem("part_ok")
        x2_ok = sem("x2_ok")
        ss3_ok = sem("ss3_ok")
        ms3_ok = sem("ms3_ok")
        root3_ok = sem("root3_ok")
        res_ok = sem("res_ok")
        out_done = sem("out_done")
        dve_step = sem("dve_step")

        block = stack.enter_context(nc.Block())

        ada_v = ada_w[0].rearrange("(k p) n -> p k n", p=P)
        win_v = w_in[0].rearrange("(k p) n -> p k n", p=P)
        wout_v = w_out[0].rearrange("(k p) n -> p k n", p=P)
        x_v = x[0].rearrange("(t p) d -> p t d", p=P)
        ctx_v = ctx[0].rearrange("(t p) d -> p t d", p=P)
        out_v = out[0].rearrange("(t p) d -> p t d", p=P)

        def row_of(ap, n, parts=P):
            return bass.AP(ap.tensor, ap.offset, [[0, parts], [1, n]])

        A_V, A_B, A_C, P_IN, Q_IN, K_IN, V_IN, F_IN = range(8)
        ORDER = [K_IN, V_IN, Q_IN, F_IN, P_IN, A_V, A_C, A_B]
        FILL = [(F_IN, 0), (F_IN, 1), (P_IN, 0), (P_IN, 1), (A_V, 0), (A_V, 1),
                (A_C, 0), (A_C, 1), (A_B, 0), (A_B, 1)]
        N_ACT_FILL = 6
        UNITS = [(2 * g + h, j) for g in range(2) for j in range(4) for h in range(2)]
        NU = len(UNITS)

        def by_column(t):
            return t.rearrange("p (c r) -> p r c", r=ROWS)

        def natural(t):
            return t.rearrange("p (r c) -> p r c", r=ROWS)

        @block.sync
        def _(sp):
            sp.dma_start(vec[0:8, :], c.rearrange("a (k p) -> (a k) p", p=P)).then_inc(vec_in, 16)
            sp.dma_start(vec[8:16, :], c_ctx.rearrange("(k p) -> k p", p=P)).then_inc(vec_in, 16)
            sp.dma_start(vec[16:24, :], norm1_g.rearrange("a (k p) -> (a k) p", p=P)).then_inc(vec_in, 16)
            sp.dma_start(vec[24:26, :], pool_scale.rearrange("a (k p) -> (a k) p", p=P)).then_inc(vec_in, 16)
            sp.dma_start(vec[26:32, :], conv_w[0].rearrange("j (k p) -> (j k) p", p=P)).then_inc(vec_in, 16)
            sp.dma_start(vec[32:48, :], ada_b[0, 0:2 * D].rearrange("(k p) -> k p", p=P)).then_inc(vec_in, 16)
            sp.dma_start(ctx_sb[:], ctx_v).then_inc(ctx_in, 16)
            for i in range(2):
                sp.dma_start(x1[:, 2 * i:2 * i + 2, :], x_v[:, 2 * i:2 * i + 2, :]).then_inc(x_in[i], 16)
            for i in range(4):
                sp.dma_start(ada[i][:], ada_v[:, :, i * 512:(i + 1) * 512]).then_inc(ada_in[i], 16)
            for i in range(4):
                if i == 3:
                    sp.wait_ge(tr_ok, 4)
                n = ORDER[i]
                sp.dma_start(win[i][:], win_v[:, :, n * GW:(n + 1) * GW]).then_inc(win_in[i], 16)
            sp.wait_ge(rows_zero, 1)
            sp.dma_start(rows[0:1, :, :].rearrange("p a d -> p (a d)"),
                         ada_b[0:1, 2 * D:6 * D]).then_inc(adab_in, 16)
            sp.wait_ge(tab_zero, 1)
            sp.dma_start(tabpad[:, PAD_C * RPB_R:(PAD_C + RPB_C) * RPB_R],
                         rpb_t.rearrange("h v u -> h (v u)")).then_inc(tabpad_in, 16)
            sp.wait_ge(tabpad_in, 16)
            sp.dma_start(tab_dram, tabpad[:, :]).then_inc(tab_out, 16)
            sp.wait_ge(tab_out, 16)
            for h in range(HEADS):
                sp.dma_start(raw[:, h].rearrange("p a b -> p (a b)"),
                             bass.AP(tab_dram.tensor, h * TAB,
                                     [[RPB_R, 16], [1, ROWS], [1, RUN]])).then_inc(raw_in, 16)
            sp.wait_ge(pw_zero, 1)
            for g in range(4):
                q = HD * (g % 2)
                sp.dma_start(pw[q:q + HD, g // 2, q:q + HD], pool_w[0, g]).then_inc(poolw_in, 16)
            sp.dma_start(head_dft[:], dft_head).then_inc(consts_in, 16)
            sp.dma_start(rw[:], router_w.rearrange("(k p) e -> p k e", p=P)).then_inc(consts_in, 16)
            sp.dma_start(rb[:], bass.AP(router_b.tensor, router_b.offset,
                                        [[0, P], [0, NT], [1, NE]])).then_inc(consts_in, 16)
            for n in range(4, 12):
                if n < 8:
                    sp.wait_ge(ada_pe, n - 3)
                else:
                    sp.wait_ge(ada_dve, n - 7)
                sp.dma_start(ada[n % 4][:], ada_v[:, :, n * 512:(n + 1) * 512]).then_inc(ada_in[n % 4], 16)
            for i in range(4, 8):
                if i < 7:
                    sp.wait_ge(kv_ok, (4, 10, 12)[i - 4])
                else:
                    sp.wait_ge(pj_ok, 2)
                n = ORDER[i]
                sp.dma_start(win[i % 4][:], win_v[:, :, n * GW:(n + 1) * GW]).then_inc(win_in[i % 4], 16)
            sp.wait_ge(ada_dve, 8)
            sp.dma_start(cos_sb[:], dft_cos.rearrange("(t p) n -> p t n", p=P)).then_inc(dft_in, 16)
            sp.dma_start(sin_sb[:], dft_sin.rearrange("(t p) n -> p t n", p=P)).then_inc(dft_in, 16)
            sp.wait_ge(zero_ok, 1)
            sp.dma_start(y_dram[NE * P:, :].rearrange("(p b) (q n) -> p (b q) n", p=P, n=256),
                         zero[:].unsqueeze(1).to_broadcast([P, OVER * 4, 256])).then_inc(zero_stored, 16)
            sp.wait_ge(kv_ok, 12)
            for g in range(4):
                q = HD * (g % 2)
                sp.dma_start(inv[q:q + HD, g // 2, :], row_of(pool_inv[g], N, HD)).then_inc(inv_in, 16)
            for i in range(4):
                sp.wait_ge(pj_ok, 4 + 2 * i)
                sp.dma_start(wout[:, 2 * i:2 * i + 2, :], wout_v[:, 2 * i:2 * i + 2, :]).then_inc(wout_in[i], 16)
            sp.wait_ge(pj_ok, 10)
            sp.dma_start(n2g[:], row_of(norm2_g, D)).then_inc(n2g_in, 16)
            sp.wait_ge(o_ok, NU)
            sp.dma_start(fing[:], row_of(final_g, D)).then_inc(fing_in, 16)
            sp.wait_ge(zero_stored, 16)
            sp.wait_ge(fn_ok, 2)
            sp.wait_ge(pool_ps, 2)
            sp.wait_ge(o_copied, 2)
            sp.wait_ge(pj_dve, 4)
            sp.dma_start(w1_sb[1][:], moe_w1[0, 1].rearrange("(k p) f -> p k f", p=P)).then_inc(w1_in[1], 16)
            sp.dma_start(w3_sb[1][:], moe_w3[0, 1].rearrange("(k p) f -> p k f", p=P)).then_inc(w3_in[1], 16)
            sp.dma_start(w2_sb[1][:], moe_w2[0, 1].rearrange("(k p) f -> p k f", p=P)).then_inc(w2_in[1], 16)
            sp.dma_start(w3_sb[0][:], moe_w3[0, 0].rearrange("(k p) f -> p k f", p=P)).then_inc(w3_in[0], 16)
            sp.dma_start(w2_sb[0][:], moe_w2[0, 0].rearrange("(k p) f -> p k f", p=P)).then_inc(w2_in[0], 16)
            sp.wait_ge(wo_ok, 2 * NT)
            sp.dma_start(w1_sb[0][:], moe_w1[0, 0].rearrange("(k p) f -> p k f", p=P)).then_inc(w1_in[0], 16)

            def load_expert(b, e, s):
                sp.wait_ge(h1_ok, s - 1)
                sp.dma_start(w1_sb[b][:], moe_w1[0, bass.ds(e, 1)].rearrange("a (k p) f -> p (a k) f", p=P)
                             ).then_inc(w1_in[b], 16)
                sp.wait_ge(h3_ok, s - 1)
                sp.dma_start(w3_sb[b][:], moe_w3[0, bass.ds(e, 1)].rearrange("a (k p) f -> p (a k) f", p=P)
                             ).then_inc(w3_in[b], 16)
                sp.wait_ge(y1_ok, s - 1)
                sp.dma_start(w2_sb[b][:], moe_w2[0, bass.ds(e, 1)].rearrange("a (k p) f -> p (a k) f", p=P)
                             ).then_inc(w2_in[b], 16)

            with sp.Fori(1, NE // 2) as i:
                for b in range(2):
                    load_expert(b, i * 2 + b, i * 2 + b)
            sp.wait_ge(route_ok, 1)
            n_pairs = sp.value_load(ints[0:1, 8:9], min_val=0, max_val=OVER // 2) + NE // 2
            with sp.If(n_pairs > NE // 2):
                with sp.Fori(NE // 2, n_pairs) as i:
                    for b in range(2):
                        e = sp.value_load(ints[0:1, bass.ds(i * 2 + b - NE, 1)], min_val=0, max_val=NE - 1)
                        load_expert(b, e, i * 2 + b)

        @block.gpsimd
        def _(gp):
            step = [0]

            def link(ins):
                step[0] += 1
                ins.then_inc(gp_step, 1)
                gp.wait_ge(gp_step, step[0])

            link(gp.memset(ident[:], 0.0))
            gp.affine_select(out=ident[:], in_=ident[:], compare_op=ALU.not_equal, fill=1.0, base=0,
                             pattern=[[-1, P]], channel_multiplier=1).then_inc(ident_ok, 1)
            gp.memset(tabpad[:], 0.0).then_inc(tab_zero, 1)
            gp.memset(rows[:].rearrange("p a d -> p (a d)"), 0.0).then_inc(rows_zero, 1)
            gp.memset(pw[:].rearrange("p a d -> p (a d)"), 0.0).then_inc(pw_zero, 1)
            link(gp.memset(ones[:], 1.0))
            gp.affine_select(out=tri[:], in_=ones[:], compare_op=ALU.is_gt, fill=0.0, base=0,
                             pattern=[[1, P]], channel_multiplier=-1).then_inc(ones_ok, 1)
            gp.wait_ge(raw_in, 16 * HEADS)

            def from_left(dst, src_, j0, n):
                return gp.affine_select(out=dst, in_=src_, compare_op=ALU.is_ge, fill=-BIG, base=8 * j0 - 57,
                                        pattern=[[8, n], [0, ROWS]], channel_multiplier=-1)

            def from_right(dst, src_, j0, n):
                return gp.affine_select(out=dst, in_=src_, compare_op=ALU.is_ge, fill=-BIG, base=184 - 8 * j0,
                                        pattern=[[-8, n], [0, ROWS]], channel_multiplier=1)

            def seg(h, a, n=1):
                return bias[:, h, 16 * a:16 * (a + n), :]

            def key(h, a, n=1):
                return raw[:, h, 48 - 16 * (a + n):48 - 16 * a, 0:ROWS][:, ::-1, ::-1]

            for h in range(HEADS):
                from_left(seg(h, 0, 3), key(h, 0, 3), 0, 48)
                from_left(seg(h, 3), key(h, 1), 16, 16)
                from_right(seg(h, 4), key(h, 2), 32, 16)
                from_left(seg(h, 5), key(h, 0), 0, 16)
                link(from_right(seg(h, 6), key(h, 1), 16, 16))
                from_right(seg(h, 0, 3), seg(h, 0, 3), 0, 48).then_inc(bias_ok, 1)
            gp.wait_ge(ada_dve, 8)
            gp.memset(zero[:], 0.0).then_inc(zero_ok, 1)
            gp.memset(z[:, :, 0:1], 0.0)
            gp.memset(z[:, :, N + 1:N + 2], 0.0)
            gp.memset(up[:, :, 0:8], 0.0)
            gp.memset(up[:, :, N + 8:N + 16], 0.0).then_inc(pads_ok, 1)
            gp.wait_ge(o_ok, NU)
            gp.iota(pri4[:], [[0, NT], [-1, GROUPS]], base=GROUPS, channel_multiplier=0,
                    allow_small_or_imprecise_dtypes=True)
            gp.iota(pri16[:], [[0, NT], [-1, NE]], base=NE, channel_multiplier=0,
                    allow_small_or_imprecise_dtypes=True)
            gp.iota(eno[:], [[1, NE]], base=0, channel_multiplier=0, allow_small_or_imprecise_dtypes=True)
            gp.iota(iota_slot[:], [[1, P]], base=0, channel_multiplier=0, allow_small_or_imprecise_dtypes=True)
            gp.iota(iota_blk[:], [[1, NB]], base=0, channel_multiplier=0, allow_small_or_imprecise_dtypes=True)
            gp.iota(iota8[:], [[1, 8]], base=0, channel_multiplier=0, allow_small_or_imprecise_dtypes=True)
            gp.memset(cs[:, :, 0:8], 0.0)
            gp.iota(tok[:], [[P, NT]], base=-EMPTY, channel_multiplier=1,
                    allow_small_or_imprecise_dtypes=True).then_inc(iota_ok, 1)
            gp.wait_ge(logit_ok, 1)
            gp.memset(xg[0][:], 0.0)
            link(gp.memset(xg[1][:], 0.0))

            gp.wait_ge(route_ok, 1)
            gp.wait_ge(h2_stored, 16 * NT)
            n_pairs = gp.value_load(ints[0:1, 8:9], min_val=0, max_val=OVER // 2) + NE // 2

            def gather(b, s, i):
                if i is not None:
                    gp.wait_ge(xt_ok, s - 1)
                gp.wait_ge(route_ok, 1)
                gp.tensor_copy(idx1[b][:, 0:1], idx[:, bass.ds(s, 1)]).then_inc(idx1_ok, 1)
                gp.wait_ge(idx1_ok, s + 1)
                gp.sem_inc(gather_go, 1)
                gp.indirect_dma_start(xg[b][:], None, h2_dram,
                                      bass.IndirectOffsetOnAxis(ap=idx1[b][:, 0:1], axis=0),
                                      bounds_check=N - 1, oob_is_err=False).then_inc(xg_in[b], 16)

            for b in range(2):
                gather(b, b, None)
            with gp.Fori(1, n_pairs) as i:
                for b in range(2):
                    gather(b, i * 2 + b, i)
            gp.wait_ge(ysb_free[0], n_pairs * 16 + 16)
            gp.wait_ge(ysb_free[1], n_pairs * 16 + 16)
            gp.sem_inc(gather_go, 1)
            for t in range(NT):
                for k in range(2):
                    gp.indirect_dma_start(ygat[:, t, k, :], None, y_dram,
                                          bass.IndirectOffsetOnAxis(ap=slot_idx[:, t, k:k + 1], axis=0)
                                          ).then_inc(gat_in[t], 16)

        @block.tensor
        def _(pe):
            pe.wait_ge(vec_in, 96)
            pe.wait_ge(ident_ok, 1)
            pe.transpose(bank[7][:, 0:48], vec[:], ident[0:48, 0:48]).then_inc(vecT_ok, 1)
            pe.wait_ge(xn_ok, LT)
            for g in range(4):
                for i in range(4):
                    k, t = 2 * g + i // 2, i % 2
                    m = pe.transpose(bank[g % 6][:, i * P:(i + 1) * P], ctx_sb[:, t, k * P:(k + 1) * P], ident[:])
                m.then_inc(tr_ok, 1)
            pe.wait_ge(xn_ok, LT + NT)
            for g in range(4, 4 + KD):
                if g >= 6:
                    pe.wait_ge(tr_free, g - 5)
                for t in range(NT):
                    m = pe.transpose(bank[g % 6][:, t * P:(t + 1) * P],
                                     xn[:, t, (g - 4) * P:(g - 3) * P], ident[:])
                m.then_inc(tr_ok, 1)
            pe.wait_ge(cc_ok, 1)
            for n in range(16):
                if n % 4 == 0:
                    pe.wait_ge(ada_in[n // 4], 16)
                for k in range(KD):
                    m = pe.matmul(bank[6][:, 2 * n:2 * n + 2], ada[n // 4][:, k, (n % 4) * P:(n % 4 + 1) * P],
                                  cc[:, k, :], start=(k == 0), stop=(k == KD - 1))
                if n % 4 == 3:
                    m.then_inc(ada_pe, 1)

            def kv_tile(n, make):
                if n < 6:
                    pe.wait_ge(tr_free, min(12, 7 + n))
                else:
                    pe.wait_ge(kv_free, n - 5)
                m = make(bank[n % 6])
                m.then_inc(kv_ok, 1)
                return m

            def channel_tile(slot_, half, src, width):
                def make(b):
                    for k in range(KD):
                        m = pe.matmul(b[:, 0:width], win[slot_][:, k, half * P:(half + 1) * P],
                                      src[:, k, :], start=(k == 0), stop=(k == KD - 1))
                    return m
                return make

            def value_tile(slot_, lhs):
                def make(b):
                    for k in range(KD):
                        m = pe.matmul(b[:, 0:GW], lhs(k), win[slot_][:, k, :],
                                      start=(k == 0), stop=(k == KD - 1))
                    return m
                return make

            pe.wait_ge(win_in[0], 16)
            pe.wait_ge(hc_ok, 1)
            kv_tile(0, channel_tile(0, 0, hcT, L))
            kv_tile(1, channel_tile(0, 1, hcT, L))
            pe.wait_ge(h_ok, 1)
            kv_tile(2, channel_tile(0, 0, hT, N))
            kv_tile(3, channel_tile(0, 1, hT, N))
            pe.wait_ge(win_in[1], 16)
            for t in range(LT):
                kv_tile(4 + t, value_tile(1, lambda k: hcT[:, k, t * P:(t + 1) * P]))
            for m_ in range(NT):
                kv_tile(6 + m_, value_tile(1, lambda k: hT[:, k, m_ * P:(m_ + 1) * P]))
            pe.wait_ge(win_in[2], 16)
            kv_tile(10, channel_tile(2, 0, hT, N))
            kv_tile(11, channel_tile(2, 1, hT, N))

            def fill(n):
                tile, part = n // 2, n % 2
                if tile >= len(FILL):
                    return
                piece, half = FILL[tile]
                i = ORDER.index(piece)
                if part == 0:
                    if half == 0:
                        pe.wait_ge(win_in[i % 4], 16 * (i // 4 + 1))
                    if 1 <= tile <= N_ACT_FILL:
                        pe.wait_ge(pj_act, tile)
                    elif tile > N_ACT_FILL:
                        pe.wait_ge(pj_dve, tile - N_ACT_FILL)
                for k in range(4 * part, 4 * part + 4):
                    m = pe.matmul(bank[7][:], win[i % 4][:, k, half * P:(half + 1) * P], hT[:, k, :],
                                  start=(k == 0), stop=(k == KD - 1))
                if part == 1:
                    m.then_inc(pj_ok, 1)

            def scores(u):
                h, j = UNITS[u]
                m0, m1, _ = KEYS[j]
                q0 = HD * (h % 2)
                if u >= 2:
                    pe.wait_ge(ex_ok, u - 1)
                q = qT[q0:q0 + HD, h // 2, j * P:(j + 1) * P]
                pe.matmul(bank[2 * (u % 2)][:, 0:(m1 - m0) * P], q, kT[q0:q0 + HD, h // 2, m0 * P:m1 * P],
                          start=True, stop=True)
                pe.matmul(bank[2 * (u % 2) + 1][:, 0:L], q, kcT[q0:q0 + HD, h // 2, :],
                          start=True, stop=True).then_inc(s_ok, 1)

            def values(u):
                h, j = UNITS[u]
                m0, m1, _ = KEYS[j]
                nb = m1 - m0 + LT
                pe.wait_ge(pn_ok, u + 1)
                if u >= 1:
                    pe.wait_ge(pt_copied, u)
                for i in range(nb):
                    m = pe.transpose(bank[4 + i // 4][:, (i % 4) * P:(i % 4 + 1) * P],
                                     pr[:, u % 2, i * P:(i + 1) * P], ident[:])
                m.then_inc(pt_ok, 1)

            def output(u):
                h, j = UNITS[u]
                m0, m1, _ = KEYS[j]
                nb = m1 - m0 + LT
                pe.wait_ge(pt_copied, u + 1)
                if u == NU // 2:
                    pe.wait_ge(o_copied, 1)
                for i in range(nb):
                    w = m1 - m0
                    v = v_sb[:, m0 + i, h * HD:(h + 1) * HD] if i < w else vc_sb[:, i - w, h * HD:(h + 1) * HD]
                    m = pe.matmul(bank[6][HD * (h % 2):HD * (h % 2) + HD, j * P:(j + 1) * P], v,
                                  pT[:, u % 2, i * P:(i + 1) * P], start=(i == 0), stop=(i == nb - 1))
                m.then_inc(o_ok, 1)

            pe.wait_ge(kv_free, 12)
            nf = 0
            for u in range(NU + 2):
                if u < NU:
                    scores(u)
                if nf < 20:
                    fill(nf)
                    nf += 1
                if 1 <= u <= NU:
                    values(u - 1)
                if u % 2 == 0 and nf < 20:
                    fill(nf)
                    nf += 1
                if u >= 2:
                    output(u - 2)
            while nf < 20:
                fill(nf)
                nf += 1

            pe.wait_ge(poolw_in, 64)
            pe.wait_ge(d_ok, 1)
            pe.wait_ge(pj_dve, 4)
            for h in range(2):
                pe.matmul(bank[4 + h][:], pw[:, h, :], dpool[:, h, :],
                          start=True, stop=True).then_inc(pool_ps, 1)
            pe.wait_ge(consts_in, 48)
            for t in range(NT):
                for h in range(2):
                    m = pe.matmul(bank[t][:, h * GW:(h + 1) * GW], fT[:, h, t * P:(t + 1) * P], head_dft[:],
                                  start=True, stop=True)
                m.then_inc(fd_ok, 1)
            pe.wait_ge(dft_in, 32)
            pe.wait_ge(pool_ok, 2)
            for h in range(2):
                for t in range(NT):
                    if h == 0:
                        pe.wait_ge(fd_copied, t + 1)
                    pe.matmul(bank[4 + h][:], fcs[:, t, h, 0:P], cos_sb[:, t, :], start=(t == 0), stop=False)
                    m = pe.matmul(bank[4 + h][:], fcs[:, t, h, P:2 * P], sin_sb[:, t, :],
                                  start=False, stop=(t == NT - 1))
                m.then_inc(fn_ok, 1)
            pe.wait_ge(ones_ok, 1)
            pe.wait_ge(ada_dve, 8)
            for n in range(8):
                if n >= 4:
                    pe.wait_ge(rows_act, n - 3)
                pe.matmul(bank[n % 4][:], ones[:], rows[:, n // 2, (n % 2) * 512:(n % 2 + 1) * 512],
                          start=True, stop=True).then_inc(rowsum_ok, 1)
            for i in range(4):
                pe.wait_ge(wout_in[i], 16)
            pe.wait_ge(o_copied, 2)
            pe.wait_ge(fn_copied, 2)
            pe.wait_ge(rows_act, 8)
            def project(n):
                t, half = n // 2, n % 2
                if n >= 4:
                    pe.wait_ge(x1_ok, n - 3)
                for k in range(KD):
                    m = pe.matmul(bank[n % 4][:], yT[:, k, t * P:(t + 1) * P],
                                  wout[:, k, half * 512:(half + 1) * 512], start=(k == 0), stop=(k == KD - 1))
                m.then_inc(wo_ok, 1)

            def turn_h2(t):
                pe.wait_ge(h2_ok, t + 1)
                for g in range(2):
                    if t >= 1:
                        pe.wait_ge(h2T_ok, 2 * (t - 1) + g + 1)
                    for i in range(4):
                        k = 4 * g + i
                        m = pe.transpose(bank[4 + g][:, i * P:(i + 1) * P], h2[:, t % 2, k * P:(k + 1) * P], ident[:])
                    m.then_inc(h2tr_ok, 1)

            for t in range(NT):
                project(2 * t)
                project(2 * t + 1)
                if t >= 1:
                    turn_h2(t - 1)
            turn_h2(NT - 1)
            for t in range(NT):
                pe.wait_ge(h2T_ok, 2 * t + 2)
                for k in range(KD):
                    m = pe.matmul(bank[6][:, t * NE:(t + 1) * NE], h2T[:, k, t * P:(t + 1) * P], rw[:, k, :],
                                  start=(k == 0), stop=(k == KD - 1))
            m.then_inc(logit_ok, 1)
            pe.wait_ge(sel_ok, 1)
            for t in range(NT):
                for i in range(t + 1):
                    pe.matmul(bank[7][:, t * NE:(t + 1) * NE], tri[:] if i == t else ones[:],
                              sel[:, i, :], start=(i == 0), stop=(i == t))
            for i in range(NT):
                m = pe.matmul(bank[7][:, NT * NE:(NT + 1) * NE], ones[:], sel[:, i, :],
                              start=(i == 0), stop=(i == NT - 1))
            m.then_inc(rank_ok, 1)
            pe.wait_ge(hot_ok, 1)
            for i in range(2 * NT):
                m = pe.matmul(bank[7][:, 128:128 + NB], hot_slot[:, i, :], hot_blk[:, i, :],
                              start=(i == 0), stop=(i == 2 * NT - 1))
            m.then_inc(idxps_ok, 1)

            pe.wait_ge(route_ok, 1)
            n_pairs = pe.value_load(ints[0:1, 8:9], min_val=0, max_val=OVER // 2) + NE // 2

            def rows_in(b, s, i):
                pe.wait_ge(xg_in[b], i * 16 + 16)
                if not (isinstance(s, int) and s == 0):
                    pe.wait_ge(xt_copied, s)
                for k in range(KD):
                    m = pe.transpose(bank[k // 4][:, (k % 4) * P:(k % 4 + 1) * P], xg[b][:, k * P:(k + 1) * P], ident[:])
                m.then_inc(xt_ok, 1)

            def hidden(b, s, i, w, w_in_, ps, freed, ok):
                pe.wait_ge(w_in_[b], i * 16 + 16)
                if not (isinstance(s, int) and s == 0):
                    pe.wait_ge(freed, s)
                for k in range(KD):
                    m = pe.matmul(ps, xgT[b][:, k, :], w[b][:, k, :], start=(k == 0), stop=(k == KD - 1))
                m.then_inc(ok, 1)

            def hidden_turned(b, s):
                pe.wait_ge(he_ok, s + 1)
                if not (isinstance(s, int) and s == 0):
                    pe.wait_ge(het_copied, s)
                for k in range(KF):
                    m = pe.transpose(bank[4][:, k * P:(k + 1) * P], he[:, k * P:(k + 1) * P], ident[:])
                m.then_inc(het_ok, 1)

            def expert_out(b, s, i, half, copied, ok, first):
                if half == 0:
                    pe.wait_ge(w2_in[b], i * 16 + 16)
                    pe.wait_ge(het_copied, s + 1)
                if not first:
                    pe.wait_ge(copied, s)
                for k in range(KF):
                    m = pe.matmul(bank[5 + half][:], heT[:, k, :], w2_sb[b][:, k, half * 512:(half + 1) * 512],
                                  start=(k == 0), stop=(k == KF - 1))
                m.then_inc(ok, 1)

            def block_(b, s, i, prev, prev_i, prev_first):
                rows_in(b, s, i)
                if prev is not None:
                    expert_out(1 - b, prev, prev_i, 0, y0_copied, y0_ok, prev_first)
                pe.wait_ge(xt_copied, s + 1)
                hidden(b, s, i, w1_sb, w1_in, bank[2][:], sg_ok, h1_ok)
                hidden(b, s, i, w3_sb, w3_in, bank[3][:], he_ok, h3_ok)
                if prev is not None:
                    expert_out(1 - b, prev, prev_i, 1, y1_copied, y1_ok, prev_first)
                hidden_turned(b, s)

            block_(0, 0, 0, None, None, False)
            block_(1, 1, 0, 0, 0, True)
            with pe.Fori(1, n_pairs) as i:
                block_(0, i * 2, i, i * 2 - 1, i - 1, False)
                block_(1, i * 2 + 1, i, i * 2, i, False)
            last = n_pairs * 2 - 1
            expert_out(1, last, n_pairs - 1, 0, y0_copied, y0_ok, False)
            expert_out(1, last, n_pairs - 1, 1, y1_copied, y1_ok, False)

        @block.scalar
        def _(act):
            act.wait_ge(cols_ok, 1)
            act.activation(cc[:].rearrange("p k v -> p v k"), cols[:, 0:16].rearrange("p (v k) -> p v k", v=2),
                           ACT.Silu).then_inc(cc_ok, 1)
            for t in range(LT + NT):
                if t == 0:
                    act.wait_ge(ctx_in, 16)
                if t >= LT and (t - LT) % 2 == 0:
                    act.wait_ge(x_in[(t - LT) // 2], 16)
                src = ctx_sb[:, t, :] if t < LT else x1[:, t - LT, :]
                act.activation(hT[:, 2 * t:2 * t + 2, :].rearrange("p a n -> p (a n)") if t < LT
                               else xn[:, t - LT, :], src, ACT.Square,
                               accum_out=stat[:, t, 0:1]).then_inc(ss_ok, 1)
            for t in range(LT + NT):
                act.wait_ge(ms_ok, t + 1)
                act.activation(stat[:, t, 2:3], stat[:, t, 1:2], ACT.Sqrt).then_inc(root_ok, 1)
            for g in range(4 + KD):
                act.wait_ge(tr_ok, g + 1)
                b = bank[g % 6]
                if g < 4:
                    m = act.copy(hcT[:, 2 * g:2 * g + 2, :].rearrange("p a t -> p (a t)"), b)
                else:
                    m = act.copy(by_column(hT[:, g - 4, :]), natural(b))
                m.then_inc(tr_free, 1)
            for n in range(12):
                act.wait_ge(kv_ok, n + 1)
                if n == 0:
                    act.wait_ge(h_ok, 1)
                b = bank[n % 6]
                if n < 2:
                    m = act.copy(kcT[:, n, :], b[:, 0:L])
                elif n < 4:
                    m = act.copy(kT[:, n - 2, :], b)
                elif n < 6:
                    m = act.copy(vc_sb[:, n - 4, :], b[:, 0:GW])
                elif n < 10:
                    m = act.copy(v_sb[:, n - 6, :], b[:, 0:GW])
                else:
                    m = act.activation(qT[:, n - 10, :], b, ACT.Copy, scale=SCALE)
                m.then_inc(kv_free, 1)

            def fill_copy(n):
                piece, half = FILL[n]
                act.wait_ge(pj_ok, n + 1)
                if n == 0:
                    act.wait_ge(ada_dve, 8)
                    act.wait_ge(pads_ok, 1)
                dst = {F_IN: fT[:, half, :], P_IN: up[:, half, 8:8 + N], A_V: av[:, half, :]}[piece]
                act.copy(natural(dst), by_column(bank[7])).then_inc(pj_act, 1)

            def expo(u):
                h, j = UNITS[u]
                w = (KEYS[j][1] - KEYS[j][0]) * P
                s = u % 2
                act.wait_ge(nm_ok, u + 1)
                if u >= 2:
                    act.wait_ge(pt_ok, u - 1)
                act.activation(pr[:, s, 0:w], sw[:, s, 0:w], ACT.Exp, bias=soft[:, s, 2:3],
                               accum_out=soft[:, s, 3:4])
                act.activation(pr[:, s, w:w + L], bank[2 * s + 1][:, 0:L], ACT.Exp, bias=soft[:, s, 2:3],
                               accum_out=soft[:, s, 4:5]).then_inc(ex_ok, 1)

            def pt_copy(u):
                h, j = UNITS[u]
                n = (KEYS[j][1] - KEYS[j][0] + LT) * P
                act.wait_ge(pt_ok, u + 1)
                if u >= 2:
                    act.wait_ge(o_ok, u - 1)
                act.copy(pT[:, u % 2, 0:n], psum[:, 4:6, :].rearrange("p a n -> p (a n)")[:, 0:n]
                         ).then_inc(pt_copied, 1)

            done = 0
            nf = 0
            for u in range(NU + 2):
                if u < NU:
                    expo(u)
                nf += 1 if nf < 20 else 0
                if done < N_ACT_FILL and nf >= 2 * (done + 1):
                    fill_copy(done)
                    done += 1
                if 1 <= u <= NU:
                    pt_copy(u - 1)
                if u % 2 == 0:
                    nf += 1 if nf < 20 else 0
                    if done < N_ACT_FILL and nf >= 2 * (done + 1):
                        fill_copy(done)
                        done += 1
            for h in range(2):
                act.wait_ge(pool_ps, h + 1)
                act.activation(yT[:, 2 + h, :], bank[4 + h], ACT.Copy, scale=cols[:, 24 + h:25 + h]
                               ).then_inc(pool_ok, 1)
            for t in range(NT):
                act.wait_ge(fd_ok, t + 1)
                act.copy(fcs[:, t].rearrange("p a n -> p (a n)"), bank[t]).then_inc(fd_copied, 1)
            for h in range(2):
                act.wait_ge(fn_ok, h + 1)
                act.copy(yT[:, 6 + h, :], bank[4 + h]).then_inc(fn_copied, 1)
            for n in range(8):
                act.wait_ge(rowsum_ok, n + 1)
                act.copy(rows[:, n // 2, (n % 2) * 512:(n % 2 + 1) * 512], bank[n % 4]).then_inc(rows_act, 1)
            for t in range(NT):
                act.wait_ge(x1_ok, 2 * t + 2)
                if t >= 2:
                    act.wait_ge(h2tr_ok, 2 * t - 2)
                    act.wait_ge(h2_stored, 16 * t)
                act.activation(h2[:, t % 2, :], x1[:, t, :], ACT.Square, accum_out=st2[:, t, 0:1]).then_inc(ss2_ok, 1)
                act.wait_ge(ms2_ok, t + 1)
                act.activation(st2[:, t, 2:3], st2[:, t, 1:2], ACT.Sqrt).then_inc(root2_ok, 1)
                act.wait_ge(h2_ok, t + 1)
                act.dma_start(h2_dram[t * P:(t + 1) * P, :], h2[:, t % 2, :]).then_inc(h2_stored, 16)
                for g in range(2):
                    act.wait_ge(h2tr_ok, 2 * t + g + 1)
                    act.copy(h2T[:, 4 * g:4 * g + 4, t * P:(t + 1) * P],
                             bank[4 + g].rearrange("p (k t) -> p k t", t=P)).then_inc(h2T_ok, 1)
            act.wait_ge(logit_ok, 1)
            act.activation(prob[:].rearrange("p t e -> p (t e)"), bank[6][:, 0:NT * NE], ACT.Sigmoid
                           ).then_inc(prob_ok, 1)

            act.wait_ge(route_ok, 1)
            n_pairs = act.value_load(ints[0:1, 8:9], min_val=0, max_val=OVER // 2) + NE // 2

            def block_(b, s, store):
                act.wait_ge(h1_ok, s + 1)
                if not (isinstance(s, int) and s == 0):
                    act.wait_ge(he_ok, s)
                act.activation(sg[:], bank[2], ACT.Silu).then_inc(sg_ok, 1)
                act.wait_ge(het_ok, s + 1)
                act.copy(heT[:].rearrange("p k t -> p (k t)"), bank[4]).then_inc(het_copied, 1)
                if store is not None:
                    store_rows(1 - b, store)

            def store_rows(b, s):
                act.wait_ge(y1_copied, s + 1)
                act.dma_start(y_dram[bass.ds(s * P, P), :], ysb[b][:]).then_inc(ysb_free[b], 16)

            for b in range(2):
                act.sem_inc(ysb_free[b], 16)
            block_(0, 0, None)
            block_(1, 1, 0)
            with act.Fori(1, n_pairs) as i:
                block_(0, i * 2, i * 2 - 1)
                block_(1, i * 2 + 1, i * 2)
            store_rows(1, n_pairs * 2 - 1)

            for t in range(NT):
                act.wait_ge(x2_ok, t + 1)
                act.activation(ygat[:, t, 0, :], x1[:, t, :], ACT.Square, accum_out=st2[:, t, 3:4]).then_inc(ss3_ok, 1)
                act.wait_ge(ms3_ok, t + 1)
                act.activation(st2[:, t, 5:6], st2[:, t, 4:5], ACT.Sqrt).then_inc(root3_ok, 1)
            for t in range(NT):
                act.wait_ge(res_ok, t + 1)
                act.dma_start(out_v[:, t, :], ygat[:, t, 1, :]).then_inc(out_done, 16)
            act.wait_ge(out_done, 16 * NT)

        @block.vector
        def _(v):
            step = [0]

            def link(ins):
                step[0] += 1
                ins.then_inc(dve_step, 1)
                v.wait_ge(dve_step, step[0])

            v.wait_ge(vecT_ok, 1)
            v.tensor_copy(cols[:], bank[7][:, 0:48]).then_inc(cols_ok, 1)
            for t in range(LT + NT):
                v.wait_ge(ss_ok, t + 1)
                v.tensor_scalar(stat[:, t, 1:2], stat[:, t, 0:1], 1.0 / D, EPS, ALU.mult, ALU.add).then_inc(ms_ok, 1)
            for t in range(LT + NT):
                v.wait_ge(root_ok, t + 1)
                link(v.reciprocal(stat[:, t, 3:4], stat[:, t, 2:3]))
                src = ctx_sb[:, t, :] if t < LT else x1[:, t - LT, :]
                dst = ctx_sb[:, t, :] if t < LT else xn[:, t - LT, :]
                if t == LT:
                    v.wait_ge(ss_ok, LT + NT)
                v.tensor_scalar(dst, src, stat[:, t, 3:4], None, ALU.mult).then_inc(xn_ok, 1)
            v.wait_ge(ada_pe, 4)
            v.wait_ge(cols_ok, 1)
            link(v.tensor_tensor(modc[:], bank[6][:, 0:32].rearrange("p (n v) -> p n v", v=2),
                                 cols[:, 32:48].unsqueeze(2).to_broadcast([P, 16, 2]), ALU.add))
            v.wait_ge(dve_step, step[0])
            link(v.scalar_tensor_tensor(out=a1[:], in0=modc[:, 8:16, :], scalar=1.0,
                                        in1=cols[:, 16:24].unsqueeze(2).to_broadcast([P, 8, 2]),
                                        op0=ALU.add, op1=ALU.mult))
            v.wait_ge(tr_free, 4)
            for k in range(KD):
                m = v.tensor_scalar(hcT[:, k, :], hcT[:, k, :], a1[:, k, 1:2], modc[:, k, 1:2], ALU.mult, ALU.add)
            m.then_inc(hc_ok, 1)
            v.wait_ge(tr_free, 12)
            for k in range(KD):
                m = v.tensor_scalar(hT[:, k, :], hT[:, k, :], a1[:, k, 0:1], modc[:, k, 0:1], ALU.mult, ALU.add)
            m.then_inc(h_ok, 1)
            v.wait_ge(adab_in, 16)
            for n in range(4, 12):
                v.wait_ge(ada_in[n % 4], 16 * (n // 4 + 1))
                o = rows[:, (n - 4) // 2, (n % 2) * 512:(n % 2 + 1) * 512]
                for k in range(KD):
                    ins = v.scalar_tensor_tensor(out=o, in0=ada[n % 4][:, k, :], scalar=cc[:, k, 0:1], in1=o,
                                                 op0=ALU.mult, op1=ALU.add)
                    if k < KD - 1:
                        link(ins)
                ins.then_inc(ada_dve, 1)

            def softmax_bias(u):
                h, j = UNITS[u]
                m0, m1, sg0 = KEYS[j]
                w = (m1 - m0) * P
                s = u % 2
                v.wait_ge(s_ok, u + 1)
                b = bias[:, h, sg0 * 16:(sg0 + m1 - m0) * 16, :].rearrange("p a b -> p (a b)")
                v.tensor_tensor_reduce(sw[:, s, 0:w], bank[2 * s][:, 0:w], b, 1.0, -3e38, ALU.add, ALU.max,
                                       soft[:, s, 0:1]).then_inc(sb_ok, 1)
                link(v.tensor_reduce(soft[:, s, 1:2], bank[2 * s + 1][:, 0:L], AX, ALU.max))
                v.wait_ge(sb_ok, u + 1)
                v.tensor_scalar(soft[:, s, 2:3], soft[:, s, 0:1], soft[:, s, 1:2], -1.0, ALU.max, ALU.mult
                                ).then_inc(nm_ok, 1)

            def softmax_norm(u):
                h, j = UNITS[u]
                w = (KEYS[j][1] - KEYS[j][0]) * P
                s = u % 2
                v.wait_ge(ex_ok, u + 1)
                link(v.tensor_tensor(soft[:, s, 5:6], soft[:, s, 3:4], soft[:, s, 4:5], ALU.add))
                link(v.reciprocal(soft[:, s, 6:7], soft[:, s, 5:6]))
                v.tensor_scalar(pr[:, s, 0:w + L], pr[:, s, 0:w + L], soft[:, s, 6:7], None, ALU.mult
                                ).then_inc(pn_ok, 1)

            def head_pair(g):
                v.wait_ge(o_ok, NU // 2 * (g + 1))
                v.tensor_copy(yT[:, 4 + g, :].rearrange("p (r c) -> p c r", r=ROWS),
                              bank[6].rearrange("p (c r) -> p c r", r=ROWS)).then_inc(o_copied, 1)

            def pool_diff():
                W = N + 16
                v.wait_ge(pj_act, 4)
                v.wait_ge(pads_ok, 1)
                v.wait_ge(inv_in, 64)
                link(v.tensor_tensor(s2[:, :, 1:W], up[:, :, 1:W], up[:, :, 0:W - 1], ALU.add))
                link(v.tensor_tensor(s4[:, :, 2:W - 1], s2[:, :, 1:W - 2], s2[:, :, 3:W], ALU.add))
                link(v.tensor_tensor(s8[:, 4:W - 3], s4[:, 1, 2:W - 5], s4[:, 1, 6:W - 1], ALU.add))
                link(v.tensor_tensor(dpool[HD:P, 1, :], s8[HD:P, 4:4 + N], s8[HD:P, 12:12 + N], ALU.add))
                c0 = slice(8, 8 + N)
                v.tensor_tensor(dpool[0:HD, 0, :], s2[0:HD, 0, c0], inv[0:HD, 0, :], ALU.mult)
                v.tensor_tensor(dpool[HD:P, 0, :], s4[HD:P, 0, c0], inv[HD:P, 0, :], ALU.mult)
                v.tensor_tensor(dpool[0:HD, 1, :], s8[0:HD, c0], inv[0:HD, 1, :], ALU.mult)
                link(v.tensor_tensor(dpool[HD:P, 1, :], dpool[HD:P, 1, :], inv[HD:P, 1, :], ALU.mult))
                v.tensor_tensor(dpool[:], dpool[:], up[:, :, c0], ALU.subtract).then_inc(d_ok, 1)

            def conv_in(h):
                v.wait_ge(pj_ok, 7 + h)
                if h == 0:
                    v.wait_ge(pj_act, 6)
                    v.wait_ge(pads_ok, 1)
                v.tensor_tensor(natural(z[:, h, 1:1 + N]), by_column(bank[7]), natural(av[:, h, :]), ALU.mult).then_inc(pj_dve, 1)

            def conv(h):
                v.wait_ge(pj_dve, h + 1)
                link(v.tensor_scalar(cv[:, h, :], z[:, h, 0:N], cols[:, 26 + h:27 + h], None, ALU.mult))
                link(v.scalar_tensor_tensor(out=cv[:, h, :], in0=z[:, h, 1:1 + N], scalar=cols[:, 28 + h:29 + h],
                                            in1=cv[:, h, :], op0=ALU.mult, op1=ALU.add))
                link(v.scalar_tensor_tensor(out=cv[:, h, :], in0=z[:, h, 2:2 + N], scalar=cols[:, 30 + h:31 + h],
                                            in1=cv[:, h, :], op0=ALU.mult, op1=ALU.add))

            def conv_out(h):
                v.wait_ge(pj_ok, 9 + h)
                v.tensor_tensor(natural(yT[:, h, :]), by_column(bank[7]), natural(cv[:, h, :]), ALU.mult).then_inc(pj_dve, 1)

            v.wait_ge(bias_ok, HEADS)
            late = [(8, pool_diff), (14, lambda: conv_in(0)), (16, lambda: (conv_in(1), conv(0), conv(1))),
                    (18, lambda: conv_out(0)), (20, lambda: conv_out(1))]
            nf = 0
            for u in range(NU + 2):
                while late and nf >= late[0][0]:
                    late.pop(0)[1]()
                if u == NU // 2 + 2:
                    head_pair(0)
                if u < NU:
                    softmax_bias(u)
                    softmax_norm(u)
                nf = min(20, nf + 1 + (u % 2 == 0))
            while late:
                late.pop(0)[1]()
            head_pair(1)
            v.wait_ge(n2g_in, 16)
            v.wait_ge(rows_act, 8)
            link(v.scalar_tensor_tensor(out=rows[:, SC2, :], in0=rows[:, SC2, :], scalar=1.0, in1=n2g[:],
                                        op0=ALU.add, op1=ALU.mult))
            def residual(n):
                t, half = n // 2, n % 2
                cs_ = slice(half * 512, (half + 1) * 512)
                v.wait_ge(wo_ok, n + 1)
                tmpv = rtmp[:, half, :]
                link(v.tensor_tensor(tmpv, bank[n % 4], rows[:, G1, cs_], ALU.mult))
                v.tensor_tensor(x1[:, t, cs_], x1[:, t, cs_], tmpv, ALU.add).then_inc(x1_ok, 1)

            def norm2(t):
                v.wait_ge(ss2_ok, t + 1)
                v.tensor_scalar(st2[:, t, 1:2], st2[:, t, 0:1], 1.0 / D, EPS, ALU.mult, ALU.add).then_inc(ms2_ok, 1)
                v.wait_ge(root2_ok, t + 1)
                link(v.reciprocal(st2[:, t, 3:4], st2[:, t, 2:3]))
                link(v.scalar_tensor_tensor(out=h2[:, t % 2, :], in0=x1[:, t, :], scalar=st2[:, t, 3:4],
                                            in1=rows[:, SC2, :], op0=ALU.mult, op1=ALU.mult))
                v.tensor_tensor(h2[:, t % 2, :], h2[:, t % 2, :], rows[:, SH2, :], ALU.add).then_inc(h2_ok, 1)

            for t in range(NT):
                residual(2 * t)
                residual(2 * t + 1)
                if t >= 1:
                    norm2(t - 1)
            norm2(NT - 1)

            E4 = [P, NT, GROUPS]

            def wide(ap, shape):
                return ap.to_broadcast(shape)

            v.wait_ge(prob_ok, 1)
            v.wait_ge(consts_in, 48)
            v.wait_ge(iota_ok, 1)
            link(v.tensor_tensor(biased[:], prob[:], rb[:], ALU.add))
            b4 = biased[:].rearrange("p t (g e) -> p (t g) e", g=GROUPS)
            v.tensor_tensor(pairs[:, :, 0:3], b4[:, :, 0:3], b4[:, :, 1:4], ALU.add)
            v.tensor_tensor(pairs[:, :, 3:5], b4[:, :, 0:2], b4[:, :, 2:4], ALU.add)
            link(v.tensor_tensor(pairs[:, :, 5:6], b4[:, :, 0:1], b4[:, :, 3:4], ALU.add))
            link(v.tensor_reduce(gs[:].rearrange("p t g -> p (t g)").unsqueeze(2), pairs[:], AX, ALU.max))

            def first_max(src, pri, shape, dst, tmp):
                link(v.tensor_reduce(r1[:], src, AX, ALU.max))
                link(v.tensor_tensor(tmp, src, wide(r1[:], shape), ALU.is_equal))
                link(v.tensor_tensor(tmp, tmp, pri, ALU.mult))
                link(v.tensor_reduce(r2[:], tmp, AX, ALU.max))
                link(v.tensor_tensor(dst, tmp, wide(r2[:], shape), ALU.is_equal))

            first_max(gs[:], pri4[:], E4, geq[:], pen[:])
            link(v.tensor_scalar(pen[:], geq[:], -1.0, BIG, ALU.add, ALU.mult))
            g16 = [P, NT * GROUPS, 4]
            ra4 = ra[:].rearrange("p t (g e) -> p (t g) e", g=GROUPS)
            link(v.tensor_tensor(ra4, b4, wide(geq[:].rearrange("p t g -> p (t g)").unsqueeze(2), g16), ALU.mult))
            link(v.tensor_tensor(ra4, ra4, wide(pen[:].rearrange("p t g -> p (t g)").unsqueeze(2), g16), ALU.add))
            E16 = [P, NT, NE]
            first_max(ra[:], pri16[:], E16, oh[:, :, 0, :], rbuf[:])
            link(v.scalar_tensor_tensor(out=ra[:], in0=oh[:, :, 0, :], scalar=-3 * BIG, in1=ra[:],
                                        op0=ALU.mult, op1=ALU.add))
            first_max(ra[:], pri16[:], E16, oh[:, :, 1, :], rbuf[:])
            v.tensor_tensor(sel[:], oh[:, :, 0, :], oh[:, :, 1, :], ALU.add).then_inc(sel_ok, 1)

            E2 = [P, NT, 2, NE]

            def pick(dst, src):
                link(v.tensor_tensor(rc[:], oh[:], src.unsqueeze(2).to_broadcast(E2), ALU.mult))
                link(v.tensor_reduce(dst.rearrange("p t k -> p (t k)").unsqueeze(2),
                                     rc[:].rearrange("p t k e -> p (t k) e"), AX, ALU.add))

            pick(wsel[:], prob[:])
            link(v.tensor_tensor(den[:], wsel[:, :, 0:1], wsel[:, :, 1:2], ALU.add))
            link(v.reciprocal(den[:], den[:]))
            link(v.tensor_tensor(gate[:], wsel[:], wide(den[:], [P, NT, 2]), ALU.mult))
            v.wait_ge(rank_ok, 1)
            rank_ps = bank[7][:, 0:NT * NE]
            v.tensor_copy(cnt[:], bank[7][:, NT * NE:(NT + 1) * NE])
            link(v.tensor_copy(rank[:].rearrange("p t e -> p (t e)"), rank_ps))

            def above(dst, src, tmp, limits):
                link(v.tensor_scalar(dst, src, float(limits[0]), None, ALU.is_ge))
                for x_ in limits[1:]:
                    link(v.tensor_scalar(tmp, src, float(x_), None, ALU.is_ge))
                    link(v.tensor_tensor(dst, dst, tmp, ALU.add))

            above(ext[:], cnt[:], ra[:, 0, :], [P + 1, 2 * P + 1, 3 * P + 1])
            link(v.tensor_copy(cs[:, 0, 8:], ext[:]))
            for i, sh in enumerate((1, 2, 4, 8)):
                a, b = cs[:, i % 2, :], cs[:, 1 - i % 2, :]
                link(v.tensor_tensor(b[:, 8:], a[:, 8:], a[:, 8 - sh:8 - sh + NE], ALU.add))
            run = cs[:, 0, 8:]
            link(v.tensor_tensor(cnt[:], run, ext[:], ALU.subtract))
            link(v.scalar_tensor_tensor(out=cnt[:], in0=cnt[:], scalar=float(NE - 1), in1=eno[:],
                                        op0=ALU.add, op1=ALU.subtract))
            above(over[:], rank[:], ra[:], [P, 2 * P, 3 * P])
            link(v.tensor_scalar(ra[:], over[:], 0.0, None, ALU.is_gt))
            link(v.tensor_tensor(ra[:], ra[:], cnt[:].unsqueeze(1).to_broadcast(E16), ALU.mult))
            link(v.tensor_tensor(ra[:], ra[:], eno[:].unsqueeze(1).to_broadcast(E16), ALU.add))
            link(v.scalar_tensor_tensor(out=ra[:], in0=ra[:], scalar=float(P), in1=rank[:],
                                        op0=ALU.mult, op1=ALU.add))
            pick(slot[:], ra[:])
            link(v.scalar_tensor_tensor(out=ra[:], in0=over[:], scalar=-float(P), in1=rank[:],
                                        op0=ALU.mult, op1=ALU.add))
            pick(rmod[:], ra[:])
            v.tensor_copy(slot_idx[:], slot[:])
            link(v.tensor_tensor(blk_no[:], slot[:], rmod[:], ALU.subtract))
            link(v.tensor_scalar(blk_no[:], blk_no[:], 1.0 / P, None, ALU.mult))
            for i in range(2 * NT):
                t, k = i // 2, i % 2
                v.tensor_scalar(hot_slot[:, i, :], iota_slot[:], rmod[:, t, k:k + 1], None, ALU.is_equal)
                m = v.tensor_scalar(hot_blk[:, i, :], iota_blk[:], blk_no[:, t, k:k + 1], tok[:, t:t + 1],
                                    ALU.is_equal, ALU.mult)
            m.then_inc(hot_ok, 1)
            run0 = cs[0:1, 0, 8:]
            link(v.tensor_tensor(ov[:], run0.unsqueeze(1).to_broadcast([1, 8, NE]),
                                 iota8[:].unsqueeze(2).to_broadcast([1, 8, NE]), ALU.is_le))
            link(v.tensor_reduce(ovf[:, 0:8].unsqueeze(2), ov[:], AX, ALU.add))
            link(v.tensor_scalar(ovf[:, 0:8], ovf[:, 0:8], float(NE - 1), None, ALU.min))
            above(ovf[:, 8:9], cs[0:1, 0, 8 + NE - 1:8 + NE], ovf[:, 9:10], [1, 3, 5, 7])
            v.tensor_copy(ints[:, 0:9], ovf[:, 0:9])
            v.wait_ge(idxps_ok, 1)
            link(v.tensor_scalar(hot_blk[:, 0, :], bank[7][:, 128:128 + NB], float(EMPTY), None, ALU.add))
            v.tensor_copy(idx[:], hot_blk[:, 0, :]).then_inc(route_ok, 1)

            v.wait_ge(route_ok, 1)
            n_pairs = v.value_load(ints[0:1, 8:9], min_val=0, max_val=OVER // 2) + NE // 2

            def turned_rows(b, s):
                v.wait_ge(xt_ok, s + 1)
                if not (isinstance(s, int) and s < 2):
                    v.wait_ge(h3_ok, s - 1)
                v.tensor_copy(xgT[b][:].rearrange("p k t -> p (k t)"),
                              psum[:, 0:2, :].rearrange("p a n -> p (a n)")).then_inc(xt_copied, 1)

            def gated(b, s):
                v.wait_ge(h3_ok, s + 1)
                v.wait_ge(sg_ok, s + 1)
                if not (isinstance(s, int) and s == 0):
                    v.wait_ge(het_ok, s)
                v.tensor_tensor(he[:], bank[3], sg[:], ALU.mult).then_inc(he_ok, 1)

            def expert_rows(b, s, i, half, ok, copied):
                v.wait_ge(ok, s + 1)
                if half == 0 and i is not None:
                    v.wait_ge(ysb_free[b], i * 16 + 16)
                cs_ = slice(half * 512, (half + 1) * 512)
                v.tensor_tensor(ysb[b][:, cs_], bank[5 + half], rows[:, G2, cs_], ALU.mult).then_inc(copied, 1)

            def block_(b, s, prev, prev_i):
                turned_rows(b, s)
                if prev is not None:
                    expert_rows(1 - b, prev, prev_i, 0, y0_ok, y0_copied)
                gated(b, s)
                if prev is not None:
                    expert_rows(1 - b, prev, prev_i, 1, y1_ok, y1_copied)

            block_(0, 0, None, None)
            block_(1, 1, 0, None)
            with v.Fori(1, n_pairs) as i:
                block_(0, i * 2, i * 2 - 1, i - 1)
                block_(1, i * 2 + 1, i * 2, i)
            expert_rows(1, n_pairs * 2 - 1, n_pairs - 1, 0, y0_ok, y0_copied)
            expert_rows(1, n_pairs * 2 - 1, n_pairs - 1, 1, y1_ok, y1_copied)

            for t in range(NT):
                v.wait_ge(gat_in[t], 32)
                link(v.scalar_tensor_tensor(out=x1[:, t, :], in0=ygat[:, t, 0, :], scalar=gate[:, t, 0:1],
                                            in1=x1[:, t, :], op0=ALU.mult, op1=ALU.add))
                v.scalar_tensor_tensor(out=x1[:, t, :], in0=ygat[:, t, 1, :], scalar=gate[:, t, 1:2],
                                       in1=x1[:, t, :], op0=ALU.mult, op1=ALU.add).then_inc(x2_ok, 1)
                v.wait_ge(ss3_ok, t + 1)
                v.tensor_scalar(st2[:, t, 4:5], st2[:, t, 3:4], 1.0 / D, EPS, ALU.mult, ALU.add).then_inc(ms3_ok, 1)
                v.wait_ge(root3_ok, t + 1)
                link(v.reciprocal(st2[:, t, 5:6], st2[:, t, 5:6]))
                if t == 0:
                    v.wait_ge(fing_in, 16)
                v.scalar_tensor_tensor(out=ygat[:, t, 1, :], in0=x1[:, t, :], scalar=st2[:, t, 5:6], in1=fing[:],
                                       op0=ALU.mult, op1=ALU.mult).then_inc(res_ok, 1)


def constants():
    n = np.arange(N)
    turn = 2 * np.pi * (np.outer(n, n) % N) / N
    m = np.arange(HD)
    head = 2 * np.pi * (np.outer(m, m) % HD) / HD
    scale = 1 / np.sqrt(N * HD)
    dft_head = np.zeros((P, 2 * P))
    for h in range(2):
        dft_head[h * HD:(h + 1) * HD, h * HD:(h + 1) * HD] = np.cos(head) * scale
        dft_head[h * HD:(h + 1) * HD, P + h * HD:P + (h + 1) * HD] = -np.sin(head) * scale
    sizes = [np.minimum(n + w // 2, N) - np.maximum(n - w // 2, 0) for w in (2, 4, 8, 16)]
    return {
        "dft_cos": np.cos(turn).astype(np.float32),
        "dft_sin": np.sin(turn).astype(np.float32),
        "dft_head": dft_head.astype(np.float32),
        "pool_inv": (1 / np.stack(sizes)).astype(np.float32),
    }


_INS = ["x", "c", "ctx", "c_ctx", "ada_w", "ada_b", "norm1_g", "norm2_g", "w_in", "conv_w", "pool_w",
        "pool_scale", "rpb_t", "w_out", "router_w", "router_b", "moe_w1", "moe_w3", "moe_w2", "final_g",
        "dft_cos", "dft_sin", "dft_head", "pool_inv"]


def kernel(**inputs):
    import concourse.bacc as bacc
    from concourse.bass_utils import run_bass_kernel_spmd

    nc = bacc.Bacc("TRN2", target_bir_lowering=False, num_devices=1)
    given = {k: np.ascontiguousarray(v) for k, v in inputs.items()}
    given["rpb_t"] = np.ascontiguousarray(given.pop("na_rpb")[0].transpose(0, 2, 1)[:, ::-1, ::-1])
    given.update(constants())
    arrays, args = {}, []
    for name in _INS:
        a = given[name]
        arrays[f"in_{name}"] = a
        args.append(nc.dram_tensor(f"in_{name}", a.shape, mybir.dt.from_np(a.dtype), kind="ExternalInput").ap())
    args.append(nc.dram_tensor("out_0", (1, N, D), F32, kind="ExternalOutput").ap())
    build(nc, *args)
    r = run_bass_kernel_spmd(nc, [arrays], core_ids=[0])
    return r.results[0]["out_0"]
```

```python
from contextlib import ExitStack

import numpy as np

import concourse.bass as bass
from concourse import mybir

F32 = mybir.dt.float32
I32 = mybir.dt.int32
F32R = mybir.dt.float32r
BF16 = mybir.dt.bfloat16
ALU = mybir.AluOpType
ACT = mybir.ActivationFunctionType
AX = mybir.AxisListType.X

P = 128
D = 1024
N = 512
L = 256
KD = D // P
NT = N // P
LT = L // P
GW = 256
HD = 64
HEADS = GW // HD
ROWS, COLS = 8, 64
WIN_COLS = 16
RPB_R, RPB_C = 15, 31
NE = 16
GROUPS = 4
FF = 512
KF = FF // P
EPS = 1e-6
SCALE = HD ** -0.5
BIG = 1e30
OVER = 8
NB = NE + OVER
EMPTY = 4096
PAD_C = 16
TAB = 960
RUN = 48 * RPB_R
NSEG = 7
KEYS = [(0, 2, 3), (0, 3, 0), (1, 4, 0), (2, 4, 5)]
K1 = 1024


def build(nc, x, c, ctx, c_ctx, ada_w, ada_b, norm1_g, norm2_g, w_in, conv_w, pool_w, pool_scale,
          rpb_t, w_out, router_w, router_b, moe_w1, moe_w3, moe_w2, final_g,
          dft_cos, dft_sin, dft_head, pool_inv, out):
    h2_dram = nc.dram_tensor("h2_rows", (N, D), F32, kind="Internal").ap()
    y_dram = nc.dram_tensor("expert_rows", (NB * P, D), F32, kind="Internal").ap()
    tab_dram = nc.dram_tensor("bias_table", (HEADS, TAB), F32, kind="Internal").ap()

    base = (nc.sbuf_base + 31) // 32 * 32
    stack = ExitStack()
    with stack:
        def at(name, offset, shape, dt=F32):
            return nc.alloc_sbuf_tensor_at(name, shape, dt, offset=base + int(offset))

        def sem(name):
            return stack.enter_context(nc.semaphore(name))

        w1_sb = [at(f"w1_{b}", 48 * K1 * b, [P, KD, FF]) for b in range(2)]
        w3_sb = [at(f"w3_{b}", 48 * K1 * b + 16 * K1, [P, KD, FF]) for b in range(2)]
        w2_sb = [at(f"w2_{b}", 48 * K1 * b + 32 * K1, [P, KF, D]) for b in range(2)]
        ada = [at(f"ada_{i}", 16 * K1 * i, [P, KD, 512]) for i in range(4)]
        yT = at("yT", 0, [P, 8, N])
        av = at("av", 16 * K1, [P, 2, N])
        z = at("z", 20 * K1, [P, 2, N + 2])
        cv = at("cv", 25 * K1, [P, 2, N])
        s8 = at("s8", 29 * K1, [P, N + 16])
        up = at("up", 32 * K1, [P, 2, N + 16])
        s2 = at("s2", 36.5 * K1, [P, 2, N + 16])
        s4 = at("s4", 41 * K1, [P, 2, N + 16])
        zero = at("zero", 46 * K1, [P, 256])
        cos_sb = at("cos_sb", 48 * K1, [P, NT, N])
        sin_sb = at("sin_sb", 56 * K1, [P, NT, N])
        bias = at("bias", 64 * K1, [P, HEADS, NSEG * 16, ROWS])
        raw = at("raw", 78 * K1, [P, HEADS, 48, RPB_R])
        sw = at("sw", 78 * K1, [P, 2, 384])
        pr = at("pr", 81 * K1, [P, 2, 640])
        pT = at("pT", 86 * K1, [P, 2, 640])
        tabpad = at("tabpad", 91 * K1, [HEADS, TAB])
        dpool = at("dpool", 91 * K1, [P, 2, N])
        win = [at(f"win_{i}", (96 + 8 * i) * K1, [P, KD, GW]) for i in range(4)]
        ctx_sb = at("ctx_sb", 120 * K1, [P, LT, D])
        mod_rows = at("mod_rows", 112 * K1, [2, 4, 512])
        wout = at("wout", 96 * K1, [P, KD, D])
        hT_hi = at("hT_hi", 48 * K1, [P, KD, N], F32R)
        hT_lo = at("hT_lo", 160 * K1, [P, KD, N], F32R)
        win_hi = [at(f"win_hi_{i}", 12 * K1 * i, [P, KD, P], F32R) for i in range(2)]
        win_lo = [at(f"win_lo_{i}", (96 + 8 * i) * K1, [P, KD, GW], F32R) for i in range(4)]
        wout_hi = at("wout_hi", 16 * K1, [P, KD, D], F32R)
        wout_lo = at("wout_lo", 96 * K1, [P, KD, D], F32R)
        yT_hi = at("yT_hi", 64 * K1, [P, 8, N], F32R)
        yT_lo = at("yT_lo", 0, [P, 8, N], F32R)
        ygat = at("ygat", 96 * K1, [P, NT, 2, D])
        x1 = at("x1", 128 * K1, [P, NT, D])
        rows = at("rows", 144 * K1, [P, 4, D])
        G1, SH2, SC2, G2 = range(4)
        hT = at("hT", 160 * K1, [P, KD, N])
        hcT = at("hcT", 176 * K1, [P, KD, L])
        fcs = at("fcs", 160 * K1, [P, NT, 2, 2 * P])
        n2g = at("n2g", 168 * K1, [P, D])
        h2T = at("h2T", 160 * K1, [P, KD, N])
        h2 = at("h2", 176 * K1, [P, 2, D])
        fT = at("fT", 176 * K1, [P, 2, N])
        inv = at("inv", 180 * K1, [P, 2, N])
        hot_slot = at("hot_slot", 172 * K1, [P, NT * 2, P], BF16)
        hot_tok = at("hot_tok", 174 * K1, [P, NT * 2, 2, NB], BF16)
        xg = [at(f"xg_{b}", (160 + 4 * b) * K1, [P, D]) for b in range(2)]
        xgT = [at(f"xgT_{b}", (168 + 4 * b) * K1, [P, KD, P]) for b in range(2)]
        ysb = [at(f"ysb_{b}", (176 + 4 * b) * K1, [P, D]) for b in range(2)]
        xn = at("xn", 184 * K1, [P, NT, D])
        qT = at("qT", 184 * K1, [P, 2, N])
        kT = at("kT", 188 * K1, [P, 2, N])
        kcT = at("kcT", 192 * K1, [P, 2, L])
        v_sb = at("v_sb", 194 * K1, [P, NT, GW])
        vc_sb = at("vc_sb", 198 * K1, [P, LT, GW])
        rtmp = at("rtmp", 184 * K1, [P, 2, 512])
        sg = at("sg", 184 * K1, [P, FF])
        he = at("he", 186 * K1, [P, FF])
        heT = at("heT", 188 * K1, [P, KF, P])
        fing = at("fing", 190 * K1, [P, D])
        cursor = [194 * K1, 200 * K1]

        def small(name, shape, dt=F32, pool=1):
            n = int(np.prod(shape[1:])) * mybir.dt.size(dt)
            n = (n + 31) // 32 * 32
            t = at(name, cursor[pool], shape, dt)
            cursor[pool] += n
            return t

        ident = small("ident", [P, P])
        ones = small("ones", [P, P])
        tri = small("tri", [P, P], BF16)
        ones_b = small("ones_b", [P, P], BF16)
        vec = small("vec", [48, P])
        cols = small("cols", [P, 48])
        cc = small("cc", [P, KD, 2])
        modc = small("modc", [P, 16, 2])
        a1 = small("a1", [P, KD, 2])
        pw = small("pw", [P, 2, P])
        head_dft = small("head_dft", [P, 2 * P])
        rw = small("rw", [P, KD, NE])
        rb = small("rb", [P, NT, NE])
        eps = small("eps", [P, 1])
        stat = small("stat", [P, 6, 4])
        st2 = small("st2", [P, NT, 8])
        soft = small("soft", [P, 2, 8])
        slot_idx = small("slot_idx", [P, NT, 2], I32)
        gate = small("gate", [P, NT, 2])
        idx = small("idx", [P, NB], I32)
        idx1 = [small(f"idx1_{b}", [P, 8], I32) for b in range(2)]
        ints = small("ints", [1, 16], I32)
        assert base + cursor[1] <= nc.sbuf_usable_end

        def rt(name, shape, dt=F32):
            return small(name, shape, dt, 0)
        prob = rt("prob", [P, NT, NE])
        biased = rt("biased", [P, NT, NE])
        ra = rt("ra", [P, NT, NE])
        rbuf = rt("rbuf", [P, NT, NE])
        pairs = rt("pairs", [P, NT * GROUPS, 6])
        gs = rt("gs", [P, NT, GROUPS])
        geq = rt("geq", [P, NT, GROUPS])
        pen = rt("pen", [P, NT, GROUPS])
        r1 = rt("r1", [P, NT, 1])
        r2 = rt("r2", [P, NT, 1])
        oh = rt("oh", [P, NT, 2, NE])
        rc = rt("rc", [P, NT, 2, NE])
        sel = rt("sel", [P, NT, NE], BF16)
        rank = rt("rank", [P, NT, 2])
        over = rt("over", [P, NT, 2])
        expert = rt("expert", [P, NT, 2])
        off = rt("off", [P, NE])
        off2 = rt("off2", [P, NT, 2])
        ext = rt("ext", [P, NE])
        cs = rt("cs", [P, 2, 8 + NE])
        slot = rt("slot", [P, NT, 2])
        rmod = rt("rmod", [P, NT, 2])
        blk_no = rt("blk_no", [P, NT, 2])
        wsel = rt("wsel", [P, NT, 2])
        den = rt("den", [P, NT, 1])
        hot_blk = rt("hot_blk", [P, NT * 2, NB])

        idx_f = rt("idx_f", [P, NB])
        ov = rt("ov", [1, 8, NE])
        ovf = rt("ovf", [1, 16])
        pri4 = rt("pri4", [P, NT, GROUPS])
        pri16 = rt("pri16", [P, NT, NE])
        eno = rt("eno", [P, NE])
        iota_slot = small("iota_slot", [P, P])
        iota_blk = rt("iota_blk", [P, NB])
        iota8 = rt("iota8", [1, 8])
        tok = rt("tok", [P, 1])
        tok_chunk = rt("tok_chunk", [P, NT * 2])
        assert cursor[0] <= 200 * K1, cursor[0]

        psum = stack.enter_context(nc.psum_tensor("psum", [P, 8, 512], F32))
        bank = [psum[:, i, :] for i in range(8)]

        vec_in = sem("vec_in")
        vec2_in = sem("vec2_in")
        ctx_in = sem("ctx_in")
        x_in = [sem(f"x_in{i}") for i in range(2)]
        ada_in = [sem(f"ada_in{i}") for i in range(4)]
        win_in = [sem(f"win_in{i}") for i in range(4)]
        adab_in = sem("adab_in")
        tabpad_in = sem("tabpad_in")
        tab_out = sem("tab_out")
        raw_in = sem("raw_in")
        consts_in = sem("consts_in")
        poolw_in = sem("poolw_in")
        inv_in = sem("inv_in")
        n2g_in = sem("n2g_in")
        fing_in = sem("fing_in")
        dft_in = sem("dft_in")
        wout_in = [sem(f"wout_in{i}") for i in range(4)]
        w1_in = [sem(f"w1_in{b}") for b in range(2)]
        w3_in = [sem(f"w3_in{b}") for b in range(2)]
        w2_in = [sem(f"w2_in{b}") for b in range(2)]
        gp_step = sem("gp_step")
        ident_ok = sem("ident_ok")
        ones_ok = sem("ones_ok")
        rows_zero = sem("rows_zero")
        tab_zero = sem("tab_zero")
        pw_zero = sem("pw_zero")
        pads_ok = sem("pads_ok")
        zero_ok = sem("zero_ok")
        zero_stored = sem("zero_stored")
        bias_ok = sem("bias_ok")
        iota_ok = sem("iota_ok")
        vecT_ok = sem("vecT_ok")
        cols_ok = sem("cols_ok")
        eps_ok = sem("eps_ok")
        mrow_ok = sem("mrow_ok")
        turn_ok = sem("turn_ok")
        cc_ok = sem("cc_ok")
        ss_ok = sem("ss_ok")
        root_ok = sem("root_ok")
        xn_ok = sem("xn_ok")
        tr_ok = sem("tr_ok")
        tr_free = sem("tr_free")
        ab_ok = sem("ab_ok")
        hc_ok = sem("hc_ok")
        h_ok = sem("h_ok")
        ada_pe = sem("ada_pe")
        ada_dve = sem("ada_dve")
        rowsum_ok = sem("rowsum_ok")
        rows_act = sem("rows_act")
        kv_ok = sem("kv_ok")
        kv_free = sem("kv_free")
        pj_ok = sem("pj_ok")
        pj_act = sem("pj_act")
        pj_dve = sem("pj_dve")
        h_hi_ok = sem("h_hi_ok")
        h_lo_dve = sem("h_lo_dve")
        h_lo_gp = sem("h_lo_gp")
        w_hi_ok = sem("w_hi_ok")
        w_lo_ok = sem("w_lo_ok")
        s_ok = sem("s_ok")
        sb_ok = sem("sb_ok")
        nm_ok = sem("nm_ok")
        ex_ok = sem("ex_ok")
        pn_ok = sem("pn_ok")
        pt_ok = sem("pt_ok")
        pt_copied = sem("pt_copied")
        o_ok = sem("o_ok")
        o_copied = sem("o_copied")
        d_ok = sem("d_ok")
        pool_ps = sem("pool_ps")
        pool_ok = sem("pool_ok")
        fd_ok = sem("fd_ok")
        fd_copied = sem("fd_copied")
        fn_ok = sem("fn_ok")
        fn_copied = sem("fn_copied")
        wo_hi_ok = sem("wo_hi_ok")
        wo_lo_ok = sem("wo_lo_ok")
        y_hi_ok = sem("y_hi_ok")
        y_lo_ok = sem("y_lo_ok")
        wo_ok = sem("wo_ok")
        x1_ok = sem("x1_ok")
        ss2_ok = sem("ss2_ok")
        ms2_ok = sem("ms2_ok")
        root2_ok = sem("root2_ok")
        h2_ok = sem("h2_ok")
        h2_stored = [sem(f"h2_stored{b}") for b in range(2)]
        h2tr_ok = sem("h2tr_ok")
        h2T_ok = sem("h2T_ok")
        logit_ok = sem("logit_ok")
        prob_ok = sem("prob_ok")
        sel_ok = sem("sel_ok")
        rank_ok = sem("rank_ok")
        hot_ok = sem("hot_ok")
        idxps_ok = sem("idxps_ok")
        route_ok = sem("route_ok")
        slots_ok = sem("slots_ok")
        idx1_ok = sem("idx1_ok")
        gather_go = sem("gather_go")
        xg_in = [sem(f"xg_in{b}") for b in range(2)]
        xt_ok = sem("xt_ok")
        xt_copied = sem("xt_copied")
        h1_ok = sem("h1_ok")
        h3_ok = sem("h3_ok")
        sg_ok = sem("sg_ok")
        he_ok = sem("he_ok")
        het_ok = sem("het_ok")
        het_copied = sem("het_copied")
        y0_ok = sem("y0_ok")
        y1_ok = sem("y1_ok")
        y0_copied = sem("y0_copied")
        y1_copied = sem("y1_copied")
        ysb_free = [sem(f"ysb_free{b}") for b in range(2)]
        gat_in = [sem(f"gat_in{i}") for i in range(NT)]
        part_ok = sem("part_ok")
        x2_ok = sem("x2_ok")
        ss3_ok = sem("ss3_ok")
        root3_ok = sem("root3_ok")
        res_ok = sem("res_ok")
        out_done = sem("out_done")
        dve_step = sem("dve_step")

        block = stack.enter_context(nc.Block())

        ada_v = ada_w[0].rearrange("(k p) n -> p k n", p=P)
        win_v = w_in[0].rearrange("(k p) n -> p k n", p=P)
        wout_v = w_out[0].rearrange("(k p) n -> p k n", p=P)
        x_v = x[0].rearrange("(t p) d -> p t d", p=P)
        ctx_v = ctx[0].rearrange("(t p) d -> p t d", p=P)
        out_v = out[0].rearrange("(t p) d -> p t d", p=P)

        def row_of(ap, n, parts=P):
            return bass.AP(ap.tensor, ap.offset, [[0, parts], [1, n]])

        A_V, A_B, A_C, P_IN, Q_IN, K_IN, V_IN, F_IN = range(8)
        ORDER = [K_IN, V_IN, Q_IN, F_IN, P_IN, A_V, A_C, A_B]
        FILL = [(F_IN, 0), (F_IN, 1), (P_IN, 0), (P_IN, 1), (A_V, 0), (A_V, 1),
                (A_C, 0), (A_C, 1), (A_B, 0), (A_B, 1)]
        N_ACT_FILL = 6
        UNITS = [(2 * g + h, j) for g in range(2) for j in range(4) for h in range(2)]
        NU = len(UNITS)

        def fills(u):
            return (0, 0) if u == 0 else (1, 1 - u % 2)

        ADA_SLOT = [n % 4 for n in range(11)] + [1]
        ADA_TURN = [ADA_SLOT[:n].count(ADA_SLOT[n]) + 1 for n in range(12)]

        def by_column(t):
            return t.rearrange("p (c r) -> p r c", r=ROWS)

        def natural(t):
            return t.rearrange("p (r c) -> p r c", r=ROWS)

        @block.sync
        def _(sp):
            sp.dma_start(vec[0:8, :], c.rearrange("a (k p) -> (a k) p", p=P)).then_inc(vec_in, 16)
            sp.dma_start(vec[8:16, :], c_ctx.rearrange("(k p) -> k p", p=P)).then_inc(vec_in, 16)
            sp.dma_start(ctx_sb[:], ctx_v).then_inc(ctx_in, 16)
            for i in range(2):
                sp.dma_start(ada[i][:], ada_v[:, :, i * 512:(i + 1) * 512]).then_inc(ada_in[i], 16)
            sp.dma_start(vec[16:24, :], norm1_g.rearrange("a (k p) -> (a k) p", p=P)).then_inc(vec2_in, 16)
            sp.dma_start(vec[24:26, :], pool_scale.rearrange("a (k p) -> (a k) p", p=P)).then_inc(vec2_in, 16)
            sp.dma_start(vec[26:32, :], conv_w[0].rearrange("j (k p) -> (j k) p", p=P)).then_inc(vec2_in, 16)
            sp.dma_start(vec[32:48, :], ada_b[0, 0:2 * D].rearrange("(k p) -> k p", p=P)).then_inc(vec2_in, 16)
            for i in range(2):
                sp.dma_start(x1[:, 2 * i:2 * i + 2, :], x_v[:, 2 * i:2 * i + 2, :]).then_inc(x_in[i], 16)
                sp.dma_start(ada[2 + i][:], ada_v[:, :, (2 + i) * 512:(3 + i) * 512]).then_inc(ada_in[2 + i], 16)

            def load_win(i):
                n = ORDER[i]
                sp.dma_start(win[i % 4][:], win_v[:, :, n * GW:(n + 1) * GW]).then_inc(win_in[i % 4], 16)

            def load_ada(n):
                a = ADA_SLOT[n]
                if n < 8:
                    sp.wait_ge(ada_pe, n - 3)
                else:
                    sp.wait_ge(ada_dve, n - 7 if n < 11 else 6)
                sp.dma_start(ada[a][:], ada_v[:, :, n * 512:(n + 1) * 512]).then_inc(ada_in[a], 16)

            load_win(0)
            load_win(1)
            sp.wait_ge(rows_zero, 1)
            sp.dma_start(rows[0:1, :, :].rearrange("p a d -> p (a d)"),
                         ada_b[0:1, 2 * D:6 * D]).then_inc(adab_in, 16)
            load_ada(4)
            load_ada(5)
            sp.wait_ge(tab_out, 16)
            for h in range(HEADS):
                sp.dma_start(raw[:, h].rearrange("p a b -> p (a b)"),
                             bass.AP(tab_dram.tensor, h * TAB,
                                     [[RPB_R, 16], [1, ROWS], [1, RUN]])).then_inc(raw_in, 16)
            load_ada(6)
            sp.wait_ge(turn_ok, 4)
            load_win(2)
            load_ada(7)
            sp.wait_ge(pw_zero, 1)
            for g in range(4):
                q = HD * (g % 2)
                sp.dma_start(pw[q:q + HD, g // 2, q:q + HD], pool_w[0, g]).then_inc(poolw_in, 16)
            sp.dma_start(head_dft[:], dft_head).then_inc(consts_in, 16)
            sp.dma_start(rw[:], router_w.rearrange("(k p) e -> p k e", p=P)).then_inc(consts_in, 16)
            sp.dma_start(rb[:], bass.AP(router_b.tensor, router_b.offset,
                                        [[0, P], [0, NT], [1, NE]])).then_inc(consts_in, 16)
            load_ada(8)
            load_ada(9)
            load_ada(10)
            sp.wait_ge(tr_ok, 4)
            load_win(3)
            load_ada(11)
            for i in range(4, 8):
                sp.wait_ge(*((kv_ok, (4, 10, 12)[i - 4]) if i < 7 else (pj_ok, 2)))
                load_win(i)
            sp.wait_ge(zero_ok, 1)
            sp.dma_start(y_dram[NE * P:, :].rearrange("(p b) (q n) -> p (b q) n", p=P, n=256),
                         zero[:].unsqueeze(1).to_broadcast([P, OVER * 4, 256])).then_inc(zero_stored, 16)
            sp.wait_ge(kv_ok, 12)
            for g in range(4):
                q = HD * (g % 2)
                sp.dma_start(inv[q:q + HD, g // 2, :], row_of(pool_inv[g], N, HD)).then_inc(inv_in, 16)
            for i in range(4):
                sp.wait_ge(pj_ok, 4 + 2 * i)
                sp.dma_start(wout[:, 2 * i:2 * i + 2, :], wout_v[:, 2 * i:2 * i + 2, :]).then_inc(wout_in[i], 16)
            sp.wait_ge(pj_ok, 10)
            sp.dma_start(cos_sb[:], dft_cos.rearrange("(t p) n -> p t n", p=P)).then_inc(dft_in, 16)
            sp.dma_start(sin_sb[:], dft_sin.rearrange("(t p) n -> p t n", p=P)).then_inc(dft_in, 16)
            sp.dma_start(n2g[:], row_of(norm2_g, D)).then_inc(n2g_in, 16)
            sp.wait_ge(o_ok, NU)
            sp.dma_start(fing[:], row_of(final_g, D)).then_inc(fing_in, 16)
            sp.wait_ge(zero_stored, 16)
            def load_first(which, sb, e, sem_):
                sp.dma_start(sb[e][:], which[0, e].rearrange("(k p) f -> p k f", p=P)).then_inc(sem_[e], 16)

            sp.wait_ge(pool_ps, 2)
            sp.wait_ge(o_copied, 2)
            load_first(moe_w2, w2_sb, 1, w2_in)
            sp.wait_ge(fn_ok, 2)
            load_first(moe_w1, w1_sb, 1, w1_in)
            sp.wait_ge(wo_ok, 2 * NT)
            for b in range(2):
                sp.wait_ge(h2_stored[b], 16 * NT // 2)
            load_first(moe_w1, w1_sb, 0, w1_in)
            load_first(moe_w3, w3_sb, 0, w3_in)
            load_first(moe_w2, w2_sb, 0, w2_in)
            sp.wait_ge(xg_in[0], 16)
            load_first(moe_w3, w3_sb, 1, w3_in)

            def load_expert(b, e, s):
                sp.wait_ge(h1_ok, s - 1)
                sp.dma_start(w1_sb[b][:], moe_w1[0, bass.ds(e, 1)].rearrange("a (k p) f -> p (a k) f", p=P)
                             ).then_inc(w1_in[b], 16)
                sp.wait_ge(h3_ok, s - 1)
                sp.dma_start(w3_sb[b][:], moe_w3[0, bass.ds(e, 1)].rearrange("a (k p) f -> p (a k) f", p=P)
                             ).then_inc(w3_in[b], 16)
                sp.wait_ge(y1_ok, s - 1)
                sp.dma_start(w2_sb[b][:], moe_w2[0, bass.ds(e, 1)].rearrange("a (k p) f -> p (a k) f", p=P)
                             ).then_inc(w2_in[b], 16)

            with sp.Fori(1, NE // 2) as i:
                for b in range(2):
                    load_expert(b, i * 2 + b, i * 2 + b)
            sp.wait_ge(route_ok, 1)
            n_pairs = sp.value_load(ints[0:1, 8:9], min_val=0, max_val=OVER // 2) + NE // 2
            with sp.If(n_pairs > NE // 2):
                with sp.Fori(NE // 2, n_pairs) as i:
                    for b in range(2):
                        e = sp.value_load(ints[0:1, bass.ds(i * 2 + b - NE, 1)], min_val=0, max_val=NE - 1)
                        load_expert(b, e, i * 2 + b)

            for t in range(NT):
                sp.wait_ge(res_ok, t + 1)
                sp.dma_start(out_v[:, t, :], ygat[:, t, 1, :]).then_inc(out_done, 16)
            sp.wait_ge(out_done, 16 * NT)

        @block.gpsimd
        def _(gp):
            step = [0]

            def link(ins):
                step[0] += 1
                ins.then_inc(gp_step, 1)
                gp.wait_ge(gp_step, step[0])

            link(gp.memset(ident[:], 0.0))
            gp.affine_select(out=ident[:], in_=ident[:], compare_op=ALU.not_equal, fill=1.0, base=0,
                             pattern=[[-1, P]], channel_multiplier=1).then_inc(ident_ok, 1)
            gp.memset(eps[:], EPS).then_inc(eps_ok, 1)
            gp.memset(tabpad[:], 0.0).then_inc(tab_zero, 1)
            gp.wait_ge(tab_zero, 1)
            gp.dma_start(tabpad[:, PAD_C * RPB_R:(PAD_C + RPB_C) * RPB_R],
                         rpb_t.rearrange("h v u -> h (v u)")).then_inc(tabpad_in, 16)
            gp.memset(rows[:].rearrange("p a d -> p (a d)"), 0.0).then_inc(rows_zero, 1)
            gp.memset(pw[:].rearrange("p a d -> p (a d)"), 0.0).then_inc(pw_zero, 1)
            link(gp.memset(ones[:], 1.0))
            link(gp.memset(ones_b[:], 1.0))
            gp.affine_select(out=tri[:], in_=ones_b[:], compare_op=ALU.is_gt, fill=0.0, base=0,
                             pattern=[[1, P]], channel_multiplier=-1).then_inc(ones_ok, 1)
            gp.wait_ge(tabpad_in, 16)
            gp.dma_start(tab_dram, tabpad[:, :]).then_inc(tab_out, 16)
            gp.wait_ge(raw_in, 16 * HEADS)

            def from_left(dst, src_, j0, n):
                return gp.affine_select(out=dst, in_=src_, compare_op=ALU.is_ge, fill=-BIG, base=8 * j0 - 57,
                                        pattern=[[8, n], [0, ROWS]], channel_multiplier=-1)

            def from_right(dst, src_, j0, n):
                return gp.affine_select(out=dst, in_=src_, compare_op=ALU.is_ge, fill=-BIG, base=184 - 8 * j0,
                                        pattern=[[-8, n], [0, ROWS]], channel_multiplier=1)

            def seg(h, a, n=1):
                return bias[:, h, 16 * a:16 * (a + n), :]

            def key(h, a, n=1):
                return raw[:, h, 48 - 16 * (a + n):48 - 16 * a, 0:ROWS][:, ::-1, ::-1]

            for h in range(HEADS):
                from_left(seg(h, 0, 3), key(h, 0, 3), 0, 48)
                from_left(seg(h, 3), key(h, 1), 16, 16)
                from_right(seg(h, 4), key(h, 2), 32, 16)
                from_left(seg(h, 5), key(h, 0), 0, 16)
                link(from_right(seg(h, 6), key(h, 1), 16, 16))
                from_right(seg(h, 0, 3), seg(h, 0, 3), 0, 48).then_inc(bias_ok, 1)
            def low_w(n):
                i, cs_ = 3 + n // 2, slice((n % 2) * P, (n % 2 + 1) * P)
                gp.wait_ge(w_hi_ok, n + 1)
                gp.tensor_tensor(win_lo[i % 4][:, :, cs_], win[i % 4][:, :, cs_], win_hi[n % 2][:], ALU.subtract
                                 ).then_inc(w_lo_ok, 1)

            low_w(0)
            low_w(1)
            gp.wait_ge(kv_ok, 12)
            gp.wait_ge(h_hi_ok, 2)
            gp.tensor_tensor(hT_lo[:, 4:KD, :], hT[:, 4:KD, :], hT_hi[:, 4:KD, :], ALU.subtract).then_inc(h_lo_gp, 1)
            gp.wait_ge(ada_dve, 8)
            gp.memset(zero[:], 0.0).then_inc(zero_ok, 1)
            gp.memset(z[:, :, 0:1], 0.0)
            gp.memset(z[:, :, N + 1:N + 2], 0.0)
            gp.memset(up[:, :, 0:8], 0.0)
            gp.memset(up[:, :, N + 8:N + 16], 0.0).then_inc(pads_ok, 1)
            for n in range(2, len(FILL)):
                low_w(n)
            gp.wait_ge(o_ok, NU)
            gp.iota(pri4[:], [[0, NT], [-1, GROUPS]], base=GROUPS, channel_multiplier=0,
                    allow_small_or_imprecise_dtypes=True)
            gp.iota(pri16[:], [[0, NT], [-1, NE]], base=NE, channel_multiplier=0,
                    allow_small_or_imprecise_dtypes=True)
            gp.iota(eno[:], [[1, NE]], base=0, channel_multiplier=0, allow_small_or_imprecise_dtypes=True)
            gp.iota(iota_slot[:], [[1, P]], base=0, channel_multiplier=0, allow_small_or_imprecise_dtypes=True)
            gp.iota(iota_blk[:], [[1, NB]], base=0, channel_multiplier=0, allow_small_or_imprecise_dtypes=True)
            gp.iota(iota8[:], [[1, 8]], base=0, channel_multiplier=0, allow_small_or_imprecise_dtypes=True)
            gp.memset(cs[:, :, 0:8], 0.0)
            gp.iota(tok[:], [[0, 1]], base=0, channel_multiplier=1, allow_small_or_imprecise_dtypes=True)
            gp.iota(tok_chunk[:].rearrange("p (t k) -> p t k", k=2), [[1, NT], [0, 2]], base=-(EMPTY // P),
                    channel_multiplier=0, allow_small_or_imprecise_dtypes=True).then_inc(iota_ok, 1)
            gp.wait_ge(logit_ok, NT)
            gp.memset(xg[0][:], 0.0)
            link(gp.memset(xg[1][:], 0.0))

            gp.wait_ge(route_ok, 1)
            for b in range(2):
                gp.wait_ge(h2_stored[b], 16 * NT // 2)
            n_pairs = gp.value_load(ints[0:1, 8:9], min_val=0, max_val=OVER // 2) + NE // 2

            def gather(b, s, i):
                if i is not None:
                    gp.wait_ge(xt_ok, s - 1)
                gp.wait_ge(route_ok, 1)
                gp.tensor_copy(idx1[b][:, 0:1], idx[:, bass.ds(s, 1)]).then_inc(idx1_ok, 1)
                gp.wait_ge(idx1_ok, s + 1)
                gp.sem_inc(gather_go, 1)
                gp.indirect_dma_start(xg[b][:], None, h2_dram,
                                      bass.IndirectOffsetOnAxis(ap=idx1[b][:, 0:1], axis=0),
                                      bounds_check=N - 1, oob_is_err=False).then_inc(xg_in[b], 16)

            for b in range(2):
                gather(b, b, None)
            with gp.Fori(1, n_pairs) as i:
                for b in range(2):
                    gather(b, i * 2 + b, i)
            gp.wait_ge(slots_ok, 1)
            gp.wait_ge(ysb_free[0], n_pairs * 16 + 16)
            gp.wait_ge(ysb_free[1], n_pairs * 16 + 16)
            gp.sem_inc(gather_go, 1)
            for t in range(NT):
                for k in range(2):
                    gp.indirect_dma_start(ygat[:, t, k, :], None, y_dram,
                                          bass.IndirectOffsetOnAxis(ap=slot_idx[:, t, k:k + 1], axis=0)
                                          ).then_inc(gat_in[t], 16)

        @block.tensor
        def _(pe):
            pe.wait_ge(vec_in, 32)
            pe.wait_ge(ident_ok, 1)
            pe.transpose(bank[7][:, 0:16], vec[0:16, :], ident[0:16, 0:16]).then_inc(vecT_ok, 1)

            def turn_input(g):
                if g >= 5:
                    pe.wait_ge(tr_free, g - 4)
                for i in range(4):
                    if g < 4:
                        src = ctx_sb[:, i % 2, (2 * g + i // 2) * P:(2 * g + i // 2 + 1) * P]
                    else:
                        src = xn[:, i, (g - 4) * P:(g - 3) * P]
                    m = pe.transpose(bank[g % 5][:, i * P:(i + 1) * P], src, ident[:])
                m.then_inc(tr_ok, 1)

            def modulation(n):
                pe.wait_ge(ada_in[n], 16)
                if n >= 2:
                    pe.wait_ge(mrow_ok, n - 1)
                for k in range(KD):
                    m = pe.matmul(bank[6 + n % 2][0:2, :], cc[:, k, :], ada[n][:, k, :],
                                  start=(k == 0), stop=(k == KD - 1))
                m.then_inc(ada_pe, 1)

            def turn_mod(n):
                pe.wait_ge(mrow_ok, n + 1)
                if n == 0:
                    pe.wait_ge(cols_ok, 2)
                for i in range(4):
                    m = pe.transpose(bank[5 + n // 3][:, 8 * n + 2 * i:8 * n + 2 * i + 2], mod_rows[:, n, i * P:(i + 1) * P],
                                     ident[0:2, 0:2])
                m.then_inc(turn_ok, 1)

            pe.wait_ge(xn_ok, LT)
            for g in range(4):
                turn_input(g)
            pe.wait_ge(cc_ok, 1)
            modulation(0)
            pe.wait_ge(vec2_in, 64)
            pe.transpose(bank[5][:, 64:112], vec[:], ident[0:48, 0:48]).then_inc(vecT_ok, 1)
            modulation(1)
            turn_mod(0)
            modulation(2)
            turn_mod(1)
            pe.wait_ge(xn_ok, LT + NT)
            for g in range(4, 4 + KD):
                turn_input(g)
            turn_mod(2)
            modulation(3)
            turn_mod(3)

            def kv_tile(n, make):
                if n < 6:
                    pe.wait_ge(tr_free, 12)
                else:
                    pe.wait_ge(kv_free, n - 5)
                m = make(bank[n % 6])
                m.then_inc(kv_ok, 1)
                return m

            def channel_tile(slot_, half, src, width, ready=None):
                def make(b):
                    for k in range(KD):
                        if ready is not None:
                            pe.wait_ge(ready, k + 1)
                        m = pe.matmul(b[:, 0:width], win[slot_][:, k, half * P:(half + 1) * P],
                                      src[:, k, :], start=(k == 0), stop=(k == KD - 1))
                    return m
                return make

            def value_tile(slot_, lhs):
                def make(b):
                    for k in range(KD):
                        m = pe.matmul(b[:, 0:GW], lhs(k), win[slot_][:, k, :],
                                      start=(k == 0), stop=(k == KD - 1))
                    return m
                return make

            pe.wait_ge(win_in[0], 16)
            kv_tile(0, channel_tile(0, 0, hT, N, h_ok))
            kv_tile(1, channel_tile(0, 1, hT, N))
            pe.wait_ge(hc_ok, 1)
            kv_tile(2, channel_tile(0, 0, hcT, L))
            kv_tile(3, channel_tile(0, 1, hcT, L))
            pe.wait_ge(win_in[1], 16)
            for t in range(LT):
                kv_tile(4 + t, value_tile(1, lambda k: hcT[:, k, t * P:(t + 1) * P]))
            for m_ in range(NT):
                kv_tile(6 + m_, value_tile(1, lambda k: hT[:, k, m_ * P:(m_ + 1) * P]))
            pe.wait_ge(win_in[2], 16)
            kv_tile(10, channel_tile(2, 0, hT, N))
            kv_tile(11, channel_tile(2, 1, hT, N))

            def fill(n):
                tile, part = n // 2, n % 2
                if tile >= len(FILL):
                    return
                i, half = 3 + tile // 2, tile % 2
                if part == 0:
                    pe.wait_ge(w_lo_ok, tile + 1)
                    if 1 <= tile <= N_ACT_FILL:
                        pe.wait_ge(pj_act, tile)
                    elif tile > N_ACT_FILL:
                        pe.wait_ge(pj_dve, tile - N_ACT_FILL)
                if tile == 0:
                    pe.wait_ge((h_lo_dve, h_lo_gp)[part], 1)
                w_lo = win_lo[i % 4][:, :, half * P:(half + 1) * P]
                for k in range(4 * part, 4 * part + 4):
                    pe.matmul(bank[7][:], win_hi[half][:, k, :], hT_hi[:, k, :], start=(k == 0), stop=False)
                    pe.matmul(bank[7][:], win_hi[half][:, k, :], hT_lo[:, k, :], start=False, stop=False)
                    m = pe.matmul(bank[7][:], w_lo[:, k, :], hT_hi[:, k, :], start=False, stop=(k == KD - 1))
                if part == 1:
                    m.then_inc(pj_ok, 1)

            def scores(u):
                h, j = UNITS[u]
                m0, m1, _ = KEYS[j]
                q0 = HD * (h % 2)
                if u >= 2:
                    pe.wait_ge(ex_ok, u - 1)
                q = qT[q0:q0 + HD, h // 2, j * P:(j + 1) * P]
                pe.matmul(bank[2 * (u % 2)][:, 0:(m1 - m0) * P], q, kT[q0:q0 + HD, h // 2, m0 * P:m1 * P],
                          start=True, stop=True)
                pe.matmul(bank[2 * (u % 2) + 1][:, 0:L], q, kcT[q0:q0 + HD, h // 2, :],
                          start=True, stop=True).then_inc(s_ok, 1)

            def values(u):
                h, j = UNITS[u]
                m0, m1, _ = KEYS[j]
                nb = m1 - m0 + LT
                pe.wait_ge(pn_ok, u + 1)
                if u >= 1:
                    pe.wait_ge(pt_copied, u)
                for i in range(nb):
                    m = pe.transpose(bank[4 + i // 4][:, (i % 4) * P:(i % 4 + 1) * P],
                                     pr[:, u % 2, i * P:(i + 1) * P], ident[:])
                m.then_inc(pt_ok, 1)

            def output(u):
                h, j = UNITS[u]
                m0, m1, _ = KEYS[j]
                nb = m1 - m0 + LT
                pe.wait_ge(pt_copied, u + 1)
                if u == NU // 2:
                    pe.wait_ge(o_copied, 1)
                for i in range(nb):
                    w = m1 - m0
                    v = v_sb[:, m0 + i, h * HD:(h + 1) * HD] if i < w else vc_sb[:, i - w, h * HD:(h + 1) * HD]
                    m = pe.matmul(bank[6][HD * (h % 2):HD * (h % 2) + HD, j * P:(j + 1) * P], v,
                                  pT[:, u % 2, i * P:(i + 1) * P], start=(i == 0), stop=(i == nb - 1))
                m.then_inc(o_ok, 1)

            pe.wait_ge(kv_free, 12)
            nf = 0
            for u in range(NU + 2):
                if u < NU:
                    scores(u)
                if fills(u)[0] and nf < 20:
                    fill(nf)
                    nf += 1
                if 1 <= u <= NU:
                    values(u - 1)
                if fills(u)[1] and nf < 20:
                    fill(nf)
                    nf += 1
                if u >= 2:
                    output(u - 2)
            while nf < 20:
                fill(nf)
                nf += 1

            pe.wait_ge(poolw_in, 64)
            pe.wait_ge(d_ok, 1)
            pe.wait_ge(pj_dve, 4)
            for h in range(2):
                pe.matmul(bank[4 + h][:], pw[:, h, :], dpool[:, h, :],
                          start=True, stop=True).then_inc(pool_ps, 1)
            pe.wait_ge(consts_in, 48)
            for t in range(NT):
                for h in range(2):
                    m = pe.matmul(bank[t][:, h * GW:(h + 1) * GW], fT[:, h, t * P:(t + 1) * P], head_dft[:],
                                  start=True, stop=True)
                m.then_inc(fd_ok, 1)
            pe.wait_ge(dft_in, 32)
            pe.wait_ge(pool_ok, 2)
            for h in range(2):
                for t in range(NT):
                    if h == 0:
                        pe.wait_ge(fd_copied, t + 1)
                    pe.matmul(bank[4 + h][:], fcs[:, t, h, 0:P], cos_sb[:, t, :], start=(t == 0), stop=False)
                    m = pe.matmul(bank[4 + h][:], fcs[:, t, h, P:2 * P], sin_sb[:, t, :],
                                  start=False, stop=(t == NT - 1))
                m.then_inc(fn_ok, 1)
            pe.wait_ge(ones_ok, 1)
            pe.wait_ge(ada_dve, 8)
            for n in range(8):
                if n >= 4:
                    pe.wait_ge(rows_act, n - 3)
                pe.matmul(bank[n % 4][:], ones[:], rows[:, n // 2, (n % 2) * 512:(n % 2 + 1) * 512],
                          start=True, stop=True).then_inc(rowsum_ok, 1)
            pe.wait_ge(wo_lo_ok, 4)
            pe.wait_ge(y_lo_ok, 5)
            pe.wait_ge(rows_act, 8)

            def project(n):
                t, half = n // 2, n % 2
                if n >= 4:
                    pe.wait_ge(x1_ok, n - 3)
                for k in range(KD):
                    tc, cc_ = slice(t * P, (t + 1) * P), slice(half * 512, (half + 1) * 512)
                    pe.matmul(bank[n % 4][:], yT_hi[:, k, tc], wout_hi[:, k, cc_], start=(k == 0), stop=False)
                    pe.matmul(bank[n % 4][:], yT_hi[:, k, tc], wout_lo[:, k, cc_], start=False, stop=False)
                    m = pe.matmul(bank[n % 4][:], yT_lo[:, k, tc], wout_hi[:, k, cc_], start=False,
                                  stop=(k == KD - 1))
                m.then_inc(wo_ok, 1)

            def turn_h2(t):
                for g in range(2):
                    pe.wait_ge(h2_ok, 2 * t + g + 1)
                    if t >= 1:
                        pe.wait_ge(h2T_ok, 2 * (t - 1) + g + 1)
                    for i in range(4):
                        k = 4 * g + i
                        m = pe.transpose(bank[4 + g][:, i * P:(i + 1) * P], h2[:, t % 2, k * P:(k + 1) * P], ident[:])
                    m.then_inc(h2tr_ok, 1)

            def router(t):
                for k in range(KD):
                    if k % 4 == 0:
                        pe.wait_ge(h2T_ok, 2 * t + 1 + k // 4)
                    m = pe.matmul(bank[7][:, t * NE:(t + 1) * NE], h2T[:, k, t * P:(t + 1) * P], rw[:, k, :],
                                  start=(k == 0), stop=(k == KD - 1))
                m.then_inc(logit_ok, 1)

            for t in range(NT):
                project(2 * t)
                if t >= 1:
                    turn_h2(t - 1)
                project(2 * t + 1)
                if t >= 1:
                    router(t - 1)
            turn_h2(NT - 1)
            router(NT - 1)
            pe.wait_ge(prob_ok, 1)
            pe.wait_ge(sel_ok, 1)
            for t in range(NT):
                for i in range(t + 1):
                    pe.matmul(bank[7][:, t * NE:(t + 1) * NE], tri[:] if i == t else ones_b[:],
                              sel[:, i, :], start=(i == 0), stop=(i == t))
            for i in range(NT):
                m = pe.matmul(bank[7][:, NT * NE:(NT + 1) * NE], ones_b[:], sel[:, i, :],
                              start=(i == 0), stop=(i == NT - 1))
            m.then_inc(rank_ok, 1)
            pe.wait_ge(hot_ok, 1)
            for i in range(2 * NT):
                m = pe.matmul(bank[6][:, 0:2 * NB], hot_slot[:, i, :], hot_tok[:, i].rearrange("p a b -> p (a b)"),
                              start=(i == 0), stop=(i == 2 * NT - 1))
            m.then_inc(idxps_ok, 1)

            pe.wait_ge(route_ok, 1)
            n_pairs = pe.value_load(ints[0:1, 8:9], min_val=0, max_val=OVER // 2) + NE // 2

            def rows_in(b, s, i):
                pe.wait_ge(xg_in[b], i * 16 + 16)
                if not (isinstance(s, int) and s == 0):
                    pe.wait_ge(xt_copied, s)
                for k in range(KD):
                    m = pe.transpose(bank[k // 4][:, (k % 4) * P:(k % 4 + 1) * P], xg[b][:, k * P:(k + 1) * P], ident[:])
                m.then_inc(xt_ok, 1)

            def hidden(b, s, i, w, w_in_, ps, freed, ok):
                pe.wait_ge(w_in_[b], i * 16 + 16)
                if not (isinstance(s, int) and s == 0):
                    pe.wait_ge(freed, s)
                for k in range(KD):
                    m = pe.matmul(ps, xgT[b][:, k, :], w[b][:, k, :], start=(k == 0), stop=(k == KD - 1))
                m.then_inc(ok, 1)

            def hidden_turned(b, s):
                pe.wait_ge(he_ok, s + 1)
                if not (isinstance(s, int) and s == 0):
                    pe.wait_ge(het_copied, s)
                for k in range(KF):
                    m = pe.transpose(bank[4][:, k * P:(k + 1) * P], he[:, k * P:(k + 1) * P], ident[:])
                m.then_inc(het_ok, 1)

            def expert_out(b, s, i, half, copied, ok, first):
                if half == 0:
                    pe.wait_ge(w2_in[b], i * 16 + 16)
                    pe.wait_ge(het_copied, s + 1)
                if not first:
                    pe.wait_ge(copied, s)
                for k in range(KF):
                    m = pe.matmul(bank[5 + half][:], heT[:, k, :], w2_sb[b][:, k, half * 512:(half + 1) * 512],
                                  start=(k == 0), stop=(k == KF - 1))
                m.then_inc(ok, 1)

            def block_(b, s, i, prev, prev_i, prev_first):
                rows_in(b, s, i)
                if prev is not None:
                    expert_out(1 - b, prev, prev_i, 0, y0_copied, y0_ok, prev_first)
                pe.wait_ge(xt_copied, s + 1)
                hidden(b, s, i, w1_sb, w1_in, bank[2][:], sg_ok, h1_ok)
                hidden(b, s, i, w3_sb, w3_in, bank[3][:], he_ok, h3_ok)
                if prev is not None:
                    expert_out(1 - b, prev, prev_i, 1, y1_copied, y1_ok, prev_first)
                hidden_turned(b, s)

            block_(0, 0, 0, None, None, False)
            block_(1, 1, 0, 0, 0, True)
            with pe.Fori(1, n_pairs) as i:
                block_(0, i * 2, i, i * 2 - 1, i - 1, False)
                block_(1, i * 2 + 1, i, i * 2, i, False)
            last = n_pairs * 2 - 1
            expert_out(1, last, n_pairs - 1, 0, y0_copied, y0_ok, False)
            expert_out(1, last, n_pairs - 1, 1, y1_copied, y1_ok, False)

        @block.scalar
        def _(act):
            act.wait_ge(cols_ok, 1)
            act.activation(cc[:].rearrange("p k v -> p v k"), cols[:, 0:16].rearrange("p (v k) -> p v k", v=2),
                           ACT.Silu).then_inc(cc_ok, 1)
            act.wait_ge(eps_ok, 1)

            def squares(t):
                src = ctx_sb[:, t, :] if t < LT else x1[:, t - LT, :]
                act.activation(hT[:, 2 * t:2 * t + 2, :].rearrange("p a n -> p (a n)") if t < LT
                               else xn[:, t - LT, :], src, ACT.Square,
                               accum_out=stat[:, t, 0:1]).then_inc(ss_ok, 1)

            def root(t):
                act.wait_ge(ss_ok, t + 1)
                act.activation(stat[:, t, 2:3], stat[:, t, 0:1], ACT.Sqrt, bias=eps[:], scale=1.0 / D
                               ).then_inc(root_ok, 1)

            def input_copy(g):
                act.wait_ge(tr_ok, g + 1)
                b = bank[g % 5]
                if g < 4:
                    m = act.copy(hcT[:, 2 * g:2 * g + 2, :].rearrange("p a t -> p (a t)"), b)
                else:
                    m = act.copy(by_column(hT[:, g - 4, :]), natural(b))
                m.then_inc(tr_free, 1)

            def mod_copy(n):
                act.wait_ge(ada_pe, n + 1)
                act.copy(mod_rows[:, n, :], bank[6 + n % 2][0:2, :]).then_inc(mrow_ok, 1)

            act.wait_ge(ctx_in, 16)
            for t in range(LT):
                squares(t)
            for t in range(LT):
                root(t)
            for g in range(4):
                input_copy(g)
            mod_copy(0)
            act.wait_ge(x_in[0], 16)
            squares(2)
            squares(3)
            mod_copy(1)
            act.wait_ge(x_in[1], 16)
            squares(4)
            squares(5)
            for t in range(LT, LT + NT):
                root(t)
            mod_copy(2)
            for g in range(4, 4 + KD):
                input_copy(g)
            mod_copy(3)
            for n in range(12):
                act.wait_ge(kv_ok, n + 1)
                b = bank[n % 6]
                if n < 2:
                    m = act.copy(kT[:, n, :], b)
                elif n < 4:
                    m = act.copy(kcT[:, n - 2, :], b[:, 0:L])
                elif n < 6:
                    m = act.copy(vc_sb[:, n - 4, :], b[:, 0:GW])
                elif n < 10:
                    m = act.copy(v_sb[:, n - 6, :], b[:, 0:GW])
                else:
                    m = act.activation(qT[:, n - 10, :], b, ACT.Copy, scale=SCALE)
                m.then_inc(kv_free, 1)
                if n == 7:
                    act.wait_ge(h_ok, KD)
                    act.wait_ge(ada_dve, 4)
                    for i in range(2):
                        act.copy(hT_hi[:, 4 * i:4 * i + 4, :].rearrange("p k n -> p (k n)"),
                                 hT[:, 4 * i:4 * i + 4, :].rearrange("p k n -> p (k n)")).then_inc(h_hi_ok, 1)

            def high_w(n):
                i, cs_ = 3 + n // 2, slice((n % 2) * P, (n % 2 + 1) * P)
                act.wait_ge(win_in[i % 4], 16 * (i // 4 + 1))
                act.copy(win_hi[n % 2][:], win[i % 4][:, :, cs_]).then_inc(w_hi_ok, 1)

            act.wait_ge(ada_dve, 5)
            high_w(0)
            high_w(1)

            def tile_done(n):
                act.wait_ge(pj_ok, n + 1)
                if n < N_ACT_FILL:
                    fill_copy(n)
                if n + 2 < len(FILL):
                    high_w(n + 2)

            def fill_copy(n):
                piece, half = FILL[n]
                if n == 0:
                    act.wait_ge(ada_dve, 8)
                    act.wait_ge(pads_ok, 1)
                dst = {F_IN: fT[:, half, :], P_IN: up[:, half, 8:8 + N], A_V: av[:, half, :]}[piece]
                act.copy(natural(dst), by_column(bank[7])).then_inc(pj_act, 1)

            def expo(u):
                h, j = UNITS[u]
                w = (KEYS[j][1] - KEYS[j][0]) * P
                s = u % 2
                act.wait_ge(nm_ok, u + 1)
                if u >= 2:
                    act.wait_ge(pt_ok, u - 1)
                act.activation(pr[:, s, 0:w], sw[:, s, 0:w], ACT.Exp, bias=soft[:, s, 2:3],
                               accum_out=soft[:, s, 3:4])
                act.activation(pr[:, s, w:w + L], bank[2 * s + 1][:, 0:L], ACT.Exp, bias=soft[:, s, 2:3],
                               accum_out=soft[:, s, 4:5]).then_inc(ex_ok, 1)

            def pt_copy(u):
                h, j = UNITS[u]
                n = (KEYS[j][1] - KEYS[j][0] + LT) * P
                act.wait_ge(pt_ok, u + 1)
                if u >= 2:
                    act.wait_ge(o_ok, u - 1)
                act.copy(pT[:, u % 2, 0:n], psum[:, 4:6, :].rearrange("p a n -> p (a n)")[:, 0:n]
                         ).then_inc(pt_copied, 1)

            done = 0
            nf = 0
            for u in range(NU + 2):
                if u < NU:
                    expo(u)
                nf = min(20, nf + fills(u)[0])
                if done < len(FILL) and nf >= 2 * (done + 1):
                    tile_done(done)
                    done += 1
                if 1 <= u <= NU:
                    pt_copy(u - 1)
                nf = min(20, nf + fills(u)[1])
                if done < len(FILL) and nf >= 2 * (done + 1):
                    tile_done(done)
                    done += 1
            assert done == len(FILL)
            for h in range(2):
                act.wait_ge(pool_ps, h + 1)
                act.activation(yT[:, 2 + h, :], bank[4 + h], ACT.Copy, scale=cols[:, 24 + h:25 + h]
                               ).then_inc(pool_ok, 1)
            for t in range(NT):
                act.wait_ge(fd_ok, t + 1)
                act.copy(fcs[:, t].rearrange("p a n -> p (a n)"), bank[t]).then_inc(fd_copied, 1)
            act.wait_ge(pj_dve, 4)
            act.wait_ge(d_ok, 1)
            act.wait_ge(zero_stored, 16)
            for i in range(4):
                act.wait_ge(wout_in[i], 16)
                act.copy(wout_hi[:, 2 * i:2 * i + 2, :].rearrange("p k n -> p (k n)"),
                         wout[:, 2 * i:2 * i + 2, :].rearrange("p k n -> p (k n)")).then_inc(wo_hi_ok, 1)
            act.wait_ge(o_copied, 2)
            act.wait_ge(pool_ok, 2)
            for i in range(3):
                act.copy(yT_hi[:, 2 * i:2 * i + 2, :].rearrange("p k n -> p (k n)"),
                         yT[:, 2 * i:2 * i + 2, :].rearrange("p k n -> p (k n)")).then_inc(y_hi_ok, 1)
            for h in range(2):
                act.wait_ge(fn_ok, h + 1)
                act.copy(yT_hi[:, 6 + h, :], bank[4 + h]).then_inc(y_hi_ok, 1)
            for n in range(8):
                act.wait_ge(rowsum_ok, n + 1)
                act.copy(rows[:, n // 2, (n % 2) * 512:(n % 2 + 1) * 512], bank[n % 4]).then_inc(rows_act, 1)
            def squares2(n):
                t, half = n // 2, n % 2
                act.wait_ge(x1_ok, n + 1)
                if n >= 1:
                    act.wait_ge(ss2_ok, n)
                act.activation(bank[6], x1[:, t, half * 512:(half + 1) * 512], ACT.Square,
                               accum_out=st2[:, t, half:half + 1]).then_inc(ss2_ok, 1)

            def h2T_copy(t):
                for g in range(2):
                    act.wait_ge(h2tr_ok, 2 * t + g + 1)
                    act.copy(h2T[:, 4 * g:4 * g + 4, t * P:(t + 1) * P],
                             bank[4 + g].rearrange("p (k t) -> p k t", t=P)).then_inc(h2T_ok, 1)

            for t in range(NT):
                squares2(2 * t)
                if t >= 1:
                    h2T_copy(t - 1)
                squares2(2 * t + 1)
                act.wait_ge(ms2_ok, t + 1)
                act.activation(st2[:, t, 3:4], st2[:, t, 2:3], ACT.Sqrt).then_inc(root2_ok, 1)
                act.wait_ge(h2_ok, 2 * t + 2)
                act.dma_start(h2_dram[t * P:(t + 1) * P, :], h2[:, t % 2, :]).then_inc(h2_stored[t % 2], 16)
            h2T_copy(NT - 1)
            act.wait_ge(logit_ok, NT)
            act.activation(prob[:].rearrange("p t e -> p (t e)"), bank[7][:, 0:NT * NE], ACT.Sigmoid
                           ).then_inc(prob_ok, 1)

            act.wait_ge(route_ok, 1)
            n_pairs = act.value_load(ints[0:1, 8:9], min_val=0, max_val=OVER // 2) + NE // 2

            def block_(b, s, store):
                act.wait_ge(h1_ok, s + 1)
                if not (isinstance(s, int) and s == 0):
                    act.wait_ge(he_ok, s)
                act.activation(sg[:], bank[2], ACT.Silu).then_inc(sg_ok, 1)
                act.wait_ge(het_ok, s + 1)
                act.copy(heT[:].rearrange("p k t -> p (k t)"), bank[4]).then_inc(het_copied, 1)
                if store is not None:
                    store_rows(1 - b, store)

            def store_rows(b, s):
                act.wait_ge(y1_copied, s + 1)
                act.dma_start(y_dram[bass.ds(s * P, P), :], ysb[b][:]).then_inc(ysb_free[b], 16)

            for b in range(2):
                act.sem_inc(ysb_free[b], 16)
            block_(0, 0, None)
            block_(1, 1, 0)
            with act.Fori(1, n_pairs) as i:
                block_(0, i * 2, i * 2 - 1)
                block_(1, i * 2 + 1, i * 2)
            store_rows(1, n_pairs * 2 - 1)

            for t in range(NT):
                act.wait_ge(x2_ok, t + 1)
                act.activation(ygat[:, t, 0, :], x1[:, t, :], ACT.Square, accum_out=st2[:, t, 5:6]).then_inc(ss3_ok, 1)
                act.wait_ge(ss3_ok, t + 1)
                act.activation(st2[:, t, 6:7], st2[:, t, 5:6], ACT.Sqrt, bias=eps[:], scale=1.0 / D
                               ).then_inc(root3_ok, 1)

        @block.vector
        def _(v):
            step = [0]

            def link(ins):
                step[0] += 1
                ins.then_inc(dve_step, 1)
                v.wait_ge(dve_step, step[0])

            v.wait_ge(vecT_ok, 1)
            v.tensor_copy(cols[:, 0:16], bank[7][:, 0:16]).then_inc(cols_ok, 1)

            def normalise(t):
                v.wait_ge(root_ok, t + 1)
                link(v.reciprocal(stat[:, t, 3:4], stat[:, t, 2:3]))
                src = ctx_sb[:, t, :] if t < LT else x1[:, t - LT, :]
                dst = ctx_sb[:, t, :] if t < LT else xn[:, t - LT, :]
                v.tensor_scalar(dst, src, stat[:, t, 3:4], None, ALU.mult).then_inc(xn_ok, 1)

            for t in range(LT):
                normalise(t)
            v.wait_ge(vecT_ok, 2)
            v.tensor_copy(cols[:, 16:48], bank[5][:, 80:112]).then_inc(cols_ok, 1)
            for t in range(LT, LT + NT):
                normalise(t)

            def mod_columns(n0, n1):
                w = n1 - n0
                link(v.tensor_tensor(modc[:, n0:n1, :], bank[5 + n0 // 12][:, 2 * n0:2 * n1].rearrange("p (n v) -> p n v", v=2),
                                     cols[:, 32 + n0:32 + n1].unsqueeze(2).to_broadcast([P, w, 2]), ALU.add))
                if n0 >= 8:
                    link(v.scalar_tensor_tensor(out=a1[:, n0 - 8:n1 - 8, :], in0=modc[:, n0:n1, :], scalar=1.0,
                                                in1=cols[:, 8 + n0:8 + n1].unsqueeze(2).to_broadcast([P, w, 2]),
                                                op0=ALU.add, op1=ALU.mult))

            def modulate(t_, k, which):
                return v.tensor_scalar(t_[:, k, :], t_[:, k, :], a1[:, k, which:which + 1],
                                       modc[:, k, which:which + 1], ALU.mult, ALU.add)

            v.wait_ge(cols_ok, 2)
            v.wait_ge(turn_ok, 3)
            mod_columns(0, 8)
            mod_columns(8, 12)
            v.wait_ge(tr_free, 12)
            for k in range(4):
                modulate(hT, k, 0).then_inc(h_ok, 1)
            for k in range(4):
                modulate(hcT, k, 1)
            v.wait_ge(turn_ok, 4)
            mod_columns(12, 16)
            for k in range(4, KD):
                modulate(hT, k, 0).then_inc(h_ok, 1)
            for k in range(4, KD):
                m = modulate(hcT, k, 1)
            m.then_inc(hc_ok, 1)
            v.wait_ge(adab_in, 16)
            for n in range(4, 12):
                a = ADA_SLOT[n]
                v.wait_ge(ada_in[a], 16 * ADA_TURN[n])
                o = rows[:, (n - 4) // 2, (n % 2) * 512:(n % 2 + 1) * 512]
                for k in range(KD):
                    ins = v.scalar_tensor_tensor(out=o, in0=ada[a][:, k, :], scalar=cc[:, k, 0:1], in1=o,
                                                 op0=ALU.mult, op1=ALU.add)
                    if k < KD - 1:
                        link(ins)
                ins.then_inc(ada_dve, 1)

            def softmax_bias(u):
                h, j = UNITS[u]
                m0, m1, sg0 = KEYS[j]
                w = (m1 - m0) * P
                s = u % 2
                v.wait_ge(s_ok, u + 1)
                b = bias[:, h, sg0 * 16:(sg0 + m1 - m0) * 16, :].rearrange("p a b -> p (a b)")
                v.tensor_tensor_reduce(sw[:, s, 0:w], bank[2 * s][:, 0:w], b, 1.0, -3e38, ALU.add, ALU.max,
                                       soft[:, s, 0:1]).then_inc(sb_ok, 1)
                link(v.tensor_reduce(soft[:, s, 1:2], bank[2 * s + 1][:, 0:L], AX, ALU.max))
                v.wait_ge(sb_ok, u + 1)
                v.tensor_scalar(soft[:, s, 2:3], soft[:, s, 0:1], soft[:, s, 1:2], -1.0, ALU.max, ALU.mult
                                ).then_inc(nm_ok, 1)

            def softmax_norm(u):
                h, j = UNITS[u]
                w = (KEYS[j][1] - KEYS[j][0]) * P
                s = u % 2
                v.wait_ge(ex_ok, u + 1)
                link(v.tensor_tensor(soft[:, s, 5:6], soft[:, s, 3:4], soft[:, s, 4:5], ALU.add))
                link(v.reciprocal(soft[:, s, 6:7], soft[:, s, 5:6]))
                v.tensor_scalar(pr[:, s, 0:w + L], pr[:, s, 0:w + L], soft[:, s, 6:7], None, ALU.mult
                                ).then_inc(pn_ok, 1)

            def head_pair(g):
                v.wait_ge(o_ok, NU // 2 * (g + 1))
                v.tensor_copy(yT[:, 4 + g, :].rearrange("p (r c) -> p c r", r=ROWS),
                              bank[6].rearrange("p (c r) -> p c r", r=ROWS)).then_inc(o_copied, 1)

            def pool_diff():
                W = N + 16
                v.wait_ge(pj_act, 4)
                v.wait_ge(pads_ok, 1)
                v.wait_ge(inv_in, 64)
                link(v.tensor_tensor(s2[:, :, 1:W], up[:, :, 1:W], up[:, :, 0:W - 1], ALU.add))
                link(v.tensor_tensor(s4[:, :, 2:W - 1], s2[:, :, 1:W - 2], s2[:, :, 3:W], ALU.add))
                link(v.tensor_tensor(s8[:, 4:W - 3], s4[:, 1, 2:W - 5], s4[:, 1, 6:W - 1], ALU.add))
                link(v.tensor_tensor(dpool[HD:P, 1, :], s8[HD:P, 4:4 + N], s8[HD:P, 12:12 + N], ALU.add))
                c0 = slice(8, 8 + N)
                v.tensor_tensor(dpool[0:HD, 0, :], s2[0:HD, 0, c0], inv[0:HD, 0, :], ALU.mult)
                v.tensor_tensor(dpool[HD:P, 0, :], s4[HD:P, 0, c0], inv[HD:P, 0, :], ALU.mult)
                v.tensor_tensor(dpool[0:HD, 1, :], s8[0:HD, c0], inv[0:HD, 1, :], ALU.mult)
                link(v.tensor_tensor(dpool[HD:P, 1, :], dpool[HD:P, 1, :], inv[HD:P, 1, :], ALU.mult))
                v.tensor_tensor(dpool[:], dpool[:], up[:, :, c0], ALU.subtract).then_inc(d_ok, 1)

            def conv_in(h):
                v.wait_ge(pj_ok, 7 + h)
                if h == 0:
                    v.wait_ge(pj_act, 6)
                    v.wait_ge(pads_ok, 1)
                v.tensor_tensor(natural(z[:, h, 1:1 + N]), by_column(bank[7]), natural(av[:, h, :]), ALU.mult).then_inc(pj_dve, 1)

            def conv(h):
                v.wait_ge(pj_dve, h + 1)
                link(v.tensor_scalar(cv[:, h, :], z[:, h, 0:N], cols[:, 26 + h:27 + h], None, ALU.mult))
                link(v.scalar_tensor_tensor(out=cv[:, h, :], in0=z[:, h, 1:1 + N], scalar=cols[:, 28 + h:29 + h],
                                            in1=cv[:, h, :], op0=ALU.mult, op1=ALU.add))
                link(v.scalar_tensor_tensor(out=cv[:, h, :], in0=z[:, h, 2:2 + N], scalar=cols[:, 30 + h:31 + h],
                                            in1=cv[:, h, :], op0=ALU.mult, op1=ALU.add))

            def conv_out(h):
                v.wait_ge(pj_ok, 9 + h)
                v.tensor_tensor(natural(yT[:, h, :]), by_column(bank[7]), natural(cv[:, h, :]), ALU.mult).then_inc(pj_dve, 1)

            v.wait_ge(bias_ok, HEADS)
            late = [(8, pool_diff), (14, lambda: conv_in(0)), (16, lambda: (conv_in(1), conv(0), conv(1))),
                    (18, lambda: conv_out(0)), (20, lambda: conv_out(1))]
            nf = 0
            for u in range(NU + 2):
                while late and nf >= late[0][0]:
                    late.pop(0)[1]()
                if u == NU // 2 + 2:
                    head_pair(0)
                if u < NU:
                    softmax_bias(u)
                    softmax_norm(u)
                if u == 0:
                    v.wait_ge(kv_ok, 12)
                    v.wait_ge(h_hi_ok, 1)
                    v.tensor_tensor(hT_lo[:, 0:4, :], hT[:, 0:4, :], hT_hi[:, 0:4, :], ALU.subtract
                                    ).then_inc(h_lo_dve, 1)
                nf = min(20, nf + sum(fills(u)))
            while late:
                late.pop(0)[1]()
            head_pair(1)
            for i in range(4):
                v.wait_ge(wo_hi_ok, i + 1)
                ks = slice(2 * i, 2 * i + 2)
                v.tensor_tensor(wout_lo[:, ks, :], wout[:, ks, :], wout_hi[:, ks, :], ALU.subtract).then_inc(wo_lo_ok, 1)
            for i in range(3):
                v.wait_ge(y_hi_ok, i + 1)
                ks = slice(2 * i, 2 * i + 2)
                v.tensor_tensor(yT_lo[:, ks, :], yT[:, ks, :], yT_hi[:, ks, :], ALU.subtract).then_inc(y_lo_ok, 1)
            for h in range(2):
                v.wait_ge(y_hi_ok, 4 + h)
                v.tensor_tensor(yT_lo[:, 6 + h, :], bank[4 + h], yT_hi[:, 6 + h, :], ALU.subtract).then_inc(y_lo_ok, 1)
            v.wait_ge(n2g_in, 16)
            v.wait_ge(rows_act, 8)
            link(v.scalar_tensor_tensor(out=rows[:, SC2, :], in0=rows[:, SC2, :], scalar=1.0, in1=n2g[:],
                                        op0=ALU.add, op1=ALU.mult))
            def residual(n):
                t, half = n // 2, n % 2
                cs_ = slice(half * 512, (half + 1) * 512)
                v.wait_ge(wo_ok, n + 1)
                tmpv = rtmp[:, half, :]
                link(v.tensor_tensor(tmpv, bank[n % 4], rows[:, G1, cs_], ALU.mult))
                v.tensor_tensor(x1[:, t, cs_], x1[:, t, cs_], tmpv, ALU.add).then_inc(x1_ok, 1)

            def norm2(t):
                v.wait_ge(ss2_ok, 2 * t + 2)
                link(v.tensor_scalar(st2[:, t, 2:3], st2[:, t, 0:1], st2[:, t, 1:2], 1.0 / D, ALU.add, ALU.mult))
                v.tensor_scalar(st2[:, t, 2:3], st2[:, t, 2:3], EPS, None, ALU.add).then_inc(ms2_ok, 1)
                v.wait_ge(root2_ok, t + 1)
                link(v.reciprocal(st2[:, t, 4:5], st2[:, t, 3:4]))
                if t >= 2:
                    v.wait_ge(h2tr_ok, 2 * t - 2)
                    v.wait_ge(h2_stored[t % 2], 16)
                for half in range(2):
                    cs_ = slice(half * 512, (half + 1) * 512)
                    link(v.scalar_tensor_tensor(out=h2[:, t % 2, cs_], in0=x1[:, t, cs_], scalar=st2[:, t, 4:5],
                                                in1=rows[:, SC2, cs_], op0=ALU.mult, op1=ALU.mult))
                    v.tensor_tensor(h2[:, t % 2, cs_], h2[:, t % 2, cs_], rows[:, SH2, cs_], ALU.add
                                    ).then_inc(h2_ok, 1)

            for t in range(NT):
                residual(2 * t)
                residual(2 * t + 1)
                norm2(t)

            E4 = [P, NT, GROUPS]

            def wide(ap, shape):
                return ap.to_broadcast(shape)

            v.wait_ge(prob_ok, 1)
            v.wait_ge(consts_in, 48)
            v.wait_ge(iota_ok, 1)
            link(v.tensor_tensor(biased[:], prob[:], rb[:], ALU.add))
            b4 = biased[:].rearrange("p t (g e) -> p (t g) e", g=GROUPS)
            v.tensor_tensor(pairs[:, :, 0:3], b4[:, :, 0:3], b4[:, :, 1:4], ALU.add)
            v.tensor_tensor(pairs[:, :, 3:5], b4[:, :, 0:2], b4[:, :, 2:4], ALU.add)
            link(v.tensor_tensor(pairs[:, :, 5:6], b4[:, :, 0:1], b4[:, :, 3:4], ALU.add))
            link(v.tensor_reduce(gs[:].rearrange("p t g -> p (t g)").unsqueeze(2), pairs[:], AX, ALU.max))

            def first_max(src, pri, shape, dst, tmp):
                link(v.tensor_reduce(r1[:], src, AX, ALU.max))
                link(v.tensor_tensor(tmp, src, wide(r1[:], shape), ALU.is_equal))
                link(v.tensor_tensor(tmp, tmp, pri, ALU.mult))
                link(v.tensor_reduce(r2[:], tmp, AX, ALU.max))
                link(v.tensor_tensor(dst, tmp, wide(r2[:], shape), ALU.is_equal))

            first_max(gs[:], pri4[:], E4, geq[:], pen[:])
            link(v.tensor_scalar(pen[:], geq[:], -1.0, BIG, ALU.add, ALU.mult))
            g16 = [P, NT * GROUPS, 4]
            ra4 = ra[:].rearrange("p t (g e) -> p (t g) e", g=GROUPS)
            link(v.tensor_tensor(ra4, b4, wide(geq[:].rearrange("p t g -> p (t g)").unsqueeze(2), g16), ALU.mult))
            link(v.tensor_tensor(ra4, ra4, wide(pen[:].rearrange("p t g -> p (t g)").unsqueeze(2), g16), ALU.add))
            E16 = [P, NT, NE]
            first_max(ra[:], pri16[:], E16, oh[:, :, 0, :], rbuf[:])
            link(v.scalar_tensor_tensor(out=ra[:], in0=oh[:, :, 0, :], scalar=-3 * BIG, in1=ra[:],
                                        op0=ALU.mult, op1=ALU.add))
            first_max(ra[:], pri16[:], E16, oh[:, :, 1, :], rbuf[:])
            v.tensor_tensor(sel[:], oh[:, :, 0, :], oh[:, :, 1, :], ALU.add).then_inc(sel_ok, 1)

            E2 = [P, NT, 2, NE]

            def pick(dst, src):
                link(v.tensor_tensor(rc[:], oh[:], src, ALU.mult))
                link(v.tensor_reduce(dst.rearrange("p t k -> p (t k)").unsqueeze(2),
                                     rc[:].rearrange("p t k e -> p (t k) e"), AX, ALU.add))

            pick(expert[:], eno[:].unsqueeze(1).unsqueeze(1).to_broadcast(E2))
            v.wait_ge(rank_ok, 1)

            def above(dst, src, limits):
                link(v.tensor_scalar(dst, src, float(limits[0]), None, ALU.is_ge))
                for x_ in limits[1:]:
                    link(v.scalar_tensor_tensor(out=dst, in0=src, scalar=float(x_), in1=dst,
                                                op0=ALU.is_ge, op1=ALU.add))

            pick(rank[:], bank[7][:, 0:NT * NE].rearrange("p (t e) -> p t e", e=NE).unsqueeze(2).to_broadcast(E2))
            above(over[:], rank[:], [P, 2 * P, 3 * P])
            link(v.scalar_tensor_tensor(out=rmod[:], in0=over[:], scalar=-float(P), in1=rank[:],
                                        op0=ALU.mult, op1=ALU.add))
            flat = [P, NT * 2, P]
            v.tensor_tensor(hot_slot[:], iota_slot[:].unsqueeze(1).to_broadcast(flat),
                            rmod[:].rearrange("p t k -> p (t k)").unsqueeze(2).to_broadcast(flat), ALU.is_equal)
            above(cs[:, 0, 8:], bank[7][:, NT * NE:(NT + 1) * NE], [P + 1, 2 * P + 1, 3 * P + 1])
            v.tensor_copy(ext[:], cs[:, 0, 8:])
            for i, sh in enumerate((1, 2, 4, 8)):
                a, b = cs[:, i % 2, :], cs[:, 1 - i % 2, :]
                link(v.tensor_tensor(b[:, 8:], a[:, 8:], a[:, 8 - sh:8 - sh + NE], ALU.add))
            run = cs[:, 0, 8:]
            link(v.tensor_tensor(off[:], run, ext[:], ALU.subtract))
            link(v.scalar_tensor_tensor(out=off[:], in0=off[:], scalar=float(NE - 1), in1=eno[:],
                                        op0=ALU.add, op1=ALU.subtract))
            pick(off2[:], off[:].unsqueeze(1).unsqueeze(1).to_broadcast(E2))
            link(v.scalar_tensor_tensor(out=off2[:], in0=over[:], scalar=0.0, in1=off2[:],
                                        op0=ALU.is_gt, op1=ALU.mult))
            link(v.tensor_tensor(blk_no[:], over[:], expert[:], ALU.add))
            link(v.tensor_tensor(blk_no[:], blk_no[:], off2[:], ALU.add))
            fb = [P, NT * 2, NB]
            link(v.tensor_tensor(hot_blk[:], iota_blk[:].unsqueeze(1).to_broadcast(fb),
                                 blk_no[:].rearrange("p t k -> p (t k)").unsqueeze(2).to_broadcast(fb), ALU.is_equal))
            v.tensor_scalar(hot_tok[:, :, 0, :], hot_blk[:], tok[:, 0:1], None, ALU.mult)
            v.tensor_tensor(hot_tok[:, :, 1, :], hot_blk[:], tok_chunk[:].unsqueeze(2).to_broadcast(fb), ALU.mult
                            ).then_inc(hot_ok, 1)
            run0 = cs[0:1, 0, 8:]
            link(v.tensor_tensor(ov[:], run0.unsqueeze(1).to_broadcast([1, 8, NE]),
                                 iota8[:].unsqueeze(2).to_broadcast([1, 8, NE]), ALU.is_le))
            link(v.tensor_reduce(ovf[:, 0:8].unsqueeze(2), ov[:], AX, ALU.add))
            link(v.tensor_scalar(ovf[:, 0:8], ovf[:, 0:8], float(NE - 1), None, ALU.min))
            above(ovf[:, 8:9], cs[0:1, 0, 8 + NE - 1:8 + NE], [1, 3, 5, 7])
            v.tensor_copy(ints[:, 0:9], ovf[:, 0:9])
            v.wait_ge(idxps_ok, 1)
            link(v.tensor_scalar(idx_f[:], bank[6][:, NB:2 * NB], float(P), float(EMPTY), ALU.mult, ALU.add))
            link(v.tensor_tensor(idx_f[:], idx_f[:], bank[6][:, 0:NB], ALU.add))
            v.tensor_copy(idx[:], idx_f[:]).then_inc(route_ok, 1)
            link(v.scalar_tensor_tensor(out=slot[:], in0=blk_no[:], scalar=float(P), in1=rmod[:],
                                        op0=ALU.mult, op1=ALU.add))
            v.tensor_copy(slot_idx[:], slot[:]).then_inc(slots_ok, 1)
            pick(wsel[:], prob[:].unsqueeze(2).to_broadcast(E2))
            link(v.tensor_tensor(den[:], wsel[:, :, 0:1], wsel[:, :, 1:2], ALU.add))
            link(v.reciprocal(den[:], den[:]))
            link(v.tensor_tensor(gate[:], wsel[:], wide(den[:], [P, NT, 2]), ALU.mult))

            v.wait_ge(route_ok, 1)
            n_pairs = v.value_load(ints[0:1, 8:9], min_val=0, max_val=OVER // 2) + NE // 2

            def turned_rows(b, s):
                v.wait_ge(xt_ok, s + 1)
                if not (isinstance(s, int) and s < 2):
                    v.wait_ge(h3_ok, s - 1)
                v.tensor_copy(xgT[b][:].rearrange("p k t -> p (k t)"),
                              psum[:, 0:2, :].rearrange("p a n -> p (a n)")).then_inc(xt_copied, 1)

            def gated(b, s):
                v.wait_ge(h3_ok, s + 1)
                v.wait_ge(sg_ok, s + 1)
                if not (isinstance(s, int) and s == 0):
                    v.wait_ge(het_ok, s)
                v.tensor_tensor(he[:], bank[3], sg[:], ALU.mult).then_inc(he_ok, 1)

            def expert_rows(b, s, i, half, ok, copied):
                v.wait_ge(ok, s + 1)
                if half == 0 and i is not None:
                    v.wait_ge(ysb_free[b], i * 16 + 16)
                cs_ = slice(half * 512, (half + 1) * 512)
                v.tensor_tensor(ysb[b][:, cs_], bank[5 + half], rows[:, G2, cs_], ALU.mult).then_inc(copied, 1)

            def block_(b, s, prev, prev_i):
                turned_rows(b, s)
                if prev is not None:
                    expert_rows(1 - b, prev, prev_i, 0, y0_ok, y0_copied)
                gated(b, s)
                if prev is not None:
                    expert_rows(1 - b, prev, prev_i, 1, y1_ok, y1_copied)

            block_(0, 0, None, None)
            block_(1, 1, 0, None)
            with v.Fori(1, n_pairs) as i:
                block_(0, i * 2, i * 2 - 1, i - 1)
                block_(1, i * 2 + 1, i * 2, i)
            expert_rows(1, n_pairs * 2 - 1, n_pairs - 1, 0, y0_ok, y0_copied)
            expert_rows(1, n_pairs * 2 - 1, n_pairs - 1, 1, y1_ok, y1_copied)

            def add_rows(t):
                v.wait_ge(gat_in[t], 32)
                link(v.scalar_tensor_tensor(out=x1[:, t, :], in0=ygat[:, t, 0, :], scalar=gate[:, t, 0:1],
                                            in1=x1[:, t, :], op0=ALU.mult, op1=ALU.add))
                v.scalar_tensor_tensor(out=x1[:, t, :], in0=ygat[:, t, 1, :], scalar=gate[:, t, 1:2],
                                       in1=x1[:, t, :], op0=ALU.mult, op1=ALU.add).then_inc(x2_ok, 1)

            def result(t):
                v.wait_ge(root3_ok, t + 1)
                link(v.reciprocal(st2[:, t, 7:8], st2[:, t, 6:7]))
                v.scalar_tensor_tensor(out=ygat[:, t, 1, :], in0=x1[:, t, :], scalar=st2[:, t, 7:8], in1=fing[:],
                                       op0=ALU.mult, op1=ALU.mult).then_inc(res_ok, 1)

            v.wait_ge(fing_in, 16)
            for t in range(NT):
                add_rows(t)
                if t >= 1:
                    result(t - 1)
            result(NT - 1)


def constants():
    n = np.arange(N)
    turn = 2 * np.pi * (np.outer(n, n) % N) / N
    m = np.arange(HD)
    head = 2 * np.pi * (np.outer(m, m) % HD) / HD
    scale = 1 / np.sqrt(N * HD)
    dft_head = np.zeros((P, 2 * P))
    for h in range(2):
        dft_head[h * HD:(h + 1) * HD, h * HD:(h + 1) * HD] = np.cos(head) * scale
        dft_head[h * HD:(h + 1) * HD, P + h * HD:P + (h + 1) * HD] = -np.sin(head) * scale
    sizes = [np.minimum(n + w // 2, N) - np.maximum(n - w // 2, 0) for w in (2, 4, 8, 16)]
    return {
        "dft_cos": np.cos(turn).astype(np.float32),
        "dft_sin": np.sin(turn).astype(np.float32),
        "dft_head": dft_head.astype(np.float32),
        "pool_inv": (1 / np.stack(sizes)).astype(np.float32),
    }


_INS = ["x", "c", "ctx", "c_ctx", "ada_w", "ada_b", "norm1_g", "norm2_g", "w_in", "conv_w", "pool_w",
        "pool_scale", "rpb_t", "w_out", "router_w", "router_b", "moe_w1", "moe_w3", "moe_w2", "final_g",
        "dft_cos", "dft_sin", "dft_head", "pool_inv"]


def kernel(**inputs):
    import concourse.bacc as bacc
    from concourse.bass_utils import run_bass_kernel_spmd

    nc = bacc.Bacc("TRN2", target_bir_lowering=False, num_devices=1)
    given = {k: np.ascontiguousarray(v) for k, v in inputs.items()}
    given["rpb_t"] = np.ascontiguousarray(given.pop("na_rpb")[0].transpose(0, 2, 1)[:, ::-1, ::-1])
    given.update(constants())
    arrays, args = {}, []
    for name in _INS:
        a = given[name]
        arrays[f"in_{name}"] = a
        args.append(nc.dram_tensor(f"in_{name}", a.shape, mybir.dt.from_np(a.dtype), kind="ExternalInput").ap())
    args.append(nc.dram_tensor("out_0", (1, N, D), F32, kind="ExternalOutput").ap())
    build(nc, *args)
    r = run_bass_kernel_spmd(nc, [arrays], core_ids=[0])
    return r.results[0]["out_0"]
```

```python
from contextlib import ExitStack

import numpy as np

import concourse.bass as bass
from concourse import mybir

F32 = mybir.dt.float32
I32 = mybir.dt.int32
F32R = mybir.dt.float32r
BF16 = mybir.dt.bfloat16
ALU = mybir.AluOpType
ACT = mybir.ActivationFunctionType
AX = mybir.AxisListType.X

P = 128
D = 1024
N = 512
L = 256
KD = D // P
NT = N // P
LT = L // P
GW = 256
HD = 64
HEADS = GW // HD
ROWS, COLS = 8, 64
WIN_COLS = 16
RPB_R, RPB_C = 15, 31
NE = 16
GROUPS = 4
FF = 512
KF = FF // P
EPS = 1e-6
SCALE = HD ** -0.5
BIG = 1e30
OVER = 8
NB = NE + OVER
EMPTY = 4096
PAD_C = 16
TAB = 960
RUN = 48 * RPB_R
NSEG = 7
KEYS = [(0, 2, 3), (0, 3, 0), (1, 4, 0), (2, 4, 5)]
K1 = 1024
WARM = 3
NC = N // 2 + 1


def build(nc, x, c, ctx, c_ctx, ada_w, ada_b, norm1_g, norm2_g, w_in, conv_w, pool_w, pool_scale,
          rpb_t, w_out, router_w, router_b, moe_w1, moe_w3, moe_w2, final_g,
          dft_seq, dft_head, pool_inv, out):
    h2_dram = nc.dram_tensor("h2_rows", (N, D), F32, kind="Internal").ap()
    y_dram = nc.dram_tensor("expert_rows", (NB * P, D), F32, kind="Internal").ap()
    tab_dram = nc.dram_tensor("bias_table", (HEADS, TAB), F32, kind="Internal").ap()

    base = (nc.sbuf_base + 31) // 32 * 32
    stack = ExitStack()
    with stack:
        def at(name, offset, shape, dt=F32):
            return nc.alloc_sbuf_tensor_at(name, shape, dt, offset=base + int(offset))

        def sem(name):
            return stack.enter_context(nc.semaphore(name))

        w1_sb = [at(f"w1_{b}", 48 * K1 * b, [P, KD, FF]) for b in range(2)]
        w3_sb = [at(f"w3_{b}", 48 * K1 * b + 16 * K1, [P, KD, FF]) for b in range(2)]
        w2_sb = [at(f"w2_{b}", 48 * K1 * b + 32 * K1, [P, KF, D]) for b in range(2)]
        ada = [at(f"ada_{i}", 16 * K1 * i, [P, KD, 512]) for i in range(4)]
        yT = at("yT", 0, [P, 8, N])
        av = at("av", 16 * K1, [P, 2, N])
        z = at("z", 20 * K1, [P, 2, N + 2])
        cv = at("cv", 25 * K1, [P, 2, N])
        s8 = at("s8", 29 * K1, [P, N + 16])
        up = at("up", 32 * K1, [P, 2, N + 16])
        s2 = at("s2", 36.5 * K1, [P, 2, N + 16])
        s4 = at("s4", 41 * K1, [P, 2, N + 16])
        zero = at("zero", 46 * K1, [P, 256])
        dft_sb = at("dft_sb", 48 * K1, [P, NT, N])
        bias = at("bias", 64 * K1, [P, HEADS, NSEG * 16, ROWS])
        raw = at("raw", 78 * K1, [P, HEADS, 48, RPB_R])
        sw = at("sw", 78 * K1, [P, 2, 384])
        pr = at("pr", 81 * K1, [P, 2, 640])
        pT = at("pT", 86 * K1, [P, 2, 640])
        tabpad = at("tabpad", 91 * K1, [HEADS, TAB])
        dpool = at("dpool", 91 * K1, [P, 2, N])
        win = [at(f"win_{i}", (96 + 8 * i) * K1, [P, KD, GW]) for i in range(4)]
        ctx_sb = at("ctx_sb", 120 * K1, [P, LT, D])
        mod_rows = at("mod_rows", 112 * K1, [2, 4, 512])
        wout = at("wout", 96 * K1, [P, KD, D])
        hT_hi = at("hT_hi", 48 * K1, [P, KD, N], F32R)
        hT_lo = at("hT_lo", 160 * K1, [P, KD, N], F32R)
        win_hi = [at(f"win_hi_{i}", 12 * K1 * i, [P, KD, P], F32R) for i in range(2)]
        win_lo = [at(f"win_lo_{i}", (96 + 8 * i) * K1, [P, KD, GW], F32R) for i in range(4)]
        wout_hi = at("wout_hi", 16 * K1, [P, KD, D], F32R)
        wout_lo = at("wout_lo", 96 * K1, [P, KD, D], F32R)
        yT_hi = at("yT_hi", 64 * K1, [P, 8, N], F32R)
        yT_lo = at("yT_lo", 0, [P, 8, N], F32R)
        w3_hi = at("w3_hi", 96 * K1, [P, KD, FF], F32R)
        w3_lo = [at(f"w3_lo_{b}", 48 * K1 * b + 16 * K1, [P, KD, FF], F32R) for b in range(2)]
        w2_hi = at("w2_hi", 112 * K1, [P, KF, D], F32R)
        w2_lo = [at(f"w2_lo_{b}", 48 * K1 * b + 32 * K1, [P, KF, D], F32R) for b in range(2)]
        ygat = at("ygat", 96 * K1, [P, NT, 2, D])
        x1 = at("x1", 128 * K1, [P, NT, D])
        rows = at("rows", 144 * K1, [P, 4, D])
        G1, SH2, SC2, G2 = range(4)
        hT = at("hT", 160 * K1, [P, KD, N])
        hcT = at("hcT", 176 * K1, [P, KD, L])
        fcs = at("fcs", 160 * K1, [P, NT, 2, 2 * P])
        n2g = at("n2g", 168 * K1, [P, D])
        h2T = at("h2T", 160 * K1, [P, KD, N])
        h2 = at("h2", 176 * K1, [P, 2, D])
        fT = at("fT", 176 * K1, [P, 2, N])
        inv = at("inv", 180 * K1, [P, 2, N])
        hot_slot = at("hot_slot", 172 * K1, [P, NT * 2, P], BF16)
        hot_tok = at("hot_tok", 174 * K1, [P, NT * 2, 2, NB], BF16)
        xg = [at(f"xg_{b}", (160 + 4 * b) * K1, [P, D]) for b in range(2)]
        xgT = at("xgT", 168 * K1, [P, KD, P])
        xgT_hi = at("xgT_hi", 172 * K1, [P, KD, P], F32R)
        xgT_lo = at("xgT_lo", 194 * K1, [P, KD, P], F32R)
        ysb = [at(f"ysb_{b}", (176 + 4 * b) * K1, [P, D]) for b in range(2)]
        xn = at("xn", 184 * K1, [P, NT, D])
        qT = at("qT", 184 * K1, [P, 2, N])
        kT = at("kT", 188 * K1, [P, 2, N])
        kcT = at("kcT", 192 * K1, [P, 2, L])
        v_sb = at("v_sb", 194 * K1, [P, NT, GW])
        vc_sb = at("vc_sb", 198 * K1, [P, LT, GW])
        rtmp = at("rtmp", 184 * K1, [P, 2, 512])
        sg = at("sg", 184 * K1, [P, FF])
        he = at("he", 186 * K1, [P, FF])
        heT_hi = at("heT_hi", 188 * K1, [P, KF, P], F32R)
        heT_lo = at("heT_lo", 198 * K1, [P, KF, P], F32R)
        fing = at("fing", 190 * K1, [P, D])
        cursor = [194 * K1, 200 * K1]

        def small(name, shape, dt=F32, pool=1):
            n = int(np.prod(shape[1:])) * mybir.dt.size(dt)
            n = (n + 31) // 32 * 32
            t = at(name, cursor[pool], shape, dt)
            cursor[pool] += n
            return t

        ident = small("ident", [P, P])
        ones = small("ones", [P, P])
        tri = small("tri", [P, P], BF16)
        ones_b = small("ones_b", [P, P], BF16)
        vec = small("vec", [48, P])
        cols = small("cols", [P, 48])
        cc = small("cc", [P, KD, 2])
        modc = small("modc", [P, 16, 2])
        a1 = small("a1", [P, KD, 2])
        pw = small("pw", [P, 2, P])
        head_dft = small("head_dft", [P, 2 * P])
        rw = small("rw", [P, KD, NE])
        rb = small("rb", [P, NT, NE])
        eps = small("eps", [P, 1])
        stat = small("stat", [P, 6, 4])
        st2 = small("st2", [P, NT, 8])
        soft = small("soft", [P, 2, 8])
        slot_idx = small("slot_idx", [P, NT, 2], I32)
        gate = small("gate", [P, NT, 2])
        idx = small("idx", [P, NB], I32)
        idx1 = [small(f"idx1_{b}", [P, 8], I32) for b in range(2)]
        ints = small("ints", [1, 16], I32)
        assert base + cursor[1] <= nc.sbuf_usable_end

        def rt(name, shape, dt=F32):
            return small(name, shape, dt, 0)
        prob = rt("prob", [P, NT, NE])
        biased = rt("biased", [P, NT, NE])
        ra = rt("ra", [P, NT, NE])
        rbuf = rt("rbuf", [P, NT, NE])
        pairs = rt("pairs", [P, NT * GROUPS, 6])
        gs = rt("gs", [P, NT, GROUPS])
        geq = rt("geq", [P, NT, GROUPS])
        pen = rt("pen", [P, NT, GROUPS])
        r1 = rt("r1", [P, NT, 1])
        r2 = rt("r2", [P, NT, 1])
        oh = rt("oh", [P, NT, 2, NE])
        rc = rt("rc", [P, NT, 2, NE])
        sel = rt("sel", [P, NT, NE], BF16)
        rank = rt("rank", [P, NT, 2])
        over = rt("over", [P, NT, 2])
        expert = rt("expert", [P, NT, 2])
        off = rt("off", [P, NE])
        off2 = rt("off2", [P, NT, 2])
        ext = rt("ext", [P, NE])
        cs = rt("cs", [P, 2, 8 + NE])
        slot = rt("slot", [P, NT, 2])
        rmod = rt("rmod", [P, NT, 2])
        blk_no = rt("blk_no", [P, NT, 2])
        wsel = rt("wsel", [P, NT, 2])
        den = rt("den", [P, NT, 1])
        hot_blk = rt("hot_blk", [P, NT * 2, NB])

        idx_f = rt("idx_f", [P, NB])
        ov = rt("ov", [1, 8, NE])
        ovf = rt("ovf", [1, 16])
        pri4 = rt("pri4", [P, NT, GROUPS])
        pri16 = rt("pri16", [P, NT, NE])
        eno = rt("eno", [P, NE])
        iota_slot = small("iota_slot", [P, P], BF16)
        iota_blk = rt("iota_blk", [P, NB])
        iota8 = rt("iota8", [1, 8])
        tok = rt("tok", [P, 1])
        tok_chunk = rt("tok_chunk", [P, NT * 2])
        assert cursor[0] <= 200 * K1, cursor[0]

        psum = stack.enter_context(nc.psum_tensor("psum", [P, 8, 512], F32))
        bank = [psum[:, i, :] for i in range(8)]

        vec_in = sem("vec_in")
        vec2_in = sem("vec2_in")
        ctx_in = sem("ctx_in")
        x_in = [sem(f"x_in{i}") for i in range(2)]
        ada_in = [sem(f"ada_in{i}") for i in range(4)]
        win_in = [sem(f"win_in{i}") for i in range(4)]
        adab_in = sem("adab_in")
        tabpad_in = sem("tabpad_in")
        tab_out = sem("tab_out")
        raw_in = sem("raw_in")
        consts_in = sem("consts_in")
        poolw_in = sem("poolw_in")
        inv_in = sem("inv_in")
        n2g_in = sem("n2g_in")
        fing_in = sem("fing_in")
        dft_in = sem("dft_in")
        wout_in = [sem(f"wout_in{i}") for i in range(4)]
        w1_in = [sem(f"w1_in{b}") for b in range(2)]
        w3_in = [sem(f"w3_in{b}") for b in range(2)]
        w2_in = [sem(f"w2_in{b}") for b in range(2)]
        gp_step = sem("gp_step")
        ident_ok = sem("ident_ok")
        ones_ok = sem("ones_ok")
        rows_zero = sem("rows_zero")
        tab_zero = sem("tab_zero")
        pw_zero = sem("pw_zero")
        pads_ok = sem("pads_ok")
        zero_ok = sem("zero_ok")
        zero_stored = sem("zero_stored")
        bias_ok = sem("bias_ok")
        iota_ok = sem("iota_ok")
        vecT_ok = sem("vecT_ok")
        cols_ok = sem("cols_ok")
        eps_ok = sem("eps_ok")
        mrow_ok = sem("mrow_ok")
        turn_ok = sem("turn_ok")
        cc_ok = sem("cc_ok")
        ss_ok = sem("ss_ok")
        root_ok = sem("root_ok")
        xn_ok = sem("xn_ok")
        tr_ok = sem("tr_ok")
        tr_free = sem("tr_free")
        hc_ok = sem("hc_ok")
        h_ok = sem("h_ok")
        ada_pe = sem("ada_pe")
        ada_dve = sem("ada_dve")
        rowsum_ok = sem("rowsum_ok")
        rows_act = sem("rows_act")
        kv_ok = sem("kv_ok")
        kv_free = sem("kv_free")
        pj_ok = sem("pj_ok")
        pj_act = sem("pj_act")
        pj_dve = sem("pj_dve")
        h_hi_ok = sem("h_hi_ok")
        h_lo_dve = sem("h_lo_dve")
        h_lo_gp = sem("h_lo_gp")
        w_hi_ok = sem("w_hi_ok")
        w_lo_ok = sem("w_lo_ok")
        s_ok = sem("s_ok")
        sb_ok = sem("sb_ok")
        nm_ok = sem("nm_ok")
        ex_ok = sem("ex_ok")
        pn_ok = sem("pn_ok")
        pt_ok = sem("pt_ok")
        pt_copied = sem("pt_copied")
        o_ok = sem("o_ok")
        o_copied = sem("o_copied")
        d_ok = sem("d_ok")
        pool_ps = sem("pool_ps")
        pool_ok = sem("pool_ok")
        fd_ok = sem("fd_ok")
        fd_copied = sem("fd_copied")
        fn_ok = sem("fn_ok")
        fn_copied = sem("fn_copied")
        wo_hi_ok = sem("wo_hi_ok")
        wo_lo_ok = sem("wo_lo_ok")
        wo_lo_gp = sem("wo_lo_gp")
        fn_even = sem("fn_even")
        y_hi_ok = sem("y_hi_ok")
        y_lo_ok = sem("y_lo_ok")
        wo_ok = sem("wo_ok")
        x1_ok = sem("x1_ok")
        ss2_ok = sem("ss2_ok")
        ms2_ok = sem("ms2_ok")
        root2_ok = sem("root2_ok")
        h2_ok = sem("h2_ok")
        h2_stored = [sem(f"h2_stored{b}") for b in range(2)]
        h2tr_ok = sem("h2tr_ok")
        h2T_ok = sem("h2T_ok")
        logit_ok = sem("logit_ok")
        prob_ok = sem("prob_ok")
        sel_ok = sem("sel_ok")
        rank_ok = sem("rank_ok")
        hot_ok = sem("hot_ok")
        idxps_ok = sem("idxps_ok")
        idx_ok = sem("idx_ok")
        route_ok = sem("route_ok")
        slots_ok = sem("slots_ok")
        idx1_ok = sem("idx1_ok")
        gather_go = sem("gather_go")
        xg_in = [sem(f"xg_in{b}") for b in range(2)]
        xt_ok = sem("xt_ok")
        xt_copied = sem("xt_copied")
        h1_ok = sem("h1_ok")
        h3_ok = sem("h3_ok")
        sg_ok = sem("sg_ok")
        he_ok = sem("he_ok")
        het_ok = sem("het_ok")
        het_hi_ok = sem("het_hi_ok")
        het_lo_ok = sem("het_lo_ok")
        x_hi_ok = sem("x_hi_ok")
        x_lo_ok = sem("x_lo_ok")
        w3_hi_ok = sem("w3_hi_ok")
        w3_lo_ok = sem("w3_lo_ok")
        w2_hi_ok = [sem(f"w2_hi_ok{half}") for half in range(2)]
        w2_lo_ok = [sem(f"w2_lo_ok{half}") for half in range(2)]
        y0_ok = sem("y0_ok")
        y1_ok = sem("y1_ok")
        y0_copied = sem("y0_copied")
        y1_copied = sem("y1_copied")
        ysb_free = [sem(f"ysb_free{b}") for b in range(2)]
        gat_in = [[sem(f"gat_in{i}_{k}") for k in range(2)] for i in range(NT)]
        x2_ok = sem("x2_ok")
        ss3_ok = sem("ss3_ok")
        root3_ok = sem("root3_ok")
        res_ok = sem("res_ok")
        out_done = sem("out_done")
        dve_step = sem("dve_step")

        block = stack.enter_context(nc.Block())

        ada_v = ada_w[0].rearrange("(k p) n -> p k n", p=P)
        win_v = w_in[0].rearrange("(k p) n -> p k n", p=P)
        wout_v = w_out[0].rearrange("(k p) n -> p k n", p=P)
        x_v = x[0].rearrange("(t p) d -> p t d", p=P)
        ctx_v = ctx[0].rearrange("(t p) d -> p t d", p=P)
        out_v = out[0].rearrange("(t p) d -> p t d", p=P)

        def row_of(ap, n, parts=P):
            return bass.AP(ap.tensor, ap.offset, [[0, parts], [1, n]])

        A_V, A_B, A_C, P_IN, Q_IN, K_IN, V_IN, F_IN = range(8)
        ORDER = [K_IN, V_IN, Q_IN, F_IN, P_IN, A_V, A_C, A_B]
        FILL = [(F_IN, 0), (F_IN, 1), (P_IN, 0), (P_IN, 1), (A_V, 0), (A_V, 1),
                (A_C, 0), (A_C, 1), (A_B, 0), (A_B, 1)]
        N_ACT_FILL = 6
        UNITS = [(2 * g + h, j) for g in range(2) for j in range(4) for h in range(2)]
        NU = len(UNITS)

        def fills(u):
            return (1, int(u % 5 == 2))

        ADA_SLOT = [n % 4 for n in range(11)] + [1]
        ADA_TURN = [ADA_SLOT[:n].count(ADA_SLOT[n]) + 1 for n in range(12)]

        def by_column(t):
            return t.rearrange("p (c r) -> p r c", r=ROWS)

        def natural(t):
            return t.rearrange("p (r c) -> p r c", r=ROWS)

        @block.sync
        def _(sp):
            sp.dma_start(vec[0:8, :], c.rearrange("a (k p) -> (a k) p", p=P)).then_inc(vec_in, 16)
            sp.dma_start(vec[8:16, :], c_ctx.rearrange("(k p) -> k p", p=P)).then_inc(vec_in, 16)
            sp.dma_start(ctx_sb[:], ctx_v).then_inc(ctx_in, 16)
            for i in range(2):
                sp.dma_start(ada[i][:], ada_v[:, :, i * 512:(i + 1) * 512]).then_inc(ada_in[i], 16)
            sp.dma_start(vec[16:24, :], norm1_g.rearrange("a (k p) -> (a k) p", p=P)).then_inc(vec2_in, 16)
            sp.dma_start(vec[24:26, :], pool_scale.rearrange("a (k p) -> (a k) p", p=P)).then_inc(vec2_in, 16)
            sp.dma_start(vec[26:32, :], conv_w[0].rearrange("j (k p) -> (j k) p", p=P)).then_inc(vec2_in, 16)
            sp.dma_start(vec[32:48, :], ada_b[0, 0:2 * D].rearrange("(k p) -> k p", p=P)).then_inc(vec2_in, 16)
            for i in range(2):
                sp.dma_start(x1[:, 2 * i:2 * i + 2, :], x_v[:, 2 * i:2 * i + 2, :]).then_inc(x_in[i], 16)
                sp.dma_start(ada[2 + i][:], ada_v[:, :, (2 + i) * 512:(3 + i) * 512]).then_inc(ada_in[2 + i], 16)

            def load_win(i):
                n = ORDER[i]
                sp.dma_start(win[i % 4][:], win_v[:, :, n * GW:(n + 1) * GW]).then_inc(win_in[i % 4], 16)

            def load_ada(n):
                a = ADA_SLOT[n]
                if n < 8:
                    sp.wait_ge(ada_pe, n - 3)
                else:
                    sp.wait_ge(ada_dve, n - 7 if n < 11 else 6)
                sp.dma_start(ada[a][:], ada_v[:, :, n * 512:(n + 1) * 512]).then_inc(ada_in[a], 16)

            load_win(0)
            load_win(1)
            sp.wait_ge(rows_zero, 1)
            sp.dma_start(rows[0:1, :, :].rearrange("p a d -> p (a d)"),
                         ada_b[0:1, 2 * D:6 * D]).then_inc(adab_in, 16)
            load_ada(4)
            load_ada(5)
            sp.wait_ge(tab_out, 16)
            for h in range(HEADS):
                sp.dma_start(raw[:, h].rearrange("p a b -> p (a b)"),
                             bass.AP(tab_dram.tensor, h * TAB,
                                     [[RPB_R, 16], [1, ROWS], [1, RUN]])).then_inc(raw_in, 16)
            load_ada(6)
            sp.wait_ge(turn_ok, 4)
            load_win(2)
            load_ada(7)
            sp.wait_ge(pw_zero, 1)
            for g in range(4):
                q = HD * (g % 2)
                sp.dma_start(pw[q:q + HD, g // 2, q:q + HD], pool_w[0, g]).then_inc(poolw_in, 16)
            sp.dma_start(head_dft[:], dft_head).then_inc(consts_in, 16)
            sp.dma_start(rw[:], router_w.rearrange("(k p) e -> p k e", p=P)).then_inc(consts_in, 16)
            sp.dma_start(rb[:], bass.AP(router_b.tensor, router_b.offset,
                                        [[0, P], [0, NT], [1, NE]])).then_inc(consts_in, 16)
            load_ada(8)
            load_ada(9)
            load_ada(10)
            sp.wait_ge(tr_ok, 4)
            load_win(3)
            load_ada(11)
            for i in range(4, 8):
                if i < 7:
                    sp.wait_ge(kv_ok, (4, 10, 12)[i - 4])
                else:
                    sp.wait_ge(pj_ok, 2)
                load_win(i)
            sp.wait_ge(zero_ok, 1)
            sp.dma_start(y_dram[NE * P:, :].rearrange("(p b) (q n) -> p (b q) n", p=P, n=256),
                         zero[:].unsqueeze(1).to_broadcast([P, OVER * 4, 256])).then_inc(zero_stored, 16)
            sp.wait_ge(kv_ok, 12)
            for g in range(4):
                q = HD * (g % 2)
                sp.dma_start(inv[q:q + HD, g // 2, :], row_of(pool_inv[g], N, HD)).then_inc(inv_in, 16)
            for i in range(4):
                sp.wait_ge(pj_ok, 4 + 2 * i)
                sp.dma_start(wout[:, 2 * i:2 * i + 2, :], wout_v[:, 2 * i:2 * i + 2, :]).then_inc(wout_in[i], 16)
            sp.wait_ge(pj_ok, 10)
            sp.dma_start(dft_sb[:], dft_seq.rearrange("(t p) n -> p t n", p=P)).then_inc(dft_in, 16)
            sp.dma_start(n2g[:], row_of(norm2_g, D)).then_inc(n2g_in, 16)
            sp.wait_ge(o_ok, NU)
            sp.dma_start(fing[:], row_of(final_g, D)).then_inc(fing_in, 16)
            sp.wait_ge(zero_stored, 16)
            def load_first(which, sb, e, sem_):
                sp.dma_start(sb[e][:], which[0, e].rearrange("(k p) f -> p k f", p=P)).then_inc(sem_[e], 16)

            sp.wait_ge(pool_ps, 2)
            sp.wait_ge(o_copied, 2)
            load_first(moe_w2, w2_sb, 1, w2_in)
            sp.wait_ge(fn_ok, 2)
            load_first(moe_w1, w1_sb, 1, w1_in)
            sp.wait_ge(wo_ok, 2 * NT)
            load_first(moe_w1, w1_sb, 0, w1_in)
            for b in range(2):
                sp.wait_ge(h2_stored[b], 16 * NT // 2)
            load_first(moe_w3, w3_sb, 0, w3_in)
            load_first(moe_w2, w2_sb, 0, w2_in)
            sp.wait_ge(xg_in[0], 16)
            load_first(moe_w3, w3_sb, 1, w3_in)

            def load_w1(b, e, s):
                sp.wait_ge(h1_ok, s - 1)
                sp.dma_start(w1_sb[b][:], moe_w1[0, bass.ds(e, 1)].rearrange("a (k p) f -> p (a k) f", p=P)
                             ).then_inc(w1_in[b], 16)

            def load_w3(b, e, s):
                sp.wait_ge(h3_ok, s - 1)
                sp.dma_start(w3_sb[b][:], moe_w3[0, bass.ds(e, 1)].rearrange("a (k p) f -> p (a k) f", p=P)
                             ).then_inc(w3_in[b], 16)

            def load_w2(b, e, s):
                sp.wait_ge(y1_ok, s - 1)
                sp.dma_start(w2_sb[b][:], moe_w2[0, bass.ds(e, 1)].rearrange("a (k p) f -> p (a k) f", p=P)
                             ).then_inc(w2_in[b], 16)

            def load_next(b, s):
                load_w1(b, s, s)
                load_w2(1 - b, s - 1, s - 1)
                load_w3(b, s, s)

            load_w1(0, 2, 2)
            load_w3(0, 2, 2)
            load_next(1, 3)
            with sp.Fori(2, NE // 2) as i:
                for b in range(2):
                    load_next(b, i * 2 + b)
            load_w2(1, NE - 1, NE - 1)
            sp.wait_ge(route_ok, 1)
            n_pairs = sp.value_load(ints[0:1, 8:9], min_val=0, max_val=OVER // 2) + NE // 2
            with sp.If(n_pairs > NE // 2):
                with sp.Fori(NE // 2, n_pairs) as i:
                    for b in range(2):
                        e = sp.value_load(ints[0:1, bass.ds(i * 2 + b - NE, 1)], min_val=0, max_val=NE - 1)
                        load_w1(b, e, i * 2 + b)
                        load_w3(b, e, i * 2 + b)
                        load_w2(b, e, i * 2 + b)

            for t in range(NT):
                sp.wait_ge(res_ok, t + 1)
                sp.dma_start(out_v[:, t, :], ygat[:, t, 1, :]).then_inc(out_done, 16)
            sp.wait_ge(out_done, 16 * NT)

        @block.gpsimd
        def _(gp):
            step = [0]

            def link(ins):
                step[0] += 1
                ins.then_inc(gp_step, 1)
                gp.wait_ge(gp_step, step[0])

            link(gp.memset(ident[:], 0.0))
            gp.affine_select(out=ident[:], in_=ident[:], compare_op=ALU.not_equal, fill=1.0, base=0,
                             pattern=[[-1, P]], channel_multiplier=1).then_inc(ident_ok, 1)
            gp.memset(eps[:], EPS).then_inc(eps_ok, 1)
            gp.memset(tabpad[:], 0.0).then_inc(tab_zero, 1)
            gp.wait_ge(tab_zero, 1)
            gp.dma_start(tabpad[:, PAD_C * RPB_R:(PAD_C + RPB_C) * RPB_R],
                         rpb_t.rearrange("h v u -> h (v u)")).then_inc(tabpad_in, 16)
            gp.memset(rows[:].rearrange("p a d -> p (a d)"), 0.0).then_inc(rows_zero, 1)
            gp.memset(pw[:].rearrange("p a d -> p (a d)"), 0.0).then_inc(pw_zero, 1)
            link(gp.memset(ones[:], 1.0))
            link(gp.memset(ones_b[:], 1.0))
            gp.affine_select(out=tri[:], in_=ones_b[:], compare_op=ALU.is_gt, fill=0.0, base=0,
                             pattern=[[1, P]], channel_multiplier=-1).then_inc(ones_ok, 1)
            gp.wait_ge(tabpad_in, 16)
            gp.dma_start(tab_dram, tabpad[:, :]).then_inc(tab_out, 16)
            gp.wait_ge(raw_in, 16 * HEADS)

            def from_left(dst, src_, j0, n):
                return gp.affine_select(out=dst, in_=src_, compare_op=ALU.is_ge, fill=-BIG, base=8 * j0 - 57,
                                        pattern=[[8, n], [0, ROWS]], channel_multiplier=-1)

            def from_right(dst, src_, j0, n):
                return gp.affine_select(out=dst, in_=src_, compare_op=ALU.is_ge, fill=-BIG, base=184 - 8 * j0,
                                        pattern=[[-8, n], [0, ROWS]], channel_multiplier=1)

            def seg(h, a, n=1):
                return bias[:, h, 16 * a:16 * (a + n), :]

            def key(h, a, n=1):
                return raw[:, h, 48 - 16 * (a + n):48 - 16 * a, 0:ROWS][:, ::-1, ::-1]

            for h in range(HEADS):
                from_left(seg(h, 0, 3), key(h, 0, 3), 0, 48)
                from_left(seg(h, 3), key(h, 1), 16, 16)
                from_right(seg(h, 4), key(h, 2), 32, 16)
                from_left(seg(h, 5), key(h, 0), 0, 16)
                link(from_right(seg(h, 6), key(h, 1), 16, 16))
                from_right(seg(h, 0, 3), seg(h, 0, 3), 0, 48).then_inc(bias_ok, 1)
            def low_w(n):
                i, cs_ = 3 + n // 2, slice((n % 2) * P, (n % 2 + 1) * P)
                gp.wait_ge(w_hi_ok, n + 1)
                gp.tensor_tensor(win_lo[i % 4][:, :, cs_], win[i % 4][:, :, cs_], win_hi[n % 2][:], ALU.subtract
                                 ).then_inc(w_lo_ok, 1)

            low_w(0)
            low_w(1)
            gp.wait_ge(kv_ok, 12)
            gp.wait_ge(h_hi_ok, 2)
            gp.tensor_tensor(hT_lo[:, 4:KD, :], hT[:, 4:KD, :], hT_hi[:, 4:KD, :], ALU.subtract).then_inc(h_lo_gp, 1)
            gp.wait_ge(ada_dve, 8)
            gp.memset(zero[:], 0.0).then_inc(zero_ok, 1)
            gp.memset(z[:, :, 0:1], 0.0)
            gp.memset(z[:, :, N + 1:N + 2], 0.0)
            gp.memset(up[:, :, 0:8], 0.0)
            gp.memset(up[:, :, N + 8:N + 16], 0.0).then_inc(pads_ok, 1)
            for n in range(2, len(FILL)):
                low_w(n)
            for i in (1, 3):
                gp.wait_ge(wo_hi_ok, i + 1)
                ks = slice(2 * i, 2 * i + 2)
                gp.tensor_tensor(wout_lo[:, ks, :], wout[:, ks, :], wout_hi[:, ks, :], ALU.subtract).then_inc(wo_lo_gp, 1)
            gp.wait_ge(o_ok, NU)
            gp.iota(pri4[:], [[0, NT], [-1, GROUPS]], base=GROUPS, channel_multiplier=0,
                    allow_small_or_imprecise_dtypes=True)
            gp.iota(pri16[:], [[0, NT], [-1, NE]], base=NE, channel_multiplier=0,
                    allow_small_or_imprecise_dtypes=True)
            gp.iota(eno[:], [[1, NE]], base=0, channel_multiplier=0, allow_small_or_imprecise_dtypes=True)
            gp.iota(iota_slot[:], [[1, P]], base=0, channel_multiplier=0, allow_small_or_imprecise_dtypes=True)
            gp.iota(iota_blk[:], [[1, NB]], base=0, channel_multiplier=0, allow_small_or_imprecise_dtypes=True)
            gp.iota(iota8[:], [[1, 8]], base=0, channel_multiplier=0, allow_small_or_imprecise_dtypes=True)
            gp.memset(cs[:, :, 0:8], 0.0)
            gp.iota(tok[:], [[0, 1]], base=0, channel_multiplier=1, allow_small_or_imprecise_dtypes=True)
            gp.iota(tok_chunk[:].rearrange("p (t k) -> p t k", k=2), [[1, NT], [0, 2]], base=-(EMPTY // P),
                    channel_multiplier=0, allow_small_or_imprecise_dtypes=True).then_inc(iota_ok, 1)
            gp.wait_ge(logit_ok, NT)
            gp.memset(xg[0][:], 0.0)
            link(gp.memset(xg[1][:], 0.0))

            gp.wait_ge(idx_ok, 1)
            for b in range(2):
                gp.wait_ge(h2_stored[b], 16 * NT // 2)

            def gather_rows(b, index):
                gp.indirect_dma_start(xg[b][:], None, h2_dram,
                                      bass.IndirectOffsetOnAxis(ap=index, axis=0),
                                      bounds_check=N - 1, oob_is_err=False).then_inc(xg_in[b], 16)

            def gather(b, s):
                gp.wait_ge(xt_ok, s - 1)
                gp.tensor_copy(idx1[b][:, 0:1], idx[:, bass.ds(s, 1)]).then_inc(idx1_ok, 1)
                gp.wait_ge(idx1_ok, s - 1)
                gp.sem_inc(gather_go, 1)
                gather_rows(b, idx1[b][:, 0:1])

            for b in range(2):
                gather_rows(b, idx[:, b:b + 1])
            gp.wait_ge(route_ok, 1)
            n_pairs = gp.value_load(ints[0:1, 8:9], min_val=0, max_val=OVER // 2) + NE // 2
            with gp.Fori(1, n_pairs) as i:
                for b in range(2):
                    gather(b, i * 2 + b)
            gp.wait_ge(slots_ok, 1)
            gp.wait_ge(ysb_free[0], n_pairs * 16 + 16)
            gp.wait_ge(ysb_free[1], n_pairs * 16 + 16)
            gp.sem_inc(gather_go, 1)
            for t in range(NT):
                for k in range(2):
                    gp.indirect_dma_start(ygat[:, t, k, :], None, y_dram,
                                          bass.IndirectOffsetOnAxis(ap=slot_idx[:, t, k:k + 1], axis=0)
                                          ).then_inc(gat_in[t][k], 16)

        @block.tensor
        def _(pe):
            pe.wait_ge(vec_in, 32)
            pe.wait_ge(ident_ok, 1)
            pe.transpose(bank[7][:, 0:16], vec[0:16, :], ident[0:16, 0:16]).then_inc(vecT_ok, 1)

            def turn_input(g):
                if g >= 5:
                    pe.wait_ge(tr_free, g - 4)
                for i in range(4):
                    if g < 4:
                        src = ctx_sb[:, i % 2, (2 * g + i // 2) * P:(2 * g + i // 2 + 1) * P]
                    else:
                        src = xn[:, i, (g - 4) * P:(g - 3) * P]
                    m = pe.transpose(bank[g % 5][:, i * P:(i + 1) * P], src, ident[:])
                m.then_inc(tr_ok, 1)

            def modulation(n):
                pe.wait_ge(ada_in[n], 16)
                if n >= 2:
                    pe.wait_ge(mrow_ok, n - 1)
                for k in range(KD):
                    m = pe.matmul(bank[6 + n % 2][0:2, :], cc[:, k, :], ada[n][:, k, :],
                                  start=(k == 0), stop=(k == KD - 1))
                m.then_inc(ada_pe, 1)

            def turn_mod(n):
                pe.wait_ge(mrow_ok, n + 1)
                if n == 0:
                    pe.wait_ge(cols_ok, 2)
                for i in range(4):
                    m = pe.transpose(bank[5 + n // 3][:, 8 * n + 2 * i:8 * n + 2 * i + 2], mod_rows[:, n, i * P:(i + 1) * P],
                                     ident[0:2, 0:2])
                m.then_inc(turn_ok, 1)

            pe.wait_ge(xn_ok, LT)
            for g in range(4):
                turn_input(g)
            pe.wait_ge(cc_ok, 1)
            modulation(0)
            pe.wait_ge(vec2_in, 64)
            pe.transpose(bank[5][:, 64:112], vec[:], ident[0:48, 0:48]).then_inc(vecT_ok, 1)
            modulation(1)
            turn_mod(0)
            modulation(2)
            turn_mod(1)
            pe.wait_ge(xn_ok, LT + NT)
            for g in range(4, 4 + KD):
                turn_input(g)
            turn_mod(2)
            modulation(3)
            turn_mod(3)

            def kv_tile(n, make):
                if n < 6:
                    pe.wait_ge(tr_free, 12)
                else:
                    pe.wait_ge(kv_free, n - 5)
                m = make(bank[n % 6])
                m.then_inc(kv_ok, 1)
                return m

            def channel_tile(slot_, half, src, width, ready=None):
                def make(b):
                    for k in range(KD):
                        if ready is not None:
                            pe.wait_ge(ready, k + 1)
                        m = pe.matmul(b[:, 0:width], win[slot_][:, k, half * P:(half + 1) * P],
                                      src[:, k, :], start=(k == 0), stop=(k == KD - 1))
                    return m
                return make

            def value_tile(slot_, lhs):
                def make(b):
                    for k in range(KD):
                        m = pe.matmul(b[:, 0:GW], lhs(k), win[slot_][:, k, :],
                                      start=(k == 0), stop=(k == KD - 1))
                    return m
                return make

            pe.wait_ge(win_in[0], 16)
            kv_tile(0, channel_tile(0, 0, hT, N, h_ok))
            kv_tile(1, channel_tile(0, 1, hT, N))
            pe.wait_ge(hc_ok, 1)
            kv_tile(2, channel_tile(0, 0, hcT, L))
            kv_tile(3, channel_tile(0, 1, hcT, L))
            pe.wait_ge(win_in[1], 16)
            for t in range(LT):
                kv_tile(4 + t, value_tile(1, lambda k: hcT[:, k, t * P:(t + 1) * P]))
            for m_ in range(NT):
                kv_tile(6 + m_, value_tile(1, lambda k: hT[:, k, m_ * P:(m_ + 1) * P]))
            pe.wait_ge(win_in[2], 16)
            kv_tile(10, channel_tile(2, 0, hT, N))
            kv_tile(11, channel_tile(2, 1, hT, N))

            def fill(n):
                tile, part = n // 2, n % 2
                if tile >= len(FILL):
                    return
                i, half = 3 + tile // 2, tile % 2
                if part == 0:
                    pe.wait_ge(w_lo_ok, tile + 1)
                    if 1 <= tile <= N_ACT_FILL:
                        pe.wait_ge(pj_act, tile)
                    elif tile > N_ACT_FILL:
                        pe.wait_ge(pj_dve, tile - N_ACT_FILL)
                if tile == 0:
                    pe.wait_ge((h_lo_dve, h_lo_gp)[part], 1)
                w_lo = win_lo[i % 4][:, :, half * P:(half + 1) * P]
                for k in range(4 * part, 4 * part + 4):
                    pe.matmul(bank[7][:], win_hi[half][:, k, :], hT_hi[:, k, :], start=(k == 0), stop=False)
                    pe.matmul(bank[7][:], win_hi[half][:, k, :], hT_lo[:, k, :], start=False, stop=False)
                    m = pe.matmul(bank[7][:], w_lo[:, k, :], hT_hi[:, k, :], start=False, stop=(k == KD - 1))
                if part == 1:
                    m.then_inc(pj_ok, 1)

            def scores(u):
                h, j = UNITS[u]
                m0, m1, _ = KEYS[j]
                q0 = HD * (h % 2)
                if u >= 2:
                    pe.wait_ge(ex_ok, u - 1)
                q = qT[q0:q0 + HD, h // 2, j * P:(j + 1) * P]
                pe.matmul(bank[2 * (u % 2)][:, 0:(m1 - m0) * P], q, kT[q0:q0 + HD, h // 2, m0 * P:m1 * P],
                          start=True, stop=True)
                pe.matmul(bank[2 * (u % 2) + 1][:, 0:L], q, kcT[q0:q0 + HD, h // 2, :],
                          start=True, stop=True).then_inc(s_ok, 1)

            def values(u):
                h, j = UNITS[u]
                m0, m1, _ = KEYS[j]
                nb = m1 - m0 + LT
                pe.wait_ge(pn_ok, u + 1)
                if u >= 1:
                    pe.wait_ge(pt_copied, u)
                for i in range(nb):
                    m = pe.transpose(bank[4 + i // 4][:, (i % 4) * P:(i % 4 + 1) * P],
                                     pr[:, u % 2, i * P:(i + 1) * P], ident[:])
                m.then_inc(pt_ok, 1)

            def output(u):
                h, j = UNITS[u]
                m0, m1, _ = KEYS[j]
                nb = m1 - m0 + LT
                pe.wait_ge(pt_copied, u + 1)
                if u == NU // 2:
                    pe.wait_ge(o_copied, 1)
                for i in range(nb):
                    w = m1 - m0
                    v = v_sb[:, m0 + i, h * HD:(h + 1) * HD] if i < w else vc_sb[:, i - w, h * HD:(h + 1) * HD]
                    m = pe.matmul(bank[6][HD * (h % 2):HD * (h % 2) + HD, j * P:(j + 1) * P], v,
                                  pT[:, u % 2, i * P:(i + 1) * P], start=(i == 0), stop=(i == nb - 1))
                m.then_inc(o_ok, 1)

            pe.wait_ge(kv_free, 12)
            nf = 0
            for u in range(NU + 2):
                if u < NU:
                    scores(u)
                if fills(u)[0] and nf < 20:
                    fill(nf)
                    nf += 1
                if 1 <= u <= NU:
                    values(u - 1)
                if fills(u)[1] and nf < 20:
                    fill(nf)
                    nf += 1
                if u >= 2:
                    output(u - 2)
            while nf < 20:
                fill(nf)
                nf += 1

            pe.wait_ge(poolw_in, 64)
            pe.wait_ge(d_ok, 1)
            pe.wait_ge(pj_dve, 4)
            for h in range(2):
                pe.matmul(bank[4 + h][:], pw[:, h, :], dpool[:, h, :],
                          start=True, stop=True).then_inc(pool_ps, 1)
            pe.wait_ge(consts_in, 48)
            for t in range(NT):
                for h in range(2):
                    m = pe.matmul(bank[t][:, h * GW:(h + 1) * GW], fT[:, h, t * P:(t + 1) * P], head_dft[:],
                                  start=True, stop=True)
                m.then_inc(fd_ok, 1)
            pe.wait_ge(dft_in, 16)
            pe.wait_ge(pool_ok, 2)
            for h in range(2):
                for part, cols_ in ((0, slice(0, NC)), (1, slice(NC, N))):
                    for t in range(NT):
                        if h == 0 and part == 0:
                            pe.wait_ge(fd_copied, t + 1)
                        m = pe.matmul(bank[4 + h][:, cols_], fcs[:, t, h, part * P:(part + 1) * P],
                                      dft_sb[:, t, cols_], start=(t == 0), stop=(t == NT - 1))
                m.then_inc(fn_ok, 1)
            pe.wait_ge(ones_ok, 1)
            pe.wait_ge(ada_dve, 8)
            def row_sum(n):
                pe.matmul(bank[n % 4][:], ones[:], rows[:, n // 2, (n % 2) * 512:(n % 2 + 1) * 512],
                          start=True, stop=True).then_inc(rowsum_ok, 1)

            for n in range(6):
                if n >= 4:
                    pe.wait_ge(rows_act, n - 3)
                row_sum(n)
            pe.wait_ge(wo_lo_ok, 2)
            pe.wait_ge(wo_lo_gp, 2)
            pe.wait_ge(y_lo_ok, 5)
            pe.wait_ge(rows_act, 6)

            def project(n):
                t, half = n // 2, n % 2
                if n >= 4:
                    pe.wait_ge(x1_ok, n - 3)
                for k in range(KD):
                    tc, cc_ = slice(t * P, (t + 1) * P), slice(half * 512, (half + 1) * 512)
                    pe.matmul(bank[n % 4][:], yT_hi[:, k, tc], wout_hi[:, k, cc_], start=(k == 0), stop=False)
                    pe.matmul(bank[n % 4][:], yT_hi[:, k, tc], wout_lo[:, k, cc_], start=False, stop=False)
                    m = pe.matmul(bank[n % 4][:], yT_lo[:, k, tc], wout_hi[:, k, cc_], start=False,
                                  stop=(k == KD - 1))
                m.then_inc(wo_ok, 1)

            def turn_h2(t):
                for g in range(2):
                    pe.wait_ge(h2_ok, 2 * t + g + 1)
                    if t >= 1:
                        pe.wait_ge(h2T_ok, 2 * (t - 1) + g + 1)
                    for i in range(4):
                        k = 4 * g + i
                        m = pe.transpose(bank[4 + g][:, i * P:(i + 1) * P], h2[:, t % 2, k * P:(k + 1) * P], ident[:])
                    m.then_inc(h2tr_ok, 1)

            def router(t):
                for k in range(KD):
                    if k % 4 == 0:
                        pe.wait_ge(h2T_ok, 2 * t + 1 + k // 4)
                    m = pe.matmul(bank[7][:, t * NE:(t + 1) * NE], h2T[:, k, t * P:(t + 1) * P], rw[:, k, :],
                                  start=(k == 0), stop=(k == KD - 1))
                m.then_inc(logit_ok, 1)

            for t in range(NT):
                project(2 * t)
                if t >= 1:
                    turn_h2(t - 1)
                project(2 * t + 1)
                if t >= 1:
                    router(t - 1)
            turn_h2(NT - 1)
            router(NT - 1)
            pe.wait_ge(x1_ok, 2 * NT)
            row_sum(6)
            row_sum(7)
            pe.wait_ge(prob_ok, 1)
            pe.wait_ge(sel_ok, 1)
            for t in range(NT):
                for i in range(t + 1):
                    pe.matmul(bank[7][:, t * NE:(t + 1) * NE], tri[:] if i == t else ones_b[:],
                              sel[:, i, :], start=(i == 0), stop=(i == t))
            for i in range(NT):
                m = pe.matmul(bank[7][:, NT * NE:(NT + 1) * NE], ones_b[:], sel[:, i, :],
                              start=(i == 0), stop=(i == NT - 1))
            m.then_inc(rank_ok, 1)
            pe.wait_ge(hot_ok, 1)
            for i in range(2 * NT):
                m = pe.matmul(bank[6][:, 0:2 * NB], hot_slot[:, i, :], hot_tok[:, i].rearrange("p a b -> p (a b)"),
                              start=(i == 0), stop=(i == 2 * NT - 1))
            m.then_inc(idxps_ok, 1)
            pe.wait_ge(rows_act, 8)
            for _ in range(WARM):
                pe.matmul(bank[3][:], ones[:], rows[:, G2, 0:512], start=True, stop=True)

            pe.wait_ge(route_ok, 1)
            n_pairs = pe.value_load(ints[0:1, 8:9], min_val=0, max_val=OVER // 2) + NE // 2

            def rows_in(b, s, i):
                pe.wait_ge(xg_in[b], i * 16 + 16)
                if not (isinstance(s, int) and s == 0):
                    pe.wait_ge(xt_copied, s)
                for k in range(KD):
                    m = pe.transpose(bank[k // 4][:, (k % 4) * P:(k % 4 + 1) * P], xg[b][:, k * P:(k + 1) * P], ident[:])
                m.then_inc(xt_ok, 1)

            def hidden1(b, s, i):
                pe.wait_ge(w1_in[b], i * 16 + 16)
                if not (isinstance(s, int) and s == 0):
                    pe.wait_ge(sg_ok, s)
                for k in range(KD):
                    m = pe.matmul(bank[2][:], xgT[:, k, :], w1_sb[b][:, k, :], start=(k == 0), stop=(k == KD - 1))
                m.then_inc(h1_ok, 1)

            def hidden3(b, s):
                pe.wait_ge(x_lo_ok, s + 1)
                if not (isinstance(s, int) and s == 0):
                    pe.wait_ge(he_ok, s)
                for k in range(KD):
                    if k % 4 == 0:
                        pe.wait_ge(w3_lo_ok, s * 2 + 1 + k // 4)
                    pe.matmul(bank[3][:], xgT_hi[:, k, :], w3_hi[:, k, :], start=(k == 0), stop=False)
                    pe.matmul(bank[3][:], xgT_hi[:, k, :], w3_lo[b][:, k, :], start=False, stop=False)
                    m = pe.matmul(bank[3][:], xgT_lo[:, k, :], w3_hi[:, k, :], start=False, stop=(k == KD - 1))
                m.then_inc(h3_ok, 1)

            def hidden_turned(b, s):
                pe.wait_ge(he_ok, s + 1)
                if not (isinstance(s, int) and s == 0):
                    pe.wait_ge(het_lo_ok, s)
                for k in range(KF):
                    m = pe.transpose(bank[4][:, k * P:(k + 1) * P], he[:, k * P:(k + 1) * P], ident[:])
                m.then_inc(het_ok, 1)

            def expert_out(b, s, half, copied, ok, first):
                if half == 0:
                    pe.wait_ge(het_lo_ok, s + 1)
                pe.wait_ge(w2_lo_ok[half], s + 1)
                if not first:
                    pe.wait_ge(copied, s)
                hs = slice(half * 512, (half + 1) * 512)
                for k in range(KF):
                    pe.matmul(bank[5 + half][:], heT_hi[:, k, :], w2_hi[:, k, hs], start=(k == 0), stop=False)
                    pe.matmul(bank[5 + half][:], heT_hi[:, k, :], w2_lo[b][:, k, hs], start=False, stop=False)
                    m = pe.matmul(bank[5 + half][:], heT_lo[:, k, :], w2_hi[:, k, hs], start=False,
                                  stop=(k == KF - 1))
                m.then_inc(ok, 1)

            def block_(b, s, i, prev, prev_first):
                rows_in(b, s, i)
                if prev is not None:
                    expert_out(1 - b, prev, 0, y0_copied, y0_ok, prev_first)
                pe.wait_ge(xt_copied, s + 1)
                hidden1(b, s, i)
                hidden3(b, s)
                if prev is not None:
                    expert_out(1 - b, prev, 1, y1_copied, y1_ok, prev_first)
                hidden_turned(b, s)

            block_(0, 0, 0, None, False)
            block_(1, 1, 0, 0, True)
            with pe.Fori(1, n_pairs) as i:
                block_(0, i * 2, i, i * 2 - 1, False)
                block_(1, i * 2 + 1, i, i * 2, False)
            last = n_pairs * 2 - 1
            expert_out(1, last, 0, y0_copied, y0_ok, False)
            expert_out(1, last, 1, y1_copied, y1_ok, False)

        @block.scalar
        def _(act):
            act.wait_ge(cols_ok, 1)
            act.activation(cc[:].rearrange("p k v -> p v k"), cols[:, 0:16].rearrange("p (v k) -> p v k", v=2),
                           ACT.Silu).then_inc(cc_ok, 1)
            act.wait_ge(eps_ok, 1)

            def squares(t):
                src = ctx_sb[:, t, :] if t < LT else x1[:, t - LT, :]
                act.activation(hT[:, 2 * t:2 * t + 2, :].rearrange("p a n -> p (a n)") if t < LT
                               else xn[:, t - LT, :], src, ACT.Square,
                               accum_out=stat[:, t, 0:1]).then_inc(ss_ok, 1)

            def root(t):
                act.wait_ge(ss_ok, t + 1)
                act.activation(stat[:, t, 2:3], stat[:, t, 0:1], ACT.Sqrt, bias=eps[:], scale=1.0 / D
                               ).then_inc(root_ok, 1)

            def input_copy(g):
                act.wait_ge(tr_ok, g + 1)
                b = bank[g % 5]
                if g < 4:
                    m = act.copy(hcT[:, 2 * g:2 * g + 2, :].rearrange("p a t -> p (a t)"), b)
                else:
                    m = act.copy(by_column(hT[:, g - 4, :]), natural(b))
                m.then_inc(tr_free, 1)

            def mod_copy(n):
                act.wait_ge(ada_pe, n + 1)
                act.copy(mod_rows[:, n, :], bank[6 + n % 2][0:2, :]).then_inc(mrow_ok, 1)

            act.wait_ge(ctx_in, 16)
            for t in range(LT):
                squares(t)
            for t in range(LT):
                root(t)
            for g in range(4):
                input_copy(g)
            mod_copy(0)
            act.wait_ge(x_in[0], 16)
            squares(2)
            squares(3)
            mod_copy(1)
            act.wait_ge(x_in[1], 16)
            squares(4)
            squares(5)
            for t in range(LT, LT + NT):
                root(t)
            mod_copy(2)
            for g in range(4, 4 + KD):
                input_copy(g)
            mod_copy(3)
            def high_w(n):
                i, cs_ = 3 + n // 2, slice((n % 2) * P, (n % 2 + 1) * P)
                act.wait_ge(win_in[i % 4], 16 * (i // 4 + 1))
                act.copy(win_hi[n % 2][:], win[i % 4][:, :, cs_]).then_inc(w_hi_ok, 1)

            for n in range(12):
                act.wait_ge(kv_ok, n + 1)
                b = bank[n % 6]
                if n < 2:
                    m = act.copy(kT[:, n, :], b)
                elif n < 4:
                    m = act.copy(kcT[:, n - 2, :], b[:, 0:L])
                elif n < 6:
                    m = act.copy(vc_sb[:, n - 4, :], b[:, 0:GW])
                elif n < 10:
                    m = act.copy(v_sb[:, n - 6, :], b[:, 0:GW])
                else:
                    m = act.activation(qT[:, n - 10, :], b, ACT.Copy, scale=SCALE)
                m.then_inc(kv_free, 1)
                if n == 10:
                    act.wait_ge(ada_dve, 5)
                    high_w(0)
                    high_w(1)
                if n == 7:
                    act.wait_ge(h_ok, KD)
                    act.wait_ge(ada_dve, 4)
                    for i in range(2):
                        act.copy(hT_hi[:, 4 * i:4 * i + 4, :].rearrange("p k n -> p (k n)"),
                                 hT[:, 4 * i:4 * i + 4, :].rearrange("p k n -> p (k n)")).then_inc(h_hi_ok, 1)


            def tile_done(n):
                act.wait_ge(pj_ok, n + 1)
                if n < N_ACT_FILL:
                    fill_copy(n)
                if n + 2 < len(FILL):
                    high_w(n + 2)

            def fill_copy(n):
                piece, half = FILL[n]
                if n == 0:
                    act.wait_ge(ada_dve, 8)
                    act.wait_ge(pads_ok, 1)
                dst = {F_IN: fT[:, half, :], P_IN: up[:, half, 8:8 + N], A_V: av[:, half, :]}[piece]
                act.copy(natural(dst), by_column(bank[7])).then_inc(pj_act, 1)

            def expo(u):
                h, j = UNITS[u]
                w = (KEYS[j][1] - KEYS[j][0]) * P
                s = u % 2
                act.wait_ge(nm_ok, u + 1)
                if u >= 2:
                    act.wait_ge(pt_ok, u - 1)
                act.activation(pr[:, s, 0:w], sw[:, s, 0:w], ACT.Exp, bias=soft[:, s, 2:3],
                               accum_out=soft[:, s, 3:4])
                act.activation(pr[:, s, w:w + L], bank[2 * s + 1][:, 0:L], ACT.Exp, bias=soft[:, s, 2:3],
                               accum_out=soft[:, s, 4:5]).then_inc(ex_ok, 1)

            def pt_copy(u):
                h, j = UNITS[u]
                n = (KEYS[j][1] - KEYS[j][0] + LT) * P
                act.wait_ge(pt_ok, u + 1)
                if u >= 2:
                    act.wait_ge(o_ok, u - 1)
                act.copy(pT[:, u % 2, 0:n], psum[:, 4:6, :].rearrange("p a n -> p (a n)")[:, 0:n]
                         ).then_inc(pt_copied, 1)

            def high_wout(i):
                act.wait_ge(wout_in[i], 16)
                act.wait_ge(pj_dve, 4)
                act.wait_ge(d_ok, 1)
                act.wait_ge(zero_stored, 16)
                act.copy(wout_hi[:, 2 * i:2 * i + 2, :].rearrange("p k n -> p (k n)"),
                         wout[:, 2 * i:2 * i + 2, :].rearrange("p k n -> p (k n)")).then_inc(wo_hi_ok, 1)

            done = 0
            nf = 0
            for u in range(NU + 2):
                if u < NU:
                    expo(u)
                nf = min(20, nf + fills(u)[0])
                if done < len(FILL) and nf >= 2 * (done + 1):
                    tile_done(done)
                    done += 1
                if 1 <= u <= NU:
                    pt_copy(u - 1)
                nf = min(20, nf + fills(u)[1])
                if done < len(FILL) and nf >= 2 * (done + 1):
                    tile_done(done)
                    done += 1
                if u >= NU:
                    high_wout(u - NU)
            assert done == len(FILL)
            for h in range(2):
                act.wait_ge(pool_ps, h + 1)
                act.activation(yT[:, 2 + h, :], bank[4 + h], ACT.Copy, scale=cols[:, 24 + h:25 + h]
                               ).then_inc(pool_ok, 1)
            for t in range(NT):
                act.wait_ge(fd_ok, t + 1)
                act.copy(fcs[:, t].rearrange("p a n -> p (a n)"), bank[t]).then_inc(fd_copied, 1)
            high_wout(2)
            high_wout(3)
            act.wait_ge(o_copied, 2)
            act.wait_ge(pool_ok, 2)
            for i in range(3):
                act.copy(yT_hi[:, 2 * i:2 * i + 2, :].rearrange("p k n -> p (k n)"),
                         yT[:, 2 * i:2 * i + 2, :].rearrange("p k n -> p (k n)")).then_inc(y_hi_ok, 1)
            for h in range(2):
                act.wait_ge(fn_ok, h + 1)
                act.copy(yT[:, 6 + h, 0:NC], bank[4 + h][:, 0:NC]).then_inc(fn_even, 1)

            def row_copy(n):
                act.wait_ge(rowsum_ok, n + 1)
                act.copy(rows[:, n // 2, (n % 2) * 512:(n % 2 + 1) * 512], bank[n % 4]).then_inc(rows_act, 1)

            for h in range(2):
                row_copy(2 * h)
                row_copy(2 * h + 1)
                act.wait_ge(fn_copied, h + 1)
                act.copy(yT_hi[:, 6 + h, :], yT[:, 6 + h, :]).then_inc(y_hi_ok, 1)
            row_copy(4)
            row_copy(5)
            def squares2(n):
                t, half = n // 2, n % 2
                act.wait_ge(x1_ok, n + 1)
                if n >= 1:
                    act.wait_ge(ss2_ok, n)
                act.activation(bank[6], x1[:, t, half * 512:(half + 1) * 512], ACT.Square,
                               accum_out=st2[:, t, half:half + 1]).then_inc(ss2_ok, 1)

            def h2T_copy(t):
                for g in range(2):
                    act.wait_ge(h2tr_ok, 2 * t + g + 1)
                    act.copy(h2T[:, 4 * g:4 * g + 4, t * P:(t + 1) * P],
                             bank[4 + g].rearrange("p (k t) -> p k t", t=P)).then_inc(h2T_ok, 1)

            for t in range(NT):
                squares2(2 * t)
                if t >= 1:
                    h2T_copy(t - 1)
                squares2(2 * t + 1)
                act.wait_ge(ms2_ok, t + 1)
                act.activation(st2[:, t, 3:4], st2[:, t, 2:3], ACT.Sqrt, bias=eps[:]).then_inc(root2_ok, 1)
                act.wait_ge(h2_ok, 2 * t + 2)
                act.dma_start(h2_dram[t * P:(t + 1) * P, :], h2[:, t % 2, :]).then_inc(h2_stored[t % 2], 16)
            h2T_copy(NT - 1)
            act.wait_ge(logit_ok, NT)
            act.activation(prob[:].rearrange("p t e -> p (t e)"), bank[7][:, 0:NT * NE], ACT.Sigmoid
                           ).then_inc(prob_ok, 1)
            row_copy(6)
            row_copy(7)

            act.wait_ge(route_ok, 1)
            n_pairs = act.value_load(ints[0:1, 8:9], min_val=0, max_val=OVER // 2) + NE // 2

            def high_w2(b, s, half, used):
                if not (isinstance(s, int) and s == 0):
                    act.wait_ge(used, s)
                hs = slice(half * 512, (half + 1) * 512)
                act.copy(w2_hi[:, :, hs], w2_sb[b][:, :, hs]).then_inc(w2_hi_ok[half], 1)

            def block_(b, s, i, store):
                act.wait_ge(w3_in[b], i * 16 + 16)
                if not (isinstance(s, int) and s == 0):
                    act.wait_ge(h3_ok, s)
                for g in range(2):
                    act.copy(w3_hi[:, 4 * g:4 * g + 4, :].rearrange("p k f -> p (k f)"),
                             w3_sb[b][:, 4 * g:4 * g + 4, :].rearrange("p k f -> p (k f)")).then_inc(w3_hi_ok, 1)
                act.wait_ge(xt_copied, s + 1)
                act.copy(xgT_hi[:].rearrange("p k t -> p (k t)"), xgT[:].rearrange("p k t -> p (k t)")
                         ).then_inc(x_hi_ok, 1)
                act.wait_ge(h1_ok, s + 1)
                if not (isinstance(s, int) and s == 0):
                    act.wait_ge(he_ok, s)
                act.activation(sg[:], bank[2], ACT.Silu).then_inc(sg_ok, 1)
                act.wait_ge(w2_in[b], i * 16 + 16)
                high_w2(b, s, 0, y0_ok)
                act.wait_ge(het_ok, s + 1)
                if not (isinstance(s, int) and s == 0):
                    act.wait_ge(y1_ok, s)
                act.copy(heT_hi[:].rearrange("p k t -> p (k t)"), bank[4]).then_inc(het_hi_ok, 1)
                if store is not None:
                    store_rows(1 - b, store)
                high_w2(b, s, 1, y1_ok)

            def store_rows(b, s):
                act.wait_ge(y1_copied, s + 1)
                act.dma_start(y_dram[bass.ds(s * P, P), :], ysb[b][:]).then_inc(ysb_free[b], 16)

            for b in range(2):
                act.sem_inc(ysb_free[b], 16)
            block_(0, 0, 0, None)
            block_(1, 1, 0, 0)
            with act.Fori(1, n_pairs) as i:
                block_(0, i * 2, i, i * 2 - 1)
                block_(1, i * 2 + 1, i, i * 2)
            store_rows(1, n_pairs * 2 - 1)

            for t in range(NT):
                act.wait_ge(x2_ok, t + 1)
                act.activation(ygat[:, t, 0, :], x1[:, t, :], ACT.Square, accum_out=st2[:, t, 5:6]).then_inc(ss3_ok, 1)
                act.wait_ge(ss3_ok, t + 1)
                act.activation(st2[:, t, 6:7], st2[:, t, 5:6], ACT.Sqrt, bias=eps[:], scale=1.0 / D
                               ).then_inc(root3_ok, 1)

        @block.vector
        def _(v):
            step = [0]

            def link(ins):
                step[0] += 1
                ins.then_inc(dve_step, 1)
                v.wait_ge(dve_step, step[0])

            v.wait_ge(vecT_ok, 1)
            v.tensor_copy(cols[:, 0:16], bank[7][:, 0:16]).then_inc(cols_ok, 1)

            def normalise(t):
                v.wait_ge(root_ok, t + 1)
                link(v.reciprocal(stat[:, t, 3:4], stat[:, t, 2:3]))
                src = ctx_sb[:, t, :] if t < LT else x1[:, t - LT, :]
                dst = ctx_sb[:, t, :] if t < LT else xn[:, t - LT, :]
                v.tensor_scalar(dst, src, stat[:, t, 3:4], None, ALU.mult).then_inc(xn_ok, 1)

            for t in range(LT):
                normalise(t)
            v.wait_ge(vecT_ok, 2)
            v.tensor_copy(cols[:, 16:48], bank[5][:, 80:112]).then_inc(cols_ok, 1)
            for t in range(LT, LT + NT):
                normalise(t)

            def mod_columns(n0, n1):
                w = n1 - n0
                link(v.tensor_tensor(modc[:, n0:n1, :], bank[5 + n0 // 12][:, 2 * n0:2 * n1].rearrange("p (n v) -> p n v", v=2),
                                     cols[:, 32 + n0:32 + n1].unsqueeze(2).to_broadcast([P, w, 2]), ALU.add))
                if n0 >= 8:
                    link(v.scalar_tensor_tensor(out=a1[:, n0 - 8:n1 - 8, :], in0=modc[:, n0:n1, :], scalar=1.0,
                                                in1=cols[:, 8 + n0:8 + n1].unsqueeze(2).to_broadcast([P, w, 2]),
                                                op0=ALU.add, op1=ALU.mult))

            def modulate(t_, k, which):
                return v.tensor_scalar(t_[:, k, :], t_[:, k, :], a1[:, k, which:which + 1],
                                       modc[:, k, which:which + 1], ALU.mult, ALU.add)

            v.wait_ge(cols_ok, 2)
            v.wait_ge(turn_ok, 3)
            mod_columns(0, 8)
            mod_columns(8, 12)
            v.wait_ge(tr_free, 12)
            for k in range(4):
                modulate(hT, k, 0).then_inc(h_ok, 1)
            for k in range(4):
                modulate(hcT, k, 1)
            v.wait_ge(turn_ok, 4)
            mod_columns(12, 16)
            for k in range(4, KD):
                modulate(hT, k, 0).then_inc(h_ok, 1)
            for k in range(4, KD):
                m = modulate(hcT, k, 1)
            m.then_inc(hc_ok, 1)
            v.wait_ge(adab_in, 16)
            for n in range(4, 12):
                a = ADA_SLOT[n]
                v.wait_ge(ada_in[a], 16 * ADA_TURN[n])
                o = rows[:, (n - 4) // 2, (n % 2) * 512:(n % 2 + 1) * 512]
                for k in range(KD):
                    ins = v.scalar_tensor_tensor(out=o, in0=ada[a][:, k, :], scalar=cc[:, k, 0:1], in1=o,
                                                 op0=ALU.mult, op1=ALU.add)
                    if k < KD - 1:
                        link(ins)
                ins.then_inc(ada_dve, 1)

            def softmax_bias(u):
                h, j = UNITS[u]
                m0, m1, sg0 = KEYS[j]
                w = (m1 - m0) * P
                s = u % 2
                v.wait_ge(s_ok, u + 1)
                b = bias[:, h, sg0 * 16:(sg0 + m1 - m0) * 16, :].rearrange("p a b -> p (a b)")
                v.tensor_tensor_reduce(sw[:, s, 0:w], bank[2 * s][:, 0:w], b, 1.0, -3e38, ALU.add, ALU.max,
                                       soft[:, s, 0:1]).then_inc(sb_ok, 1)
                link(v.tensor_reduce(soft[:, s, 1:2], bank[2 * s + 1][:, 0:L], AX, ALU.max))
                v.wait_ge(sb_ok, u + 1)
                v.tensor_scalar(soft[:, s, 2:3], soft[:, s, 0:1], soft[:, s, 1:2], -1.0, ALU.max, ALU.mult
                                ).then_inc(nm_ok, 1)

            def softmax_norm(u):
                h, j = UNITS[u]
                w = (KEYS[j][1] - KEYS[j][0]) * P
                s = u % 2
                v.wait_ge(ex_ok, u + 1)
                link(v.tensor_tensor(soft[:, s, 5:6], soft[:, s, 3:4], soft[:, s, 4:5], ALU.add))
                link(v.reciprocal(soft[:, s, 6:7], soft[:, s, 5:6]))
                v.tensor_scalar(pr[:, s, 0:w + L], pr[:, s, 0:w + L], soft[:, s, 6:7], None, ALU.mult
                                ).then_inc(pn_ok, 1)

            def head_pair(g):
                v.wait_ge(o_ok, NU // 2 * (g + 1))
                v.tensor_copy(yT[:, 4 + g, :].rearrange("p (r c) -> p c r", r=ROWS),
                              bank[6].rearrange("p (c r) -> p c r", r=ROWS)).then_inc(o_copied, 1)

            def pool_diff():
                W = N + 16
                v.wait_ge(pj_act, 4)
                v.wait_ge(pads_ok, 1)
                v.wait_ge(inv_in, 64)
                link(v.tensor_tensor(s2[:, :, 1:W], up[:, :, 1:W], up[:, :, 0:W - 1], ALU.add))
                link(v.tensor_tensor(s4[:, :, 2:W - 1], s2[:, :, 1:W - 2], s2[:, :, 3:W], ALU.add))
                link(v.tensor_tensor(s8[:, 4:W - 3], s4[:, 1, 2:W - 5], s4[:, 1, 6:W - 1], ALU.add))
                link(v.tensor_tensor(dpool[HD:P, 1, :], s8[HD:P, 4:4 + N], s8[HD:P, 12:12 + N], ALU.add))
                c0 = slice(8, 8 + N)
                v.tensor_tensor(dpool[0:HD, 0, :], s2[0:HD, 0, c0], inv[0:HD, 0, :], ALU.mult)
                v.tensor_tensor(dpool[HD:P, 0, :], s4[HD:P, 0, c0], inv[HD:P, 0, :], ALU.mult)
                v.tensor_tensor(dpool[0:HD, 1, :], s8[0:HD, c0], inv[0:HD, 1, :], ALU.mult)
                link(v.tensor_tensor(dpool[HD:P, 1, :], dpool[HD:P, 1, :], inv[HD:P, 1, :], ALU.mult))
                v.tensor_tensor(dpool[:], dpool[:], up[:, :, c0], ALU.subtract).then_inc(d_ok, 1)

            def conv_in(h):
                v.wait_ge(pj_ok, 7 + h)
                if h == 0:
                    v.wait_ge(pj_act, 6)
                    v.wait_ge(pads_ok, 1)
                v.tensor_tensor(natural(z[:, h, 1:1 + N]), by_column(bank[7]), natural(av[:, h, :]), ALU.mult).then_inc(pj_dve, 1)

            def conv(h):
                v.wait_ge(pj_dve, h + 1)
                link(v.tensor_scalar(cv[:, h, :], z[:, h, 0:N], cols[:, 26 + h:27 + h], None, ALU.mult))
                link(v.scalar_tensor_tensor(out=cv[:, h, :], in0=z[:, h, 1:1 + N], scalar=cols[:, 28 + h:29 + h],
                                            in1=cv[:, h, :], op0=ALU.mult, op1=ALU.add))
                link(v.scalar_tensor_tensor(out=cv[:, h, :], in0=z[:, h, 2:2 + N], scalar=cols[:, 30 + h:31 + h],
                                            in1=cv[:, h, :], op0=ALU.mult, op1=ALU.add))

            def conv_out(h):
                v.wait_ge(pj_ok, 9 + h)
                v.tensor_tensor(natural(yT[:, h, :]), by_column(bank[7]), natural(cv[:, h, :]), ALU.mult).then_inc(pj_dve, 1)

            v.wait_ge(kv_ok, 12)
            v.wait_ge(h_hi_ok, 1)
            v.tensor_tensor(hT_lo[:, 0:4, :], hT[:, 0:4, :], hT_hi[:, 0:4, :], ALU.subtract).then_inc(h_lo_dve, 1)
            v.wait_ge(bias_ok, HEADS)
            late = [(8, pool_diff), (14, lambda: conv_in(0)), (16, lambda: (conv_in(1), conv(0), conv(1))),
                    (18, lambda: conv_out(0)), (20, lambda: conv_out(1))]
            nf = 0
            for u in range(NU + 2):
                while late and nf >= late[0][0]:
                    late.pop(0)[1]()
                if u == NU // 2 + 2:
                    head_pair(0)
                if u < NU:
                    softmax_bias(u)
                    softmax_norm(u)
                nf = min(20, nf + sum(fills(u)))
            while late:
                late.pop(0)[1]()
            head_pair(1)
            def low_y(i, n, first):
                v.wait_ge(y_hi_ok, i + 1)
                ks = slice(first, first + n)
                v.tensor_tensor(yT_lo[:, ks, :], yT[:, ks, :], yT_hi[:, ks, :], ALU.subtract).then_inc(y_lo_ok, 1)

            def fourier_out(h):
                v.wait_ge(fn_even, h + 1)
                even, odd = yT[:, 6 + h, 1:NC - 1], bank[4 + h][:, NC:N]
                link(v.tensor_tensor(yT[:, 6 + h, NC:N][:, ::-1], even, odd, ALU.subtract))
                v.tensor_tensor(even, even, odd, ALU.add).then_inc(fn_copied, 1)

            for i in (0, 2):
                v.wait_ge(wo_hi_ok, i + 1)
                ks = slice(2 * i, 2 * i + 2)
                v.tensor_tensor(wout_lo[:, ks, :], wout[:, ks, :], wout_hi[:, ks, :], ALU.subtract).then_inc(wo_lo_ok, 1)
            fourier_out(0)
            for i in range(3):
                low_y(i, 2, 2 * i)
            fourier_out(1)
            for h in range(2):
                low_y(3 + h, 1, 6 + h)
            v.wait_ge(n2g_in, 16)
            v.wait_ge(rows_act, 6)
            link(v.scalar_tensor_tensor(out=rows[:, SC2, :], in0=rows[:, SC2, :], scalar=1.0, in1=n2g[:],
                                        op0=ALU.add, op1=ALU.mult))
            def residual(n):
                t, half = n // 2, n % 2
                cs_ = slice(half * 512, (half + 1) * 512)
                v.wait_ge(wo_ok, n + 1)
                tmpv = rtmp[:, half, :]
                link(v.tensor_tensor(tmpv, bank[n % 4], rows[:, G1, cs_], ALU.mult))
                v.tensor_tensor(x1[:, t, cs_], x1[:, t, cs_], tmpv, ALU.add).then_inc(x1_ok, 1)

            def norm2(t):
                v.wait_ge(ss2_ok, 2 * t + 2)
                v.tensor_scalar(st2[:, t, 2:3], st2[:, t, 0:1], st2[:, t, 1:2], 1.0 / D, ALU.add, ALU.mult
                                ).then_inc(ms2_ok, 1)
                v.wait_ge(root2_ok, t + 1)
                link(v.reciprocal(st2[:, t, 4:5], st2[:, t, 3:4]))
                if t >= 2:
                    v.wait_ge(h2tr_ok, 2 * t - 2)
                    v.wait_ge(h2_stored[t % 2], 16)
                for half in range(2):
                    cs_ = slice(half * 512, (half + 1) * 512)
                    link(v.scalar_tensor_tensor(out=h2[:, t % 2, cs_], in0=x1[:, t, cs_], scalar=st2[:, t, 4:5],
                                                in1=rows[:, SC2, cs_], op0=ALU.mult, op1=ALU.mult))
                    v.tensor_tensor(h2[:, t % 2, cs_], h2[:, t % 2, cs_], rows[:, SH2, cs_], ALU.add
                                    ).then_inc(h2_ok, 1)

            for t in range(NT):
                residual(2 * t)
                residual(2 * t + 1)
                norm2(t)

            E4 = [P, NT, GROUPS]

            def wide(ap, shape):
                return ap.to_broadcast(shape)

            v.wait_ge(prob_ok, 1)
            v.wait_ge(consts_in, 48)
            v.wait_ge(iota_ok, 1)
            link(v.tensor_tensor(biased[:], prob[:], rb[:], ALU.add))
            b4 = biased[:].rearrange("p t (g e) -> p (t g) e", g=GROUPS)
            v.tensor_tensor(pairs[:, :, 0:3], b4[:, :, 0:3], b4[:, :, 1:4], ALU.add)
            v.tensor_tensor(pairs[:, :, 3:5], b4[:, :, 0:2], b4[:, :, 2:4], ALU.add)
            link(v.tensor_tensor(pairs[:, :, 5:6], b4[:, :, 0:1], b4[:, :, 3:4], ALU.add))
            link(v.tensor_reduce(gs[:].rearrange("p t g -> p (t g)").unsqueeze(2), pairs[:], AX, ALU.max))

            def first_max(src, pri, shape, dst, tmp):
                link(v.tensor_reduce(r1[:], src, AX, ALU.max))
                link(v.tensor_tensor(tmp, src, wide(r1[:], shape), ALU.is_equal))
                link(v.tensor_tensor(tmp, tmp, pri, ALU.mult))
                link(v.tensor_reduce(r2[:], tmp, AX, ALU.max))
                link(v.tensor_tensor(dst, tmp, wide(r2[:], shape), ALU.is_equal))

            first_max(gs[:], pri4[:], E4, geq[:], pen[:])
            link(v.tensor_scalar(pen[:], geq[:], -1.0, BIG, ALU.add, ALU.mult))
            g16 = [P, NT * GROUPS, 4]
            ra4 = ra[:].rearrange("p t (g e) -> p (t g) e", g=GROUPS)
            link(v.tensor_tensor(ra4, b4, wide(pen[:].rearrange("p t g -> p (t g)").unsqueeze(2), g16), ALU.add))
            E16 = [P, NT, NE]
            first_max(ra[:], pri16[:], E16, oh[:, :, 0, :], rbuf[:])
            link(v.scalar_tensor_tensor(out=ra[:], in0=oh[:, :, 0, :], scalar=-3 * BIG, in1=ra[:],
                                        op0=ALU.mult, op1=ALU.add))
            first_max(ra[:], pri16[:], E16, oh[:, :, 1, :], rbuf[:])
            v.tensor_tensor(sel[:], oh[:, :, 0, :], oh[:, :, 1, :], ALU.add).then_inc(sel_ok, 1)

            E2 = [P, NT, 2, NE]

            def pick(dst, src):
                link(v.tensor_tensor(rc[:], oh[:], src, ALU.mult))
                link(v.tensor_reduce(dst.rearrange("p t k -> p (t k)").unsqueeze(2),
                                     rc[:].rearrange("p t k e -> p (t k) e"), AX, ALU.add))

            pick(expert[:], eno[:].unsqueeze(1).unsqueeze(1).to_broadcast(E2))
            v.wait_ge(rank_ok, 1)

            def above(dst, src, limits):
                link(v.tensor_scalar(dst, src, float(limits[0]), None, ALU.is_ge))
                for x_ in limits[1:]:
                    link(v.scalar_tensor_tensor(out=dst, in0=src, scalar=float(x_), in1=dst,
                                                op0=ALU.is_ge, op1=ALU.add))

            pick(rank[:], bank[7][:, 0:NT * NE].rearrange("p (t e) -> p t e", e=NE).unsqueeze(2).to_broadcast(E2))
            above(over[:], rank[:], [P, 2 * P, 3 * P])
            link(v.scalar_tensor_tensor(out=rmod[:], in0=over[:], scalar=-float(P), in1=rank[:],
                                        op0=ALU.mult, op1=ALU.add))
            for i in range(NT * 2):
                v.tensor_scalar(hot_slot[:, i, :], iota_slot[:], rmod[:, i // 2, i % 2:i % 2 + 1], None, ALU.is_equal)
            above(cs[:, 0, 8:], bank[7][:, NT * NE:(NT + 1) * NE], [P + 1, 2 * P + 1, 3 * P + 1])
            v.tensor_copy(ext[:], cs[:, 0, 8:])
            for i, sh in enumerate((1, 2, 4, 8)):
                a, b = cs[:, i % 2, :], cs[:, 1 - i % 2, :]
                link(v.tensor_tensor(b[:, 8:], a[:, 8:], a[:, 8 - sh:8 - sh + NE], ALU.add))
            run = cs[:, 0, 8:]
            link(v.tensor_tensor(off[:], run, ext[:], ALU.subtract))
            link(v.scalar_tensor_tensor(out=off[:], in0=off[:], scalar=float(NE - 1), in1=eno[:],
                                        op0=ALU.add, op1=ALU.subtract))
            pick(off2[:], off[:].unsqueeze(1).unsqueeze(1).to_broadcast(E2))
            link(v.scalar_tensor_tensor(out=off2[:], in0=over[:], scalar=0.0, in1=off2[:],
                                        op0=ALU.is_gt, op1=ALU.mult))
            link(v.tensor_tensor(blk_no[:], over[:], expert[:], ALU.add))
            link(v.tensor_tensor(blk_no[:], blk_no[:], off2[:], ALU.add))
            fb = [P, NT * 2, NB]
            link(v.tensor_tensor(hot_blk[:], iota_blk[:].unsqueeze(1).to_broadcast(fb),
                                 blk_no[:].rearrange("p t k -> p (t k)").unsqueeze(2).to_broadcast(fb), ALU.is_equal))
            v.tensor_scalar(hot_tok[:, :, 0, :], hot_blk[:], tok[:, 0:1], None, ALU.mult)
            v.tensor_tensor(hot_tok[:, :, 1, :], hot_blk[:], tok_chunk[:].unsqueeze(2).to_broadcast(fb), ALU.mult
                            ).then_inc(hot_ok, 1)
            v.wait_ge(idxps_ok, 1)
            link(v.tensor_scalar(idx_f[:], bank[6][:, NB:2 * NB], float(P), float(EMPTY), ALU.mult, ALU.add))
            link(v.tensor_tensor(idx_f[:], idx_f[:], bank[6][:, 0:NB], ALU.add))
            v.tensor_copy(idx[:], idx_f[:]).then_inc(idx_ok, 1)
            run0 = cs[0:1, 0, 8:]
            link(v.tensor_tensor(ov[:], run0.unsqueeze(1).to_broadcast([1, 8, NE]),
                                 iota8[:].unsqueeze(2).to_broadcast([1, 8, NE]), ALU.is_le))
            link(v.tensor_reduce(ovf[:, 0:8].unsqueeze(2), ov[:], AX, ALU.add))
            link(v.tensor_scalar(ovf[:, 0:8], ovf[:, 0:8], float(NE - 1), None, ALU.min))
            above(ovf[:, 8:9], cs[0:1, 0, 8 + NE - 1:8 + NE], [1, 3, 5, 7])
            v.tensor_copy(ints[:, 0:9], ovf[:, 0:9]).then_inc(route_ok, 1)
            link(v.scalar_tensor_tensor(out=slot[:], in0=blk_no[:], scalar=float(P), in1=rmod[:],
                                        op0=ALU.mult, op1=ALU.add))
            v.tensor_copy(slot_idx[:], slot[:]).then_inc(slots_ok, 1)
            pick(wsel[:], prob[:].unsqueeze(2).to_broadcast(E2))
            link(v.tensor_tensor(den[:], wsel[:, :, 0:1], wsel[:, :, 1:2], ALU.add))
            link(v.reciprocal(den[:], den[:]))
            link(v.tensor_tensor(gate[:], wsel[:], wide(den[:], [P, NT, 2]), ALU.mult))

            v.wait_ge(rows_act, 8)
            v.wait_ge(route_ok, 1)
            n_pairs = v.value_load(ints[0:1, 8:9], min_val=0, max_val=OVER // 2) + NE // 2

            def turned_rows(b, s):
                v.wait_ge(xt_ok, s + 1)
                if not (isinstance(s, int) and s == 0):
                    v.wait_ge(h1_ok, s)
                    v.wait_ge(x_hi_ok, s)
                v.tensor_copy(xgT[:].rearrange("p k t -> p (k t)"),
                              psum[:, 0:2, :].rearrange("p a n -> p (a n)")).then_inc(xt_copied, 1)

            def low_w3(b, s):
                for g in range(2):
                    v.wait_ge(w3_hi_ok, s * 2 + 1 + g)
                    ks = slice(4 * g, 4 * g + 4)
                    v.tensor_tensor(w3_lo[b][:, ks, :], w3_sb[b][:, ks, :], w3_hi[:, ks, :], ALU.subtract
                                    ).then_inc(w3_lo_ok, 1)

            def low_rows(s):
                v.wait_ge(x_hi_ok, s + 1)
                v.tensor_tensor(xgT_lo[:], xgT[:], xgT_hi[:], ALU.subtract).then_inc(x_lo_ok, 1)

            def low_w2(b, s, half):
                v.wait_ge(w2_hi_ok[half], s + 1)
                hs = slice(half * 512, (half + 1) * 512)
                v.tensor_tensor(w2_lo[b][:, :, hs], w2_sb[b][:, :, hs], w2_hi[:, :, hs], ALU.subtract
                                ).then_inc(w2_lo_ok[half], 1)

            def low_hidden(s):
                v.wait_ge(het_hi_ok, s + 1)
                v.tensor_tensor(heT_lo[:].rearrange("p k t -> p (k t)"), bank[4],
                                heT_hi[:].rearrange("p k t -> p (k t)"), ALU.subtract).then_inc(het_lo_ok, 1)

            def gated(b, s):
                v.wait_ge(h3_ok, s + 1)
                v.wait_ge(sg_ok, s + 1)
                if not (isinstance(s, int) and s == 0):
                    v.wait_ge(het_ok, s)
                v.tensor_tensor(he[:], bank[3], sg[:], ALU.mult).then_inc(he_ok, 1)

            def expert_rows(b, s, i, half, ok, copied):
                v.wait_ge(ok, s + 1)
                if half == 0 and i is not None:
                    v.wait_ge(ysb_free[b], i * 16 + 16)
                cs_ = slice(half * 512, (half + 1) * 512)
                v.tensor_tensor(ysb[b][:, cs_], bank[5 + half], rows[:, G2, cs_], ALU.mult).then_inc(copied, 1)

            def block_(b, s, prev, prev_i):
                turned_rows(b, s)
                low_w3(b, s)
                if prev is not None:
                    expert_rows(1 - b, prev, prev_i, 0, y0_ok, y0_copied)
                low_rows(s)
                if prev is not None:
                    low_w2(1 - b, prev, 1)
                gated(b, s)
                low_w2(b, s, 0)
                if prev is not None:
                    expert_rows(1 - b, prev, prev_i, 1, y1_ok, y1_copied)
                low_hidden(s)

            block_(0, 0, None, None)
            block_(1, 1, 0, None)
            with v.Fori(1, n_pairs) as i:
                block_(0, i * 2, i * 2 - 1, i - 1)
                block_(1, i * 2 + 1, i * 2, i)
            last = n_pairs * 2 - 1
            low_w2(1, last, 1)
            expert_rows(1, last, n_pairs - 1, 0, y0_ok, y0_copied)
            expert_rows(1, last, n_pairs - 1, 1, y1_ok, y1_copied)

            def add_rows(t):
                for k in range(2):
                    v.wait_ge(gat_in[t][k], 16)
                    ins = v.scalar_tensor_tensor(out=x1[:, t, :], in0=ygat[:, t, k, :], scalar=gate[:, t, k:k + 1],
                                                 in1=x1[:, t, :], op0=ALU.mult, op1=ALU.add)
                    if k == 0:
                        link(ins)
                ins.then_inc(x2_ok, 1)

            def result(t):
                v.wait_ge(root3_ok, t + 1)
                link(v.reciprocal(st2[:, t, 7:8], st2[:, t, 6:7]))
                v.scalar_tensor_tensor(out=ygat[:, t, 1, :], in0=x1[:, t, :], scalar=st2[:, t, 7:8], in1=fing[:],
                                       op0=ALU.mult, op1=ALU.mult).then_inc(res_ok, 1)

            v.wait_ge(fing_in, 16)
            for t in range(NT):
                add_rows(t)
                if t >= 1:
                    result(t - 1)
            result(NT - 1)


def constants():
    n = np.arange(N)
    turn = 2 * np.pi * (np.outer(n, n) % N) / N
    m = np.arange(HD)
    head = 2 * np.pi * (np.outer(m, m) % HD) / HD
    scale = 1 / np.sqrt(N * HD)
    dft_head = np.zeros((P, 2 * P))
    for h in range(2):
        dft_head[h * HD:(h + 1) * HD, h * HD:(h + 1) * HD] = np.cos(head) * scale
        dft_head[h * HD:(h + 1) * HD, P + h * HD:P + (h + 1) * HD] = -np.sin(head) * scale
    sizes = [np.minimum(n + w // 2, N) - np.maximum(n - w // 2, 0) for w in (2, 4, 8, 16)]
    return {
        "dft_seq": np.concatenate([np.cos(turn)[:, 0:NC], np.sin(turn)[:, 1:NC - 1]], axis=1).astype(np.float32),
        "dft_head": dft_head.astype(np.float32),
        "pool_inv": (1 / np.stack(sizes)).astype(np.float32),
    }


_INS = ["x", "c", "ctx", "c_ctx", "ada_w", "ada_b", "norm1_g", "norm2_g", "w_in", "conv_w", "pool_w",
        "pool_scale", "rpb_t", "w_out", "router_w", "router_b", "moe_w1", "moe_w3", "moe_w2", "final_g",
        "dft_seq", "dft_head", "pool_inv"]


def kernel(**inputs):
    import concourse.bacc as bacc
    from concourse.bass_utils import run_bass_kernel_spmd

    nc = bacc.Bacc("TRN2", target_bir_lowering=False, num_devices=1)
    given = {k: np.ascontiguousarray(v) for k, v in inputs.items()}
    given["rpb_t"] = np.ascontiguousarray(given.pop("na_rpb")[0].transpose(0, 2, 1)[:, ::-1, ::-1])
    given.update(constants())
    arrays, args = {}, []
    for name in _INS:
        a = given[name]
        arrays[f"in_{name}"] = a
        args.append(nc.dram_tensor(f"in_{name}", a.shape, mybir.dt.from_np(a.dtype), kind="ExternalInput").ap())
    args.append(nc.dram_tensor("out_0", (1, N, D), F32, kind="ExternalOutput").ap())
    build(nc, *args)
    r = run_bass_kernel_spmd(nc, [arrays], core_ids=[0])
    return r.results[0]["out_0"]
```
